# Optimizing a Trainium2 kernel written in Bass

```python
import math
import jax, jax.numpy as jnp
from jax import lax
import numpy as np

D_MODEL = 1024
BATCH = 1
SEQ = 512
DEPTH = 2

N_EVEN = (DEPTH + 1) // 2
N_ODD = DEPTH // 2
MIX_WIDTH = D_MODEL
EPS = 1e-6

HG_DIM = 128
HG_WIDTH = MIX_WIDTH // 2
HG_HEADS = HG_WIDTH // HG_DIM
DA_HEAD_DIM = 64
DA_V_DIM = 2 * DA_HEAD_DIM
DA_WIDTH = MIX_WIDTH - HG_WIDTH
DA_HEADS = DA_WIDTH // DA_V_DIM
DA_QK_WIDTH = DA_HEADS * 2 * DA_HEAD_DIM
Q_BLOCK = 128
GLA_HEADS = 4
GLA_DK = MIX_WIDTH // 2 // GLA_HEADS
GLA_DV = MIX_WIDTH // GLA_HEADS
GLA_GATE_RANK = 16
GLA_TAU = 16.0
CHUNK = 64
N_GROUPS = 4
EXPERTS_PER_GROUP = 4
N_EXPERTS = N_GROUPS * EXPERTS_PER_GROUP
TOP_K = 2
D_EXPERT = D_MODEL // 2

EVEN_SIZES = (HG_WIDTH, HG_WIDTH, HG_WIDTH, HG_WIDTH, DA_QK_WIDTH, DA_QK_WIDTH, DA_WIDTH)
EVEN_IN = 3584
ODD_SIZES = (GLA_HEADS * GLA_DK, GLA_HEADS * GLA_DK, GLA_HEADS * GLA_DV, MIX_WIDTH, GLA_GATE_RANK)
ODD_IN = 3088

kernel_name = 'hybrid_hgrn2_diffattn_gla_hmoe'

def rms_norm(x, w):
    xf = x.astype(jnp.float32)
    y = xf * lax.rsqrt(jnp.mean(xf * xf, axis=-1, keepdims=True) + EPS)
    return (y * w.astype(jnp.float32)).astype(x.dtype)

def split_cols(p, sizes):
    idx = np.cumsum(sizes)[:-1].tolist()
    return jnp.split(p, idx, axis=-1)

def split_heads(a, n_heads):
    b, t, _ = a.shape
    return a.reshape(b, t, n_heads, -1).transpose(0, 2, 1, 3)

def merge_heads(a):
    b, h, t, d = a.shape
    return a.transpose(0, 2, 1, 3).reshape(b, t, h * d)

def chunk_gated_linear_attention(q, k, v, log_f):
    b, h, t, dk = q.shape
    dv = v.shape[-1]
    n = t // CHUNK

    def to_chunks(a):
        return jnp.moveaxis(a.reshape(b, h, n, CHUNK, a.shape[-1]), 2, 0)

    qc, kc, vc, gc = (to_chunks(a.astype(jnp.float32)) for a in (q, k, v, log_f))
    causal = jnp.tril(jnp.ones((CHUNK, CHUNK), dtype=bool))

    def step(state, inp):
        qi, ki, vi, gi = inp
        cum = jnp.cumsum(gi, axis=-2)
        rel = cum[..., :, None, :] - cum[..., None, :, :]
        decay = jnp.exp(jnp.where(causal[:, :, None], rel, -jnp.inf))
        scores = jnp.sum(qi[..., :, None, :] * ki[..., None, :, :] * decay, axis=-1)
        o_intra = jnp.einsum('bhij,bhjv->bhiv', scores, vi)
        o_inter = jnp.einsum('bhid,bhdv->bhiv', qi * jnp.exp(cum), state)
        last = cum[..., -1:, :]
        k_dec = ki * jnp.exp(last - cum)
        new_state = jnp.exp(last[..., 0, :])[..., None] * state + jnp.einsum('bhjd,bhjv->bhdv', k_dec, vi)
        return new_state, o_intra + o_inter

    s0 = jnp.zeros((b, h, dk, dv), jnp.float32)
    _, o = lax.scan(step, s0, (qc, kc, vc, gc))
    o = jnp.moveaxis(o, 0, 2).reshape(b, h, t, dv)
    return o.astype(v.dtype)

def differential_attention(q1, q2, k1, k2, v, lam):
    scale = DA_HEAD_DIM ** -0.5
    t = q1.shape[2]
    outs = []
    for blk in range(t // Q_BLOCK):
        s, e = blk * Q_BLOCK, (blk + 1) * Q_BLOCK
        mask = jnp.arange(e)[None, :] <= jnp.arange(s, e)[:, None]

        def probs(q, k):
            sc = jnp.einsum('bhqd,bhkd->bhqk', q[:, :, s:e], k[:, :, :e]).astype(jnp.float32) * scale
            return jax.nn.softmax(jnp.where(mask, sc, -jnp.inf), axis=-1)

        w = probs(q1, k1) - lam * probs(q2, k2)
        outs.append(jnp.einsum('bhqk,bhkv->bhqv', w.astype(v.dtype), v[:, :, :e]))
    return jnp.concatenate(outs, axis=2)

def hgrn2_diff_mixer(h, w_in, w_out, lb, hg_o_norm, q_norm, k_norm, lam_vecs, subln, lam_init):
    b, t, _ = h.shape
    hg_q, hg_f, hg_i, hg_g, da_q, da_k, da_v = split_cols(h @ w_in, EVEN_SIZES)
    lb_h = lb.reshape(HG_HEADS, 1, HG_DIM)
    fl = split_heads(hg_f, HG_HEADS).astype(jnp.float32)
    log_f = jnp.log(lb_h + (1.0 - lb_h) * jax.nn.sigmoid(fl))
    key_in = (1.0 - lb_h) * jax.nn.sigmoid(-fl)
    q_hg = jax.nn.silu(split_heads(hg_q, HG_HEADS)) * (HG_DIM ** -0.5)
    o_hg = chunk_gated_linear_attention(q_hg, key_in, split_heads(hg_i, HG_HEADS), log_f)
    o_a = merge_heads(rms_norm(o_hg, hg_o_norm)) * jax.nn.silu(hg_g)
    dq = rms_norm(da_q.reshape(b, t, DA_HEADS, 2, DA_HEAD_DIM), q_norm)
    dk = rms_norm(da_k.reshape(b, t, DA_HEADS, 2, DA_HEAD_DIM), k_norm)
    q1, q2 = dq[..., 0, :].transpose(0, 2, 1, 3), dq[..., 1, :].transpose(0, 2, 1, 3)
    k1, k2 = dk[..., 0, :].transpose(0, 2, 1, 3), dk[..., 1, :].transpose(0, 2, 1, 3)
    lv = lam_vecs.astype(jnp.float32)
    lam = jnp.exp(jnp.sum(lv[0] * lv[1])) - jnp.exp(jnp.sum(lv[2] * lv[3])) + lam_init
    o_da = differential_attention(q1, q2, k1, k2, split_heads(da_v, DA_HEADS), lam)
    o_b = merge_heads(rms_norm(o_da, subln)) * (1.0 - lam_init)
    return jnp.concatenate([o_a, o_b], axis=-1) @ w_out

def gla_mixer(h, w_in, w_alpha, b_alpha, o_norm, w_out):
    q, k, v, g, a = split_cols(h @ w_in, ODD_SIZES)
    log_alpha = jax.nn.log_sigmoid((a @ w_alpha).astype(jnp.float32) + b_alpha.astype(jnp.float32)) / GLA_TAU
    o = chunk_gated_linear_attention(split_heads(q, GLA_HEADS) * (GLA_DK ** -0.5), split_heads(k, GLA_HEADS),
                                     split_heads(v, GLA_HEADS), split_heads(log_alpha, GLA_HEADS))
    o = merge_heads(rms_norm(o, o_norm)) * jax.nn.silu(g)
    return o @ w_out

def hierarchical_moe(h, w_group, b_group, w_router, b_router, w_gate, w_up, w_down):
    b, t, d = h.shape
    hf = h.reshape(b * t, d)
    grp_p = jax.nn.softmax((hf @ w_group).astype(jnp.float32) + b_group.astype(jnp.float32), axis=-1)
    g_sel = jnp.argmax(grp_p, axis=-1)
    g_w = jnp.take_along_axis(grp_p, g_sel[:, None], axis=-1)
    logits_all = jnp.einsum('nd,gde->nge', hf, w_router).astype(jnp.float32) + b_router.astype(jnp.float32)
    exp_logits = jnp.take_along_axis(logits_all, g_sel[:, None, None], axis=1)[:, 0]
    top_p, top_i = lax.top_k(jax.nn.softmax(exp_logits, axis=-1), TOP_K)
    weights = g_w * top_p / jnp.sum(top_p, axis=-1, keepdims=True)
    expert_id = g_sel[:, None] * EXPERTS_PER_GROUP + top_i
    combine = jnp.sum(jax.nn.one_hot(expert_id, N_EXPERTS, dtype=jnp.float32) * weights[..., None], axis=1)
    combine = combine.astype(h.dtype)
    y = jnp.zeros_like(hf)
    for e in range(N_EXPERTS):
        act = jax.nn.silu(hf @ w_gate[e]) * (hf @ w_up[e])
        y = y + combine[:, e:e + 1] * (act @ w_down[e])
    return y.reshape(b, t, d)

def setup_inputs(seed: int = 0) -> dict:
    key = jax.random.key(seed)
    ks = jax.random.split(key, 24)

    def nrm(k, shape, scale):
        return jax.random.normal(k, shape, jnp.float32) * scale

    out_scale = (2 * DEPTH) ** -0.5
    dsc = D_MODEL ** -0.5
    return {
        'x': nrm(ks[0], (BATCH, SEQ, D_MODEL), 1.0),
        'attn_norm': 1.0 + nrm(ks[1], (DEPTH, D_MODEL), 0.02),
        'ffn_norm': 1.0 + nrm(ks[2], (DEPTH, D_MODEL), 0.02),
        'even_w_in': nrm(ks[3], (N_EVEN, D_MODEL, EVEN_IN), dsc),
        'even_w_out': nrm(ks[4], (N_EVEN, MIX_WIDTH, D_MODEL), MIX_WIDTH ** -0.5 * out_scale),
        'hg_lb_logits': nrm(ks[5], (N_EVEN, HG_WIDTH), 0.5),
        'hg_o_norm': 1.0 + nrm(ks[6], (N_EVEN, HG_DIM), 0.02),
        'da_q_norm': 1.0 + nrm(ks[7], (N_EVEN, DA_HEAD_DIM), 0.02),
        'da_k_norm': 1.0 + nrm(ks[8], (N_EVEN, DA_HEAD_DIM), 0.02),
        'da_lambda': nrm(ks[9], (N_EVEN, 4, DA_HEAD_DIM), 0.1),
        'da_subln': 1.0 + nrm(ks[10], (N_EVEN, DA_V_DIM), 0.02),
        'odd_w_in': nrm(ks[11], (N_ODD, D_MODEL, ODD_IN), dsc),
        'gla_w_alpha': nrm(ks[12], (N_ODD, GLA_GATE_RANK, GLA_HEADS * GLA_DK), GLA_GATE_RANK ** -0.5),
        'gla_b_alpha': nrm(ks[13], (N_ODD, GLA_HEADS * GLA_DK), 0.1),
        'gla_o_norm': 1.0 + nrm(ks[14], (N_ODD, GLA_DV), 0.02),
        'odd_w_out': nrm(ks[15], (N_ODD, MIX_WIDTH, D_MODEL), MIX_WIDTH ** -0.5 * out_scale),
        'moe_w_group': nrm(ks[16], (DEPTH, D_MODEL, N_GROUPS), dsc),
        'moe_b_group': nrm(ks[17], (DEPTH, N_GROUPS), 0.01),
        'moe_w_router': nrm(ks[18], (DEPTH, N_GROUPS, D_MODEL, EXPERTS_PER_GROUP), dsc),
        'moe_b_router': nrm(ks[19], (DEPTH, N_GROUPS, EXPERTS_PER_GROUP), 0.01),
        'moe_w_gate': nrm(ks[20], (DEPTH, N_EXPERTS, D_MODEL, D_EXPERT), dsc),
        'moe_w_up': nrm(ks[21], (DEPTH, N_EXPERTS, D_MODEL, D_EXPERT), dsc),
        'moe_w_down': nrm(ks[22], (DEPTH, N_EXPERTS, D_EXPERT, D_MODEL), D_EXPERT ** -0.5 * out_scale),
    }

def reference(x, attn_norm, ffn_norm, even_w_in, even_w_out, hg_lb_logits, hg_o_norm, da_q_norm, da_k_norm,
              da_lambda, da_subln, odd_w_in, gla_w_alpha, gla_b_alpha, gla_o_norm, odd_w_out,
              moe_w_group, moe_b_group, moe_w_router, moe_b_router, moe_w_gate, moe_w_up, moe_w_down):
    lb_sm = jax.nn.softmax(hg_lb_logits.astype(jnp.float32), axis=0)
    lb_all = jnp.cumsum(lb_sm, axis=0) - lb_sm[0:1]
    for layer in range(DEPTH):
        j = layer // 2
        h = rms_norm(x, attn_norm[layer])
        if layer % 2 == 0:
            lam_init = 0.8 - 0.6 * math.exp(-0.3 * layer)
            mix = hgrn2_diff_mixer(h, even_w_in[j], even_w_out[j], lb_all[j], hg_o_norm[j], da_q_norm[j],
                                   da_k_norm[j], da_lambda[j], da_subln[j], lam_init)
        else:
            mix = gla_mixer(h, odd_w_in[j], gla_w_alpha[j], gla_b_alpha[j], gla_o_norm[j], odd_w_out[j])
        x = x + mix
        h = rms_norm(x, ffn_norm[layer])
        x = x + hierarchical_moe(h, moe_w_group[layer], moe_b_group[layer], moe_w_router[layer],
                                 moe_b_router[layer], moe_w_gate[layer], moe_w_up[layer], moe_w_down[layer])
    return x


_drawn_inputs = setup_inputs


def setup_inputs(seed=0):
    import zlib

    import numpy as np

    out = dict(_drawn_inputs(seed))
    spreads = {}
    factors = {'ffn_norm': 3.005,
     'hg_o_norm': 5.322,
     'da_q_norm': 6.65,
     'da_k_norm': 6.897,
     'da_lambda': 6.163,
     'da_subln': 4.738,
     'gla_b_alpha': 3.956,
     'gla_o_norm': 7.126,
     'moe_b_group': 7.994,
     'moe_b_router': 7.217}
    for name, (base, spread) in spreads.items():
        noise = np.random.default_rng([zlib.crc32(name.encode()), seed]).standard_normal(out[name].shape)
        drawn = base * np.exp(spread * noise) if base else spread * noise
        out[name] = __import__('jax').numpy.asarray(drawn.astype(out[name].dtype))
    for name, factor in factors.items():
        out[name] = (out[name] * factor).astype(out[name].dtype)
    return out
```

```python
from contextlib import ExitStack

import concourse.bass as bass
from concourse import mybir

F32 = mybir.dt.float32
I32 = mybir.dt.int32
U8 = mybir.dt.uint8
ALU = mybir.AluOpType
ACT = mybir.ActivationFunctionType
AX = mybir.AxisListType.X

P = 128
EPS = 1e-6
NEG = -1e30


class PsumBanks:

    def __init__(self, full, free):
        self.full, self.free = full, free
        self.count = [0] * 8
        self.last = [None] * 8
        self.uses = {}

    def plan(self, key, banks):
        s = banks[0]
        before = sorted({self.last[b] for b in banks if self.last[b] is not None})
        self.count[s] += 1
        self.uses[key] = (s, self.count[s], before)
        for b in banks:
            self.last[b] = (s, self.count[s])

    def plan_loop(self, key, bank, rounds):
        self.uses[key] = (bank, self.count[bank] + 1, [])
        self.count[bank] += rounds
        self.last[bank] = (bank, self.count[bank])

    def acquire(self, pe, key):
        for s, n in self.uses[key][2]:
            pe.wait_ge(self.free[s], n)

    def acquire_in_loop(self, pe, key, i):
        s, n, _ = self.uses[key]
        pe.wait_ge(self.free[s], i + (n - 1))

    def wait_full(self, eng, key, i=0):
        s, n, _ = self.uses[key]
        eng.wait_ge(self.full[s], i + n)

    def filled(self, key):
        return self.full[self.uses[key][0]]

    def freed(self, key):
        return self.free[self.uses[key][0]]


class Chain:

    def __init__(self, eng, sem):
        self.eng, self.sem, self.n, self.i, self.per = eng, sem, 0, None, 0

    def __call__(self, ins):
        self.n += 1
        ins.then_inc(self.sem, 1)
        if self.i is None:
            self.eng.wait_ge(self.sem, self.n)
        else:
            self.eng.wait_ge(self.sem, self.i * self.per + self.n)

    def enter(self, i, per):
        self.i, self.per, self.start = i, per, self.n

    def leave(self, rounds):
        assert self.n - self.start == self.per
        self.n = self.start + self.per * rounds
        self.i = None


def build(nc, t):
    x_in = t["x"]
    B, T, D = x_in.shape
    NT = T // P
    KD = D // P
    NL = t["attn_norm"].shape[0]
    HW = t["hg_lb_logits"].shape[1]
    NH = 4
    DK = P
    DVS = (t["hg_o_norm"].shape[1], t["gla_o_norm"].shape[1])
    DA_D = t["da_q_norm"].shape[1]
    RANK = t["gla_w_alpha"].shape[1]
    NG, EPG = t["moe_w_group"].shape[2], t["moe_w_router"].shape[3]
    NE = NG * EPG
    NR = NG + NE
    DE = t["moe_w_gate"].shape[3]
    CAP = P
    NX = (2 * T - NE) // CAP
    NB = NE + NX
    GC = 512
    LAM0 = 0.2
    QSCALE = float(DK) ** -0.5
    DASCALE = float(DA_D) ** -0.5
    GATE_SCALE = (1.0, 1.0 / 16.0)
    LEVELS = 7
    assert (B, NT, KD, NL, HW, DE, NH * DVS[1]) == (1, 4, 8, 2, 512, 512, D) and NB <= 24

    EVEN = [("f", 1), ("q", 0), ("v", 2), ("g", 3), ("dq", 4), ("dk", 5), ("dv", 6)]
    ODD = [("q", 0), ("k", 1), ("v", 2), ("v2", 3), ("g", 4), ("g2", 5)]
    MIX = [EVEN, ODD]
    first_group = [0, len(EVEN) + 2 + 3 * NB]

    def mixer_steps(l):
        units = [("proj", l, k, u) for k, _ in MIX[l] for u in range(4)]
        levels = [("cum", l)] + [("prep", l, 0)]
        for s in range(1, LEVELS):
            levels += [("prep", l, s), ("mm", l, s - 1), ("put", l, s - 1)]
        levels += [("mm", l, LEVELS - 1), ("put", l, LEVELS - 1), ("mm", l, LEVELS), ("put", l, LEVELS), ("inter", l)]
        steps = ([("alpha", l)] if l == 1 else []) + units[:8]
        rest, work = units[8:], levels
        while rest or work:
            if rest:
                steps.append(rest.pop(0))
            steps += work[:3]
            work = work[3:]
        steps += [("out", l, i) for i in range(NT)]
        if l == 0:
            steps += [("da", l, i) for i in range(NT * NH + 1)]
        return steps

    STEPS = [mixer_steps(0), mixer_steps(1)]
    NBK = [NH * dv // GC for dv in DVS]

    ctx = ExitStack()
    with ctx:
        base = nc.sbuf_base
        base += -base % 64
        cursor = [base]

        def at(name, shape, dt, offset):
            return nc.alloc_sbuf_tensor_at(name, shape, dt, offset=offset)

        def size_of(shape, dt):
            n = 1 if dt == U8 else 4
            for s in shape[1:]:
                n *= s
            return n + (-n % 64)

        def sb(name, shape, dt=F32):
            o = cursor[0]
            cursor[0] += size_of(shape, dt)
            return at(name, shape, dt, o)

        def sem(name):
            return ctx.enter_context(nc.semaphore(name))

        x = sb("x_sb", [P, NT, D])
        wbuf = sb("weight_ring", [P, 3, KD, GC])
        etmp = sb("exp_tmp", [P, 2, GC])
        ident = sb("ident", [P, P])
        masks = sb("level_masks", [P, LEVELS + 1, P], U8)
        ones = sb("ones", [P, P])
        triu = sb("tri_before", [P, P])
        negmask = sb("causal_neg", [P, P])
        reset = sb("scan_reset", [P, T], U8)
        iota_f = sb("iota_free", [P, P])
        tok_id = sb("token_id", [P, NT])
        normw = sb("norm_weight", [P, D])
        rw = sb("router_w", [P, KD, NR])
        rb = sb("router_b", [P, NR])
        lb = sb("lower_bound", [P, 4 * NH])
        onw = sb("o_norm_w", [P, DVS[1]])
        subw = sb("subln_w", [P, DVS[0]])
        dqw = sb("da_q_w", [P, 1])
        dkw = sb("da_k_w", [P, 1])
        lamv = sb("lambda_vecs", [P, 4 * DA_D])
        lam = sb("lambda", [P, 4])
        balpha = sb("b_alpha", [P, NH])
        walpha = sb("w_alpha", [P, NH * DK])
        wa = sb("w_a", [P, KD, RANK])
        ss = sb("sum_sq", [P, 8])
        rstd = sb("rstd", [P, 8])
        el = sb("exp_last", [P, NH, NT])
        mx = sb("score_max", [P, 2, 2])
        nb = sb("score_bias", [P, 2, 2])
        sm = sb("score_sum", [P, 2, 2])
        rs = sb("score_rec", [P, 2, 2])
        arena = cursor[0]
        h = sb("h", [P, NT, D])
        hT = sb("hT", [P, KD, T])
        Q = sb("Q", [P, NH, T])
        K = sb("K", [P, NH, T])
        C = sb("C", [P, NH, T])
        G = sb("G", [P, NT, D])
        W = sb("W", [P, 2, NH * T])
        AT = sb("AT", [P, NT, NH, P])
        dqT = sb("dqT", [P, NH, T])
        dkT = sb("dkT", [P, NH, T])
        S_at = cursor[0]
        S0 = sb("S0", [P, 2, NH, DVS[0]])
        stag = sb("da_stage", [P, 2, GC])
        assert cursor[0] <= nc.sbuf_usable_end
        dq_at = S_at - 2 * NH * T * 4
        S1 = at("S1", [P, 2, NH, DVS[1]], F32, dq_at)
        aT = at("aT", [P, T], F32, dq_at + 2 * NH * DVS[1] * 4)
        S = [S0, S1]
        w_at = dq_at - NT * NH * P * 4 - 2 * NH * T * 4
        prob = at("prob", [P, 2, 2, T], F32, w_at)
        wgt = at("wgt", [P, 2, T], F32, w_at + 4 * T * 4)
        wgtT = at("wgtT", [P, 2, T], F32, w_at + 6 * T * 4)
        cursor[0] = arena + 2 * NT * D * 4
        xg = sb("xg", [P, D])
        xgT = sb("xgT", [P, KD, P])
        ex = sb("ex", [P, DE])
        act = sb("act", [P, DE])
        actT = sb("actT", [P, DE // P, P])
        yb = sb("yb", [P, D])
        yg = sb("yg", [P, 4, D])
        ohj = sb("ohj", [P, 2, P])
        ohb = sb("ohb", [P, 2, 24])
        idx = sb("idx", [P, 24], I32)
        idxcol = sb("idxcol", [P, 1], I32)
        eid = sb("eid", [P, 8], I32)
        rt = {}
        for name, shape in dict(
            L=[NT, NR], gmax=[NT], cand=[NT, NG], m=[NT], ohg=[NT, NG], eg=[NT, NG], gsum=[NT], sel=[NT, EPG, NG],
            xl=[NT, EPG], m1=[NT], oh1=[NT, EPG], xl2=[NT, EPG], m2=[NT], oh2=[NT, EPG], e2=[NT], den=[NT],
            wt=[2, NT], OH=[2, NT, NE], M=[NT, NE], R=[NT, NE], N=[NE], nx=[NE], off=[NE], q=[NT, NE], j=[NT, NE],
            b=[NT, NE], tA=[NT, NE], bc=[2, NT], jc=[2, NT], sl=[2, NT], ein=[8, NE], ein2=[8, NE], eidf=[8],
        ).items():
            rt[name] = sb("r_" + name, [P] + shape)
        slot = sb("slot", [P, 2, NT], I32)
        ii = at("iota_i", [P, P], I32, arena)
        jj = at("iota_j", [P, P], I32, arena + 512)
        xx = at("iota_x", [P, P], I32, arena + 1024)
        m1_ = at("mask_1", [P, P], I32, arena + 1536)
        m2_ = at("mask_2", [P, P], I32, arena + 2048)
        lbt = at("lb_tmp", [P, 2, NH], F32, arena + 2560)

        PS = ctx.enter_context(nc.psum_tensor("PS", [P, 8, GC], F32))

        hbuf = [nc.dram_tensor(f"h_rows{l}", (T, D), F32).ap() for l in range(NL)]
        ybuf = [nc.dram_tensor(f"y_rows{l}", (NB * CAP, D), F32).ap() for l in range(NL)]

        bk = PsumBanks([sem(f"bank{b}_full") for b in range(8)], [sem(f"bank{b}_free") for b in range(8)])
        x_loaded = [sem(f"x_loaded{i}") for i in range(NT)]
        par1, par2 = sem("params_even_loaded"), sem("params_rest_loaded")
        nw_loaded = sem("norm_weight_loaded")
        w_loaded = [sem(f"w_loaded{i}") for i in range(3)]
        w_used = sem("w_used")
        rw_loaded = sem("router_loaded")
        consts = sem("consts_ready")
        masks_ready = sem("masks_ready")
        v_step, a_step = sem("vector_step"), sem("scalar_step")
        sq_done, rstd_done = sem("sq_done"), sem("rstd_done")
        h_ready, hT_a, hT_v = sem("h_ready"), sem("hT_by_scalar"), sem("hT_by_vector")
        x_new = sem("x_updated")
        e_ready, etmp_free = sem("exp_ready"), sem("exp_tmp_free")
        sig_ready = sem("sigmoid_ready")
        C_ready = sem("log_decay_ready")
        QKV_a, QKV_v = sem("heads_by_scalar"), sem("heads_by_vector")
        st_ready, daT = sem("da_staged"), sem("daT_ready")
        aT_ready = sem("aT_ready")
        D_ready, E_ready, X_ready = sem("diff_ready"), sem("decay_ready"), sem("scaled_ready")
        mm_done, put_done = sem("level_scored"), sem("level_put")
        keT_ready, S_ready = sem("keT_ready"), sem("state_ready")
        o_stat, o_done = sem("o_stat"), sem("o_done")
        nb_ready, p_ready, wgt_ready, wT_ready = sem("bias_ready"), sem("prob_ready"), sem("wgt_ready"), sem("wgtT_ready")
        lam_s, lam_e = sem("lambda_sums"), sem("lambda_exps")
        h_stored = sem("h_stored")
        r_gl, r_eg, r_x2, r_e2 = sem("r_groups"), sem("r_exp_groups"), sem("r_second"), sem("r_exp_second")
        M_ready, oh_ready, idx_ready, eid_ready = sem("assigned"), sem("onehots"), sem("idx_ready"), sem("eid_ready")
        idxcol_ready, gathered = sem("idxcol_ready"), sem("gathered")
        xgT_ready, ex_ready = sem("xgT_ready"), sem("gate_exp_ready")
        act_ready, actT_ready, y_ready, y_stored = sem("act_ready"), sem("actT_ready"), sem("y_ready"), sem("y_stored")
        yg_sem = [sem(f"y_gathered{i}") for i in range(4)]
        stored = sem("out_stored")
        idx_step, v_half = sem("idx_step"), sem("vector_half")
        gather_issued = sem("gather_issued")
        halves = [0]

        def plan_transposes(key):
            for i in range(NT):
                for g in range(2):
                    bk.plan((*key, i, g), [6 + g])

        nproj = 0
        for l in range(NL):
            plan_transposes(("hT", 2 * l))
            for s in STEPS[l]:
                if s[0] == "alpha":
                    bk.plan(s, [4])
                    for u in range(4):
                        bk.plan((*s, u), [u])
                elif s[0] == "proj":
                    bk.plan(s, [s[3]])
                    if s[2] in ("dq", "dk"):
                        bk.plan(("dT", *s[1:]), [s[3]])
                elif s[0] == "mm":
                    for i in range(NT):
                        bk.plan((*s, i), [4 + i])
                elif s[0] == "inter":
                    for i in range(NT - 1):
                        bk.plan((*s, i), [4 + i])
                elif s[0] == "out":
                    if s[2] < NT - 1:
                        bk.plan(("dS", l, s[2]), [4, 5][:NBK[l]])
                    bk.plan(s, [6, 7][:NBK[l]])
                elif s[0] == "da":
                    i = s[2]
                    if i < NT * NH:
                        bk.plan(("score", i), [0, 1] if i % 2 == 0 else [2, 3])
                    if i:
                        bk.plan(("wT", i - 1), [4 + (i - 1) % 2])
                        if (i - 1) % NH == 0:
                            bk.plan(("pv", (i - 1) // NH), [6 + (i - 1) // NH % 2])
            plan_transposes(("oT", l))
            for n in range(2):
                for i in range(NT):
                    bk.plan(("wo", l, n, i), [i])
            plan_transposes(("hT", 2 * l + 1))
            bk.plan(("route", l), [0])
            bk.plan(("rank", l), [1])
            bk.plan(("idx", l), [2])
            for g in range(2):
                bk.plan(("first", l, g), [4 + g])
            for k, b in (("gate", 0), ("up", 1), ("down0", 2), ("down1", 3), ("actT", 6)):
                bk.plan_loop((k, l), b, NB)
            for g in range(2):
                bk.plan_loop(("xgT", l, g), 4 + g, NB - 1)

        def bank(key):
            return PS[:, bk.uses[key][0], :]

        def dv_of(l):
            return DVS[l]

        block = ctx.enter_context(nc.Block())

        @block.sync
        def _(sp):
            def load_group(n, src):
                if n >= 3:
                    sp.wait_ge(w_used, n - 2)
                sp.dma_start(wbuf[:, n % 3], src).then_inc(w_loaded[n % 3], 16)

            def cols(w, c):
                return w[:, c * GC:(c + 1) * GC].rearrange("(k p) n -> p k n", p=P)

            for i in range(NT):
                sp.dma_start(x[:, i], x_in[0, i * P:(i + 1) * P, :]).then_inc(x_loaded[i], 16)
                if i == 0:
                    load_group(0, cols(t["even_w_in"][0], EVEN[0][1]))
            for l in range(NL):
                w_in, w_out = (t["even_w_in"][0], t["even_w_out"][0]) if l == 0 else (t["odd_w_in"][0], t["odd_w_out"][0])
                n = first_group[l]
                for i, (_, c) in enumerate(MIX[l]):
                    if l or i:
                        load_group(n + i, cols(w_in, c))
                n += len(MIX[l])
                for c in range(2):
                    load_group(n + c, cols(w_out, c))
                n += 2

                def load_expert(e, wait):
                    for g, w in enumerate((t["moe_w_gate"], t["moe_w_up"], t["moe_w_down"])):
                        src = w[l, bass.ds(e, 1)].rearrange("a (k p) n -> p (a k) n", p=P)
                        dst = wbuf[:, (n + g) % 3]
                        if g == 2:
                            dst = dst.rearrange("p (k c) n -> p k (c n)", c=2)
                        sp.wait_ge(w_used, wait + g)
                        sp.dma_start(dst, src).then_inc(w_loaded[(n + g) % 3], 16)

                load_expert(0, n - 2)
                for i in range(NT):
                    sp.wait_ge(h_ready, NT * (2 * l + 1) + i + 1)
                    sp.dma_start(hbuf[l][i * P:(i + 1) * P, :], h[:, i]).then_inc(h_stored, 16)
                with sp.Fori(1, NE) as e:
                    load_expert(e, e * 3 + (n - 2))
                sp.wait_ge(eid_ready, l + 1)
                with sp.Fori(0, NX) as b:
                    e = sp.value_load(eid[0:1, bass.ds(b, 1)], min_val=0, max_val=NE - 1)
                    load_expert(e, b * 3 + (n - 2 + 3 * NE))
            for i in range(NT):
                sp.wait_ge(x_new, NL * 3 * NT - NT + i + 1)
                sp.dma_start(t["out"][0, i * P:(i + 1) * P, :], x[:, i]).then_inc(stored, 16)
            sp.wait_ge(stored, 16 * NT)

        @block.gpsimd
        def _(pool):
            pool.memset(ident[:], 0.0).then_inc(consts, 1)
            pool.memset(ones[:], 1.0).then_inc(consts, 1)
            pool.memset(negmask[:], 0.0).then_inc(consts, 1)
            pool.wait_ge(consts, 3)
            pool.affine_select(out=ident[:], in_=ident[:], compare_op=ALU.not_equal, fill=1.0, base=0,
                               pattern=[[-1, P]], channel_multiplier=1).then_inc(consts, 1)
            pool.affine_select(out=triu[:], in_=ones[:], compare_op=ALU.is_gt, fill=0.0, base=0,
                               pattern=[[1, P]], channel_multiplier=-1).then_inc(consts, 1)
            pool.affine_select(out=negmask[:], in_=negmask[:], compare_op=ALU.is_ge, fill=NEG, base=0,
                               pattern=[[-1, P]], channel_multiplier=1).then_inc(consts, 1)
            pool.iota(iota_f[:], [[1, P]], base=0, channel_multiplier=0,
                      allow_small_or_imprecise_dtypes=True).then_inc(consts, 1)
            pool.iota(tok_id[:], [[P, NT]], base=0, channel_multiplier=1,
                      allow_small_or_imprecise_dtypes=True).then_inc(consts, 1)
            pool.iota(ii[:], [[1, P]], base=0, channel_multiplier=0).then_inc(consts, 1)
            pool.iota(jj[:], [[0, P]], base=0, channel_multiplier=1).then_inc(consts, 1)

            def gather(l, i, b):
                g0 = l * NB
                pool.tensor_copy(idxcol[:], idx[:, bass.ds(b, 1)]).then_inc(idxcol_ready, 1)
                pool.wait_ge(idxcol_ready, b + (g0 + 1))
                pool.sem_inc(gather_issued, 1)
                pool.indirect_dma_start(xg[:], None, hbuf[l][:], bass.IndirectOffsetOnAxis(idxcol[:], 0)
                                        ).then_inc(gathered, 16)

            for l in range(NL):
                pool.wait_ge(idx_ready, l + 1)
                pool.wait_ge(h_stored, 16 * NT * (l + 1))
                gather(l, 0, 0)
                bk.wait_full(pool, ("first", l, 1))
                gather(l, 0, 1)
                with pool.Fori(0, NB - 2) as b:
                    bk.wait_full(pool, ("xgT", l, 1), b)
                    pool.wait_ge(gathered, b * 16 + 16 * (l * NB + 2))
                    gather(l, 0, b + 2)
                pool.wait_ge(y_stored, 16 * NB * (l + 1))
                for c in range(2):
                    for i in range(NT):
                        k = c * NT + i
                        if k >= 4:
                            pool.wait_ge(x_new, NT * (3 * l + 1) + (k - 4) + 1)
                        pool.indirect_dma_start(yg[:, k % 4], None, ybuf[l][:], bass.IndirectOffsetOnAxis(
                            slot[:, c, i:i + 1], 0)).then_inc(yg_sem[k % 4], 16)

        @block.scalar
        def _(sc):
            link = Chain(sc, a_step)
            act_ = sc.activation
            etmp_uses = [0]

            def take_etmp():
                if etmp_uses[0]:
                    sc.wait_ge(etmp_free, etmp_uses[0])
                etmp_uses[0] += 1

            def param(dst, src, s):
                sc.dma_start(dst, src, allow_slow_non_contiguous=True).then_inc(s, 16)

            def load_norm(n):
                if n:
                    sc.wait_ge(h_ready, NT * n)
                w = t["attn_norm"] if n % 2 == 0 else t["ffn_norm"]
                param(normw[:], w[n // 2:n // 2 + 1, :].broadcast_to([P, D]), nw_loaded)

            load_norm(0)
            param(lb[:, 0:NH], t["hg_lb_logits"][0].rearrange("(h p) -> p h", p=P), par1)
            for half in range(2):
                param(dqw[half * DA_D:(half + 1) * DA_D, :], t["da_q_norm"].rearrange("a n -> n a"), par1)
                param(dkw[half * DA_D:(half + 1) * DA_D, :], t["da_k_norm"].rearrange("a n -> n a"), par1)
            param(lamv[:], t["da_lambda"].rearrange("a b n -> a (b n)").broadcast_to([P, 4 * DA_D]), par1)
            param(subw[:], t["da_subln"].broadcast_to([P, DVS[0]]), par1)
            param(onw[:, 0:DVS[0]], t["hg_o_norm"].broadcast_to([P, DVS[0]]), par1)
            param(balpha[:], t["gla_b_alpha"][0].rearrange("(h p) -> p h", p=P), par2)
            param(walpha[0:RANK, :], t["gla_w_alpha"][0], par2)
            param(wa[:], t["odd_w_in"][0][:, NH * 2 * DK + 2 * D:].rearrange("(k p) n -> p k n", p=P), par2)

            def load_router(l):
                param(rw[:, :, 0:NG], t["moe_w_group"][l].rearrange("(k p) g -> p k g", p=P), rw_loaded)
                for g in range(NG):
                    param(rw[:, :, NG + g * EPG:NG + (g + 1) * EPG],
                          t["moe_w_router"][l, g].rearrange("(k p) e -> p k e", p=P), rw_loaded)
                param(rb[:, 0:NG], t["moe_b_group"][l:l + 1, :].broadcast_to([P, NG]), rw_loaded)
                param(rb[:, NG:], t["moe_b_router"][l:l + 1].rearrange("a g e -> a (g e)").broadcast_to([P, NE]),
                      rw_loaded)

            def norm(n):
                for i in range(NT):
                    if n == 0:
                        sc.wait_ge(x_loaded[i], 16)
                    else:
                        sc.wait_ge(x_new, NT * (3 * ((n - 1) // 2) + (1 if n % 2 else 3)) - NT + i + 1)
                    if i == 0:
                        take_etmp()
                    act_(etmp[:].rearrange("p a b -> p (a b)"), x[:, i], ACT.Square,
                         accum_out=ss[:, i:i + 1]).then_inc(sq_done, 1)
                    sc.wait_ge(sq_done, NT * n + i + 1)
                link(act_(rstd[:, 0:NT], ss[:, 0:NT], ACT.Ln, scale=1.0 / D, bias=EPS))
                act_(rstd[:, 0:NT], rstd[:, 0:NT], ACT.Exp, scale=-0.5).then_inc(rstd_done, 1)

            def transposes(key):
                for i in range(NT):
                    bk.wait_full(sc, (*key, i, 0))
                    link(act_(hT[:, 0:4, i * P:(i + 1) * P],
                              bank((*key, i, 0)).rearrange("p (k n) -> p k n", k=4), ACT.Copy))
                    sc.sem_inc(hT_a, 1)
                    sc.sem_inc(bk.freed((*key, i, 0)), 1)

            def head_norm(key, l, dv):
                z = PS[:, bk.uses[key][0]:bk.uses[key][0] + NH * dv // GC, :]
                bk.wait_full(sc, key)
                take_etmp()
                act_(etmp[:, 0:NH * dv // GC], z, ACT.Square).then_inc(e_ready, 1)
                e_uses[0] += 1
                sig_uses[0] += 1
                sc.wait_ge(sig_ready, sig_uses[0])
                link(act_(rstd[:, 0:NH], ss[:, 0:NH], ACT.Ln, scale=1.0 / dv, bias=EPS))
                act_(rstd[:, 0:NH], rstd[:, 0:NH], ACT.Exp, scale=-0.5).then_inc(o_stat, 1)

            e_uses, sig_uses = [0], [0]

            for l in range(NL):
                norm(2 * l)
                if l == 0:
                    sc.wait_ge(lam_s, 1)
                    act_(lam[:, 0:2], lam[:, 2:4], ACT.Exp).then_inc(lam_e, 1)
                transposes(("hT", 2 * l))
                load_norm(2 * l + 1)
                if l:
                    param(onw[:], t["gla_o_norm"].broadcast_to([P, DVS[1]]), par2)
                load_router(l)
                for s in STEPS[l]:
                    kind = s[0]
                    if kind == "alpha":
                        for u in range(4):
                            sig_uses[0] += 1
                            sc.wait_ge(sig_ready, sig_uses[0])
                            link(act_(etmp[:, 1], etmp[:, 1], ACT.Exp, scale=-1.0))
                            act_(etmp[:, 1], etmp[:, 1], ACT.Ln, bias=1.0).then_inc(e_ready, 1)
                            etmp_uses[0] += 1
                    elif kind == "proj":
                        _, _, what, u = s
                        bk.wait_full(sc, s)
                        z = bank(s)
                        if what in ("q", "g", "g2") and not (l == 1 and what == "q"):
                            take_etmp()
                            act_(etmp[:, 0], z, ACT.Exp, scale=-1.0).then_inc(e_ready, 1)
                        elif what == "f":
                            take_etmp()
                            link(act_(etmp[:, 0], z, ACT.Exp, scale=-1.0))
                            link(act_(etmp[:, 1], z, ACT.Exp, scale=1.0))
                            sc.sem_inc(e_ready, 1)
                            sc.sem_inc(bk.freed(s), 1)
                            sig_uses[0] += 1
                            sc.wait_ge(sig_ready, sig_uses[0])
                            link(act_(C[:, u], etmp[:, 0], ACT.Ln, scale=lb[:, 2 * NH + u:2 * NH + u + 1],
                                 bias=lb[:, NH + u:NH + u + 1]))
                            sc.sem_inc(C_ready, 1)
                            sc.sem_inc(etmp_free, 1)
                        elif what in ("dq", "dk"):
                            take_etmp()
                            act_(etmp[:, 0], z, ACT.Square).then_inc(e_ready, 1)
                            sig_uses[0] += 1
                            sc.wait_ge(sig_ready, sig_uses[0])
                            link(act_(rstd[:], ss[:], ACT.Ln, scale=1.0 / DA_D, bias=EPS))
                            act_(rstd[:], rstd[:], ACT.Exp, scale=-0.5).then_inc(o_stat, 1)
                            key = ("dT", *s[1:])
                            bk.wait_full(sc, key)
                            dst, w = (dqT, dqw) if what == "dq" else (dkT, dkw)
                            link(act_(dst[:, :, u * P:(u + 1) * P], bank(key).rearrange("p (h n) -> p h n", h=NH),
                                 ACT.Copy, scale=w[:, 0:1]))
                            sc.sem_inc(daT, 1)
                            sc.sem_inc(bk.freed(key), 1)
                        else:
                            if what == "v":
                                dst = h[:, u, 0:GC]
                            elif what in ("v2", "dv"):
                                dst = h[:, u, GC:D]
                            else:
                                dst = (Q if what == "q" else K)[:, u]
                            link(act_(dst, z, ACT.Copy, scale=QSCALE if what == "q" else 1.0))
                            sc.sem_inc(QKV_a, 1)
                            sc.sem_inc(bk.freed(s), 1)
                    elif kind == "prep":
                        sc.wait_ge(D_ready, (LEVELS + 1) * l + s[2] + 1)
                        buf = W[:, s[2] % 2]
                        act_(buf, buf, ACT.Exp, scale=GATE_SCALE[l]).then_inc(E_ready, 1)
                    elif kind == "inter":
                        sc.wait_ge(D_ready, (LEVELS + 1) * (l + 1))
                        act_(W[:, 1], W[:, 1], ACT.Exp, scale=GATE_SCALE[l]).then_inc(E_ready, 1)
                        c_last = C[:].rearrange("p h (i j) -> p h i j", j=P)[:, :, :, P - 1]
                        link(act_(el[:], c_last, ACT.Exp, scale=GATE_SCALE[l]))
                        act_(W[:, 0], C[:].rearrange("p h n -> p (h n)"), ACT.Exp,
                             scale=GATE_SCALE[l]).then_inc(E_ready, 1)
                        for i in range(NT - 1):
                            key = (*s, i)
                            bk.wait_full(sc, key)
                            link(act_(K[:, i], bank(key), ACT.Copy))
                            sc.sem_inc(keT_ready, 1)
                            sc.sem_inc(bk.freed(key), 1)
                    elif kind == "out":
                        head_norm(s, l, dv_of(l))
                    elif kind == "da":
                        i = s[2]
                        if i < NT * NH:
                            n = (i // NH + 1) * P
                            sc.wait_ge(nb_ready, i + 1)
                            s0 = bk.uses[("score", i)][0]
                            if i >= 2:
                                sc.wait_ge(wgt_ready, i - 1)
                            for c in range(2):
                                ins = act_(prob[:, i % 2, c, 0:n], PS[:, s0 + c, 0:n], ACT.Exp, scale=DASCALE,
                                           bias=nb[:, i % 2, c:c + 1], accum_out=sm[:, i % 2, c:c + 1])
                                if c == 0:
                                    link(ins)
                                else:
                                    link(ins)
                            sc.sem_inc(p_ready, 1)
                            sc.sem_inc(bk.freed(("score", i)), 1)
                        if i:
                            i -= 1
                            n = (i // NH + 1) * P
                            key = ("wT", i)
                            bk.wait_full(sc, key)
                            link(act_(wgtT[:, i % 2, 0:n], bank(key)[:, 0:n], ACT.Copy))
                            sc.sem_inc(wT_ready, 1)
                            sc.sem_inc(bk.freed(key), 1)
                            if i % NH == NH - 1:
                                head_norm(("pv", i // NH), l, DVS[0])
                transposes(("oT", l))
                norm(2 * l + 1)
                transposes(("hT", 2 * l + 1))
                if l + 1 < NL:
                    load_norm(2 * l + 2)
                sc.wait_ge(r_gl, l + 1)
                act_(rt["eg"][:], rt["eg"][:], ACT.Exp).then_inc(r_eg, 1)
                sc.wait_ge(r_x2, l + 1)
                act_(rt["e2"][:], rt["e2"][:], ACT.Exp).then_inc(r_e2, 1)
                bk.wait_full(sc, ("first", l, 0))
                link(act_(xgT[:, 0:4], bank(("first", l, 0)).rearrange("p (k n) -> p k n", k=4), ACT.Copy))
                sc.sem_inc(xgT_ready, 1)
                sc.sem_inc(bk.freed(("first", l, 0)), 1)

                def block_act(b, last):
                    g0 = l * NB
                    bk.wait_full(sc, ("gate", l), b)
                    sc.wait_ge(act_ready, b + g0) if l or not isinstance(b, int) or b else None
                    act_(ex[:], bank(("gate", l)), ACT.Exp, scale=-1.0).then_inc(ex_ready, 1)
                    if not last:
                        key = ("xgT", l, 0)
                        bk.wait_full(sc, key, b)
                        link(act_(xgT[:, 0:4], bank(key).rearrange("p (k n) -> p k n", k=4), ACT.Copy))
                        sc.sem_inc(xgT_ready, 1)
                        sc.sem_inc(bk.freed(key), 1)
                    key = ("actT", l)
                    bk.wait_full(sc, key, b)
                    link(act_(actT[:].rearrange("p k n -> p (k n)"), bank(key), ACT.Copy))
                    sc.sem_inc(actT_ready, 1)
                    sc.sem_inc(bk.freed(key), 1)
                    sc.wait_ge(y_stored, b * 16 + 16 * g0) if l or not isinstance(b, int) or b else None
                    for c in range(2):
                        key = (f"down{c}", l)
                        bk.wait_full(sc, key, b)
                        link(act_(yb[:, c * GC:(c + 1) * GC], bank(key), ACT.Copy))
                        sc.sem_inc(bk.freed(key), 1)
                    sc.dma_start(ybuf[l][bass.ds(b * P, P), :], yb[:]).then_inc(y_stored, 16)

                link.enter(0, 4)
                if True:
                    link.i = None
                    n0 = link.n
                    block_act(0, False)
                    per = link.n - n0
                    with sc.Fori(1, NB - 1) as b:
                        link.enter(b - 1, per)
                        block_act(b, False)
                        link.leave(NB - 2)
                    block_act(NB - 1, True)

        @block.tensor
        def _(pe):
            def transposes(key, src, ready, n0):
                for i in range(NT):
                    if ready is not None:
                        pe.wait_ge(ready, n0 + i + 1)
                    for g in range(2):
                        k = (*key, i, g)
                        bk.acquire(pe, k)
                        for c in range(4):
                            d = (4 * g + c) * P
                            ins = pe.transpose(bank(k)[:, c * P:(c + 1) * P], src[:, i, d:d + P], ident[:])
                        ins.then_inc(bk.filled(k), 1)

            pe.wait_ge(consts, 10)
            nT = 0
            for l in range(NL):
                n_g = first_group[l]
                transposes(("hT", 2 * l), h, h_ready, NT * 2 * l)
                nT += 1
                pe.wait_ge(hT_a, NT * nT)
                pe.wait_ge(hT_v, NT * nT)
                n_da = 0
                for s in STEPS[l]:
                    kind = s[0]
                    if kind == "alpha":
                        pe.wait_ge(par2, 16 * 4)
                        bk.acquire(pe, s)
                        for k in range(KD):
                            ins = pe.matmul(bank(s)[0:RANK, :], wa[:, k, :], hT[:, k, :], start=k == 0, stop=k == KD - 1)
                        ins.then_inc(bk.filled(s), 1)
                        pe.wait_ge(aT_ready, 1)
                        for u in range(4):
                            key = (*s, u)
                            bk.acquire(pe, key)
                            pe.matmul(bank(key), walpha[0:RANK, u * P:(u + 1) * P], aT[0:RANK, :], start=True,
                                      stop=True).then_inc(bk.filled(key), 1)
                    elif kind == "proj":
                        _, _, what, u = s
                        g = n_g + [k for k, _ in MIX[l]].index(what)
                        if u == 0:
                            pe.wait_ge(w_loaded[g % 3], 16 * (g // 3 + 1))
                        bk.acquire(pe, s)
                        wg = wbuf[:, g % 3]
                        by_feature = what in ("f", "q", "k")
                        for k in range(KD):
                            a, b = ((wg[:, k, u * P:(u + 1) * P], hT[:, k, :]) if by_feature
                                    else (hT[:, k, u * P:(u + 1) * P], wg[:, k, :]))
                            ins = pe.matmul(bank(s), a, b, start=k == 0, stop=k == KD - 1)
                        ins.then_inc(bk.filled(s), 1)
                        if u == 3:
                            pe.wait_ge(bk.filled(s), bk.uses[s][1])
                            pe.sem_inc(w_used, 1)
                        if what in ("dq", "dk"):
                            key = ("dT", *s[1:])
                            n_da += 1
                            pe.wait_ge(st_ready, n_da)
                            bk.acquire(pe, key)
                            for c in range(NH):
                                ins = pe.transpose(bank(key)[:, c * P:(c + 1) * P],
                                                   stag[:, u % 2, c * P:(c + 1) * P], ident[:])
                            ins.then_inc(bk.filled(key), 1)
                    elif kind == "mm":
                        lev = s[2]
                        if lev < LEVELS:
                            pe.wait_ge(X_ready, (LEVELS + 2) * l + lev + 1)
                        for i in range(NT):
                            key = (*s, i)
                            bk.acquire(pe, key)
                            for c in range(NH):
                                if lev < LEVELS:
                                    a = b = W[:, lev % 2, c * T + i * P:c * T + (i + 1) * P]
                                else:
                                    a, b = K[:, c, i * P:(i + 1) * P], Q[:, c, i * P:(i + 1) * P]
                                ins = pe.matmul(bank(key)[:, c * P:(c + 1) * P], a, b, start=True, stop=True)
                            ins.then_inc(bk.filled(key), 1)
                    elif kind == "inter":
                        pe.wait_ge(X_ready, (LEVELS + 2) * l + LEVELS + 1)
                        for i in range(NT - 1):
                            key = (*s, i)
                            bk.acquire(pe, key)
                            for c in range(NH):
                                ins = pe.transpose(bank(key)[:, c * P:(c + 1) * P],
                                                   W[:, 1, c * T + i * P:c * T + (i + 1) * P], ident[:])
                            ins.then_inc(bk.filled(key), 1)
                        pe.wait_ge(X_ready, (LEVELS + 2) * l + LEVELS + 2)
                        pe.wait_ge(QKV_a, 4 if l == 0 else 8 + 16)
                    elif kind == "out":
                        i = s[2]
                        dv = dv_of(l)
                        if i < NT - 1:
                            key = ("dS", l, i)
                            pe.wait_ge(keT_ready, (NT - 1) * l + i + 1)
                            bk.acquire(pe, key)
                            ds_ = PS[:, 4:4 + NBK[l], :].rearrange("p a b -> p (a b)")
                            for c in range(NH):
                                ins = pe.matmul(ds_[:, c * dv:(c + 1) * dv], K[:, i, c * P:(c + 1) * P],
                                                h[:, i, c * dv:(c + 1) * dv], start=True, stop=True)
                            ins.then_inc(bk.filled(key), 1)
                        bk.acquire(pe, s)
                        o_ = PS[:, 6:6 + NBK[l], :].rearrange("p a b -> p (a b)")
                        if i:
                            pe.wait_ge(S_ready, (NT - 1) * l + i)
                        for c in range(NH):
                            ins = pe.matmul(o_[:, c * dv:(c + 1) * dv], AT[:, i, c], h[:, i, c * dv:(c + 1) * dv],
                                            start=True, stop=i == 0)
                            if i:
                                ins = pe.matmul(o_[:, c * dv:(c + 1) * dv], W[:, 0, c * T + i * P:c * T + (i + 1) * P],
                                                S[l][:, (i - 1) % 2, c], start=False, stop=True)
                        ins.then_inc(bk.filled(s), 1)
                    elif kind == "da":
                        i = s[2]
                        if i == 0:
                            pe.wait_ge(daT, 2 * NT)
                            pe.wait_ge(QKV_a, 8)
                        if i < NT * NH:
                            ti, c = divmod(i, NH)
                            n = (ti + 1) * P
                            key = ("score", i)
                            bk.acquire(pe, key)
                            s0 = bk.uses[key][0]
                            for m in range(2):
                                r = slice(m * DA_D, (m + 1) * DA_D)
                                ins = pe.matmul(PS[:, s0 + m, 0:n], dqT[r, c, ti * P:(ti + 1) * P], dkT[r, c, 0:n],
                                                start=True, stop=True)
                            ins.then_inc(bk.filled(key), 1)
                        if i:
                            i -= 1
                            ti, c = divmod(i, NH)
                            key = ("wT", i)
                            pe.wait_ge(wgt_ready, i + 1)
                            bk.acquire(pe, key)
                            for j in range(ti + 1):
                                ins = pe.transpose(bank(key)[:, j * P:(j + 1) * P], wgt[:, i % 2, j * P:(j + 1) * P],
                                                   ident[:])
                            ins.then_inc(bk.filled(key), 1)
                            pe.wait_ge(wT_ready, i + 1)
                            key = ("pv", ti)
                            if c == 0:
                                bk.acquire(pe, key)
                            for j in range(ti + 1):
                                ins = pe.matmul(bank(key)[:, c * P:(c + 1) * P], wgtT[:, i % 2, j * P:(j + 1) * P],
                                                h[:, j, GC + c * P:GC + (c + 1) * P], start=j == 0, stop=j == ti)
                            if c == NH - 1:
                                ins.then_inc(bk.filled(key), 1)
                pe.wait_ge(o_done, 2 * NT if l == 0 else 3 * NT)
                transposes(("oT", l), G, None, 0)
                nT += 1
                pe.wait_ge(hT_a, NT * nT)
                pe.wait_ge(hT_v, NT * nT)
                n_g += len(MIX[l])
                for c in range(2):
                    g = n_g + c
                    pe.wait_ge(w_loaded[g % 3], 16 * (g // 3 + 1))
                    for i in range(NT):
                        key = ("wo", l, c, i)
                        bk.acquire(pe, key)
                        for k in range(KD):
                            ins = pe.matmul(bank(key), hT[:, k, i * P:(i + 1) * P], wbuf[:, g % 3, k, :],
                                            start=k == 0, stop=k == KD - 1)
                        ins.then_inc(bk.filled(key), 1)
                    pe.wait_ge(bk.filled(key), bk.uses[key][1])
                    pe.sem_inc(w_used, 1)
                n_g += 2
                transposes(("hT", 2 * l + 1), h, h_ready, NT * (2 * l + 1))
                nT += 1
                pe.wait_ge(hT_a, NT * nT)
                pe.wait_ge(hT_v, NT * nT)
                key = ("route", l)
                pe.wait_ge(rw_loaded, 16 * (NG + 3) * (l + 1))
                bk.acquire(pe, key)
                for i in range(NT):
                    for k in range(KD):
                        ins = pe.matmul(bank(key)[:, i * NR:(i + 1) * NR], hT[:, k, i * P:(i + 1) * P], rw[:, k, :],
                                        start=k == 0, stop=k == KD - 1)
                ins.then_inc(bk.filled(key), 1)
                key = ("rank", l)
                pe.wait_ge(M_ready, l + 1)
                bk.acquire(pe, key)
                M = rt["M"]
                for i in range(NT + 1):
                    n = min(i, NT - 1) + 1 if i < NT else NT
                    for k in range(n):
                        own = i < NT and k == i
                        ins = pe.matmul(bank(key)[:, i * NE:(i + 1) * NE], (triu if own else ones)[:], M[:, k, :],
                                        start=k == 0, stop=k == n - 1)
                ins.then_inc(bk.filled(key), 1)
                key = ("idx", l)
                bk.acquire(pe, key)
                for k in range(2 * NT):
                    pe.wait_ge(oh_ready, 2 * NT * l + k + 1)
                    ins = pe.matmul(bank(key)[:, 0:24], ohj[:, k % 2], ohb[:, k % 2], start=k == 0, stop=k == 2 * NT - 1)
                    ins.then_inc(bk.filled(key) if k == 2 * NT - 1 else idx_step, 1)
                for g in range(2):
                    key = ("first", l, g)
                    bk.acquire(pe, key)
                    if g == 0:
                        pe.wait_ge(gathered, 16 * (l * NB + 1))
                    for c in range(4):
                        ins = pe.transpose(bank(key)[:, c * P:(c + 1) * P], xg[:, (4 * g + c) * P:(4 * g + c + 1) * P],
                                           ident[:])
                    ins.then_inc(bk.filled(key), 1)
                ring = [(n_g + g) % 3 for g in range(3)]

                def weights(g, b):
                    n = n_g + g
                    pe.wait_ge(w_loaded[n % 3], b * 16 + 16 * (n // 3 + 1))
                    return wbuf[:, ring[g]]

                def done_with_weights(key, b):
                    s_, n, _ = bk.uses[key]
                    pe.wait_ge(bk.full[s_], b + n)
                    pe.sem_inc(w_used, 1)

                def block_pe(b, last):
                    g0 = l * NB
                    pe.wait_ge(xgT_ready, b * 2 + 2 * (g0 + 1))
                    for g, name in enumerate(("gate", "up")):
                        key = (name, l)
                        wg = weights(g, b)
                        bk.acquire_in_loop(pe, key, b)
                        for k in range(KD):
                            ins = pe.matmul(bank(key), xgT[:, k], wg[:, k, :], start=k == 0, stop=k == KD - 1)
                        ins.then_inc(bk.filled(key), 1)
                        if g == 1:
                            done_with_weights(("gate", l), b)
                    if not last:
                        pe.wait_ge(gathered, b * 16 + 16 * (g0 + 2))
                        for g in range(2):
                            key = ("xgT", l, g)
                            bk.acquire_in_loop(pe, key, b)
                            for c in range(4):
                                ins = pe.transpose(bank(key)[:, c * P:(c + 1) * P],
                                                   xg[:, (4 * g + c) * P:(4 * g + c + 1) * P], ident[:])
                            ins.then_inc(bk.filled(key), 1)
                    done_with_weights(("up", l), b)
                    key = ("actT", l)
                    pe.wait_ge(act_ready, b + (g0 + 1))
                    bk.acquire_in_loop(pe, key, b)
                    for c in range(DE // P):
                        ins = pe.transpose(bank(key)[:, c * P:(c + 1) * P], act[:, c * P:(c + 1) * P], ident[:])
                    ins.then_inc(bk.filled(key), 1)
                    wg = weights(2, b)
                    pe.wait_ge(actT_ready, b + (g0 + 1))
                    for c in range(2):
                        key = (f"down{c}", l)
                        bk.acquire_in_loop(pe, key, b)
                        for k in range(DE // P):
                            ins = pe.matmul(bank(key), actT[:, k], wg[:, 2 * k + c, :], start=k == 0,
                                            stop=k == DE // P - 1)
                        ins.then_inc(bk.filled(key), 1)
                    done_with_weights(("down1", l), b)

                with pe.Fori(0, NB - 1) as b:
                    block_pe(b, False)
                block_pe(NB - 1, True)

        @block.vector
        def _(ve):
            link = Chain(ve, v_step)
            tt, ts, stt, cp = ve.tensor_tensor, ve.tensor_scalar, ve.scalar_tensor_tensor, ve.tensor_copy
            red = ve.tensor_reduce
            e_uses, x_count = [0], [0]
            o_stats = [0]

            link(ve.memset(AT[:], 0.0))
            link(ve.memset(reset[:], 1.0))
            link(ve.memset(reset[:].rearrange("p (i j) -> p i j", j=P)[:, :, 0], 0.0))
            ve.wait_ge(consts, 10)
            link(tt(xx[:], ii[:], jj[:], ALU.bitwise_xor))
            link(tt(m1_[:], ii[:], jj[:], ALU.is_gt))
            for s in range(LEVELS):
                link(stt(m2_[:], xx[:], float(1 << s), m1_[:], ALU.is_ge, ALU.mult))
                link(stt(masks[:, s], xx[:], float(2 << s), m2_[:], ALU.is_lt, ALU.mult))
            link(tt(masks[:, LEVELS], ii[:], jj[:], ALU.is_equal))
            ve.sem_inc(masks_ready, 1)
            ve.wait_ge(par1, 16 * 8)
            link(tt(lb[:, NH:2 * NH], lb[:, 0:NH], lb[:, 0:NH], ALU.subtract))
            link(ts(lb[:, NH:2 * NH], lb[:, NH:2 * NH], 1.0, None, ALU.add))
            link(ve.reciprocal(lbt[:, 0], lb[:, NH:2 * NH]))
            link(tt(lbt[:, 1], lb[:, NH:2 * NH], lbt[:, 0], ALU.mult))
            link(tt(lb[:, NH:2 * NH], lbt[:, 1], lbt[:, 1], ALU.subtract))
            link(ts(lb[:, 2 * NH:3 * NH], lb[:, NH:2 * NH], -1.0, 1.0, ALU.mult, ALU.add))
            for c in range(2):
                v = lamv[:].rearrange("p (a n) -> p a n", a=4)
                link(tt(v[:, 2 * c], v[:, 2 * c], v[:, 2 * c + 1], ALU.mult))
                ins = red(lam[:, 2 + c:3 + c], v[:, 2 * c], AX, ALU.add)
                if c == 0:
                    link(ins)
                else:
                    ins.then_inc(lam_s, 1)
            link(ts(subw[:], subw[:], 1.0 - LAM0, None, ALU.mult))

            def norm(n):
                ve.wait_ge(rstd_done, n + 1)
                ve.wait_ge(nw_loaded, 16 * (n + 1))
                if n == 0:
                    pass
                for i in range(NT):
                    ins = stt(h[:, i], x[:, i], rstd[:, i:i + 1], normw[:], ALU.mult, ALU.mult)
                    ins.then_inc(h_ready, 1)
                ve.sem_inc(etmp_free, 1)

            def transposes(key):
                for i in range(NT):
                    bk.wait_full(ve, (*key, i, 1))
                    link(cp(hT[:, 4:8, i * P:(i + 1) * P], bank((*key, i, 1)).rearrange("p (k n) -> p k n", k=4)))
                    ve.sem_inc(hT_v, 1)
                    ve.sem_inc(bk.freed((*key, i, 1)), 1)

            def wait_e():
                e_uses[0] += 1
                ve.wait_ge(e_ready, e_uses[0])

            def head_norm(key, l, dv, i, outer, dst):
                z = PS[:, bk.uses[key][0]:bk.uses[key][0] + NH * dv // GC, :].rearrange("p a b -> p (a b)")
                wait_e()
                e = etmp[:].rearrange("p a b -> p (a b)")[:, 0:NH * dv].rearrange("p (h n) -> p h n", h=NH)
                link(red(ss[:, 0:NH], e, AX, ALU.add))
                ve.sem_inc(sig_ready, 1)
                ve.sem_inc(etmp_free, 1)
                o_stats[0] += 1
                ve.wait_ge(o_stat, o_stats[0])
                for c in range(NH):
                    link(stt(dst[:, c * dv:(c + 1) * dv], z[:, c * dv:(c + 1) * dv], rstd[:, c:c + 1],
                             outer(c), ALU.mult, ALU.mult))
                ve.sem_inc(o_done, 1)
                ve.sem_inc(bk.freed(key), 1)

            for l in range(NL):
                norm(2 * l)
                transposes(("hT", 2 * l))
                sgn = [(0, 0)]
                Cf = C[:].rearrange("p h n -> p (h n)")
                Qf, Kf = Q[:].rearrange("p h n -> p (h n)"), K[:].rearrange("p h n -> p (h n)")
                if l:
                    ve.wait_ge(par2, 16 * 4)
                n_da = 0
                for s in STEPS[l]:
                    kind = s[0]
                    if kind == "alpha":
                        bk.wait_full(ve, s)
                        link(cp(aT[0:RANK, :], bank(s)[0:RANK, :]))
                        ve.sem_inc(aT_ready, 1)
                        ve.sem_inc(bk.freed(s), 1)
                        for u in range(4):
                            key = (*s, u)
                            bk.wait_full(ve, key)
                            b_ = balpha[:, u:u + 1]
                            link(ts(etmp[:, 0], bank(key), b_, None, ALU.add))
                            link(stt(etmp[:, 1], etmp[:, 0], -1.0, etmp[:, 0], ALU.mult, ALU.max))
                            ve.sem_inc(bk.freed(key), 1)
                            ve.sem_inc(sig_ready, 1)
                            wait_e()
                            link(stt(C[:, u], etmp[:, 0], 0.0, etmp[:, 1], ALU.min, ALU.subtract))
                            ve.sem_inc(etmp_free, 1)
                    elif kind == "proj":
                        _, _, what, u = s
                        z = bank(s)
                        e0, e1 = etmp[:, 0], etmp[:, 1]
                        if what in ("q", "g", "g2") and not (l == 1 and what == "q"):
                            wait_e()
                            link(ts(e0, e0, 1.0, None, ALU.add))
                            link(ve.reciprocal(e0, e0))
                            if what == "q":
                                link(stt(Q[:, u], z, QSCALE, e0, ALU.mult, ALU.mult))
                            else:
                                c0 = GC if what == "g2" else 0
                                dv = dv_of(l)
                                gd = G[:, u, c0:c0 + GC]
                                link(tt(gd, z, e0, ALU.mult))
                                gd = gd.rearrange("p (h n) -> p h n", n=dv)
                                link(tt(gd, gd, onw[:, 0:dv].unsqueeze(1).broadcast_to([P, GC // dv, dv]), ALU.mult))
                            ve.sem_inc(QKV_v, 1)
                            ve.sem_inc(bk.freed(s), 1)
                            ve.sem_inc(etmp_free, 1)
                        elif what == "f":
                            wait_e()
                            link(ts(etmp[:], etmp[:], 1.0, None, ALU.add))
                            link(ve.reciprocal(etmp[:], etmp[:]))
                            link(ts(K[:, u], e1, lb[:, 2 * NH + u:2 * NH + u + 1], None, ALU.mult))
                            ve.sem_inc(sig_ready, 1)
                        elif what in ("dq", "dk"):
                            wait_e()
                            link(red(ss[:], e0.rearrange("p (g n) -> p g n", n=DA_D), AX, ALU.add))
                            ve.sem_inc(sig_ready, 1)
                            ve.sem_inc(etmp_free, 1)
                            o_stats[0] += 1
                            ve.wait_ge(o_stat, o_stats[0])
                            link(tt(stag[:, u % 2].rearrange("p (g n) -> p g n", n=DA_D),
                                    z.rearrange("p (g n) -> p g n", n=DA_D),
                                    rstd[:].unsqueeze(2).broadcast_to([P, 8, DA_D]), ALU.mult))
                            ve.sem_inc(st_ready, 1)
                            ve.sem_inc(bk.freed(s), 1)
                    elif kind == "cum":
                        if l == 0:
                            ve.wait_ge(C_ready, NH)
                        for c in range(NH):
                            link(ve.tensor_tensor_scan(C[:, c], reset[:], C[:, c], 0.0, ALU.mult, ALU.add))
                        if l:
                            ve.wait_ge(QKV_a, 8 + 8)
                    elif kind == "prep":
                        lev = s[2]
                        half = 1 << lev
                        n = (LEVELS + 2) * l + lev
                        buf = W[:, lev % 2].rearrange("p (m c j) -> p m c j", c=2, j=half)
                        Cv = Cf.rearrange("p (m c j) -> p m c j", c=2, j=half)
                        mid = Cv[:, :, 0, half - 1:half].broadcast_to([P, NH * T // (2 * half), half])
                        if lev >= 2:
                            for i in range(NT):
                                bk.wait_full(ve, ("mm", l, lev - 2, i))
                        elif l == 1:
                            pass
                        tt(buf[:, :, 0], mid, Cv[:, :, 0], ALU.subtract).then_inc(v_half, 1)
                        halves[0] += 1
                        tt(buf[:, :, 1], Cv[:, :, 1], mid, ALU.subtract).then_inc(D_ready, 1)
                        ve.wait_ge(v_half, halves[0])
                        ve.wait_ge(E_ready, (LEVELS + 2) * l + lev + 1)
                        Kv = Kf.rearrange("p (m c j) -> p m c j", c=2, j=half)
                        Qv = Qf.rearrange("p (m c j) -> p m c j", c=2, j=half)
                        link(tt(buf[:, :, 0], buf[:, :, 0], Kv[:, :, 0], ALU.mult))
                        link(tt(buf[:, :, 1], buf[:, :, 1], Qv[:, :, 1], ALU.mult))
                        ve.sem_inc(X_ready, 1)
                    elif kind == "put":
                        for i in range(NT):
                            key = ("mm", *s[1:], i)
                            bk.wait_full(ve, key)
                            m = masks[:, s[2]].unsqueeze(1).broadcast_to([P, NH, P])
                            ve.copy_predicated(AT[:, i], m, bank(key).rearrange("p (h n) -> p h n", h=NH)
                                               ).then_inc(bk.freed(key), 1)
                    elif kind == "inter":
                        for i in range(NT):
                            bk.wait_full(ve, ("mm", l, LEVELS, i))
                        n = (LEVELS + 2) * l + LEVELS
                        Cv = C[:].rearrange("p h (i j) -> p (h i) j", j=P)
                        last = Cv[:, :, P - 1:P].broadcast_to([P, NH * NT, P])
                        tt(W[:, 1].rearrange("p (m j) -> p m j", j=P), last, Cv, ALU.subtract).then_inc(D_ready, 1)
                        ve.wait_ge(E_ready, n + 1)
                        tt(W[:, 1], W[:, 1], Kf, ALU.mult).then_inc(X_ready, 1)
                        ve.wait_ge(E_ready, n + 2)
                        tt(W[:, 0], W[:, 0], Qf, ALU.mult).then_inc(X_ready, 1)
                    elif kind == "out":
                        i = s[2]
                        dv = dv_of(l)
                        if i < NT - 1:
                            key = ("dS", l, i)
                            bk.wait_full(ve, key)
                            if i == 2:
                                bk.wait_full(ve, ("out", l, 1))
                            ds_ = PS[:, 4:4 + NBK[l], :].rearrange("p a b -> p (a b)")
                            for c in range(NH):
                                z = ds_[:, c * dv:(c + 1) * dv]
                                if i == 0:
                                    link(cp(S[l][:, 0, c], z))
                                else:
                                    link(stt(S[l][:, i % 2, c], S[l][:, (i - 1) % 2, c], el[:, c, i:i + 1], z,
                                             ALU.mult, ALU.add))
                            ve.sem_inc(S_ready, 1)
                            ve.sem_inc(bk.freed(key), 1)
                        head_norm(s, l, dv, i, lambda c: G[:, i, c * dv:(c + 1) * dv], G[:, i, 0:NH * dv])
                    elif kind == "da":
                        i = s[2]
                        if i == 0:
                            ve.wait_ge(lam_e, 1)
                            link(tt(lam[:, 2:3], lam[:, 1:2], lam[:, 0:1], ALU.subtract))
                            link(ts(lam[:, 3:4], lam[:, 2:3], -LAM0, None, ALU.add))
                        if i < NT * NH:
                            n = (i // NH + 1) * P
                            key = ("score", i)
                            bk.wait_full(ve, key)
                            s0 = bk.uses[key][0]
                            sc_ = PS[:, s0:s0 + 2, 0:n]
                            diag = PS[:, s0:s0 + 2, n - P:n]
                            link(tt(diag, diag, negmask[:].unsqueeze(1).broadcast_to([P, 2, P]), ALU.add))
                            link(red(mx[:, i % 2], sc_, AX, ALU.max))
                            ts(nb[:, i % 2], mx[:, i % 2], -DASCALE, None, ALU.mult).then_inc(nb_ready, 1)
                            if i >= 2:
                                bk.wait_full(ve, ("wT", i - 2))
                            ve.wait_ge(p_ready, i + 1)
                            link(ve.reciprocal(rs[:, i % 2], sm[:, i % 2]))
                            link(tt(rs[:, i % 2, 1:2], rs[:, i % 2, 1:2], lam[:, 3:4], ALU.mult))
                            link(ts(wgt[:, i % 2, 0:n], prob[:, i % 2, 0, 0:n], rs[:, i % 2, 0:1], None, ALU.mult))
                            stt(wgt[:, i % 2, 0:n], prob[:, i % 2, 1, 0:n], rs[:, i % 2, 1:2], wgt[:, i % 2, 0:n],
                                ALU.mult, ALU.add).then_inc(wgt_ready, 1)
                        if i and i % NH == 0:
                            ti = i // NH - 1
                            head_norm(("pv", ti), l, DVS[0], ti, lambda c: subw[:], G[:, ti, GC:D])
                transposes(("oT", l))
                for c in range(2):
                    for i in range(NT):
                        key = ("wo", l, c, i)
                        bk.wait_full(ve, key)
                        xs = x[:, i, c * GC:(c + 1) * GC]
                        link(tt(xs, bank(key), xs, ALU.add))
                        ve.sem_inc(bk.freed(key), 1)
                        if c == 1:
                            ve.sem_inc(x_new, 1)
                norm(2 * l + 1)
                transposes(("hT", 2 * l + 1))
                r = {k: v[:] for k, v in rt.items()}
                key = ("route", l)
                bk.wait_full(ve, key)
                link(tt(r["L"], bank(key)[:, 0:NT * NR].rearrange("p (i n) -> p i n", n=NR),
                        rb[:].unsqueeze(1).broadcast_to([P, NT, NR]), ALU.add))
                ve.sem_inc(bk.freed(key), 1)
                gl = r["L"][:, :, 0:NG]
                elg = r["L"][:, :, NG:NR]

                def bc(a, n):
                    return a.unsqueeze(2).broadcast_to([P, NT, n])

                def first_of(oh, v, m):
                    link(tt(oh, v, bc(m, NG), ALU.is_equal))
                    it = iota_f[:, 0:NG].unsqueeze(1).broadcast_to([P, NT, NG])
                    link(stt(r["cand"], oh, -64.0, it, ALU.mult, ALU.add))
                    link(red(r["m"], r["cand"], AX, ALU.min))
                    link(tt(oh, r["cand"], bc(r["m"], NG), ALU.is_equal))

                link(red(r["gmax"], gl, AX, ALU.max))
                link(tt(r["eg"], gl, bc(r["gmax"], NG), ALU.subtract))
                ve.sem_inc(r_gl, 1)
                first_of(r["ohg"], gl, r["gmax"])
                for i in range(NT):
                    link(tt(r["sel"][:, i], elg[:, i].rearrange("p (g e) -> p e g", g=NG),
                            r["ohg"][:, i].unsqueeze(1).broadcast_to([P, EPG, NG]), ALU.mult))
                link(red(r["xl"], r["sel"], AX, ALU.add))
                link(red(r["m1"], r["xl"], AX, ALU.max))
                first_of(r["oh1"], r["xl"], r["m1"])
                link(stt(r["xl2"], r["oh1"], NEG, r["xl"], ALU.mult, ALU.add))
                link(red(r["m2"], r["xl2"], AX, ALU.max))
                link(tt(r["e2"], r["m2"], r["m1"], ALU.subtract))
                ve.sem_inc(r_x2, 1)
                first_of(r["oh2"], r["xl2"], r["m2"])
                for c, oh in enumerate(("oh1", "oh2")):
                    for i in range(NT):
                        link(tt(r["OH"][:, c, i].rearrange("p (g e) -> p g e", g=NG),
                                r["ohg"][:, i].unsqueeze(2).broadcast_to([P, NG, EPG]),
                                r[oh][:, i].unsqueeze(1).broadcast_to([P, NG, EPG]), ALU.mult))
                link(tt(r["M"], r["OH"][:, 0], r["OH"][:, 1], ALU.add))
                ve.sem_inc(M_ready, 1)
                ve.wait_ge(r_eg, l + 1)
                link(red(r["gsum"], r["eg"], AX, ALU.add))
                ve.wait_ge(r_e2, l + 1)
                link(ts(r["den"], r["e2"], 1.0, None, ALU.add))
                link(tt(r["den"], r["den"], r["gsum"], ALU.mult))
                link(ve.reciprocal(r["wt"][:, 0], r["den"]))
                link(tt(r["wt"][:, 1], r["wt"][:, 0], r["e2"], ALU.mult))
                key = ("rank", l)
                bk.wait_full(ve, key)
                link(cp(r["R"], bank(key)[:, 0:NT * NE].rearrange("p (i n) -> p i n", n=NE)))
                link(cp(r["N"], bank(key)[:, NT * NE:(NT + 1) * NE]))
                ve.sem_inc(bk.freed(key), 1)
                link(ts(r["nx"], r["N"], float(CAP), None, ALU.is_gt))
                link(stt(r["nx"], r["N"], 2.0 * CAP, r["nx"], ALU.is_gt, ALU.add))
                link(stt(r["nx"], r["N"], 3.0 * CAP, r["nx"], ALU.is_gt, ALU.add))
                link(ve.tensor_tensor_scan(r["off"], ones[:, 0:NE], r["nx"], 0.0, ALU.mult, ALU.add))
                link(tt(r["off"], r["off"], r["nx"], ALU.subtract))
                link(ts(r["q"], r["R"], float(CAP), None, ALU.is_ge))
                link(tt(r["ein"][:, 0], r["off"], iota_f[:, 0:NE], ALU.subtract))
                link(ts(r["ein"][:, 0], r["ein"][:, 0], float(NE - 1), None, ALU.add))
                link(tt(r["b"], r["q"], r["ein"][:, 0:1].broadcast_to([P, NT, NE]), ALU.mult))
                link(stt(r["q"], r["R"], 2.0 * CAP, r["q"], ALU.is_ge, ALU.add))
                link(stt(r["q"], r["R"], 3.0 * CAP, r["q"], ALU.is_ge, ALU.add))
                link(tt(r["b"], r["b"], r["q"], ALU.add))
                link(tt(r["b"], r["b"], iota_f[:, 0:NE].unsqueeze(1).broadcast_to([P, NT, NE]), ALU.add))
                link(stt(r["j"], r["q"], -float(CAP), r["R"], ALU.mult, ALU.add))
                for c in range(2):
                    link(tt(r["tA"], r["OH"][:, c], r["b"], ALU.mult))
                    link(red(r["bc"][:, c], r["tA"], AX, ALU.add))
                    link(tt(r["tA"], r["OH"][:, c], r["j"], ALU.mult))
                    link(red(r["jc"][:, c], r["tA"], AX, ALU.add))
                link(stt(r["sl"], r["bc"], float(CAP), r["jc"], ALU.mult, ALU.add))
                link(cp(slot[:], r["sl"]))
                for c in range(2):
                    for i in range(NT):
                        k = c * NT + i
                        if k >= 2:
                            ve.wait_ge(idx_step, (2 * NT - 1) * l + k - 1)
                        link(ts(ohj[:, k % 2], iota_f[:], r["jc"][:, c, i:i + 1], None, ALU.is_equal))
                        link(ts(ohb[:, k % 2], iota_f[:, 0:24], r["bc"][:, c, i:i + 1], tok_id[:, i:i + 1],
                                ALU.is_equal, ALU.mult))
                        ve.sem_inc(oh_ready, 1)
                key = ("idx", l)
                bk.wait_full(ve, key)
                link(cp(idx[:], bank(key)[:, 0:24]))
                ve.sem_inc(idx_ready, 1)
                ve.sem_inc(bk.freed(key), 1)
                it8 = iota_f[:, 0:8].unsqueeze(2).broadcast_to([P, 8, NE])
                off8 = r["off"].unsqueeze(1).broadcast_to([P, 8, NE])
                nx8 = r["nx"].unsqueeze(1).broadcast_to([P, 8, NE])
                link(tt(r["ein"], it8, off8, ALU.subtract))
                link(tt(r["ein2"], r["ein"], nx8, ALU.is_lt))
                link(stt(r["ein2"], r["ein"], 0.0, r["ein2"], ALU.is_ge, ALU.mult))
                link(tt(r["ein2"], r["ein2"], iota_f[:, 0:NE].unsqueeze(1).broadcast_to([P, 8, NE]), ALU.mult))
                link(red(r["eidf"], r["ein2"], AX, ALU.add))
                link(cp(eid[:], r["eidf"]))
                ve.sem_inc(eid_ready, 1)
                key = ("first", l, 1)
                bk.wait_full(ve, key)
                link(cp(xgT[:, 4:8], bank(key).rearrange("p (k n) -> p k n", k=4)))
                ve.sem_inc(xgT_ready, 1)
                ve.sem_inc(bk.freed(key), 1)

                def block_ve(b, last):
                    g0 = l * NB
                    ve.wait_ge(ex_ready, b + (g0 + 1))
                    link(ts(ex[:], ex[:], 1.0, None, ALU.add))
                    link(ve.reciprocal(ex[:], ex[:]))
                    if l or not isinstance(b, int) or b:
                        s_, n_, _ = bk.uses[("actT", l)]
                        if n_ > 1 or not isinstance(b, int) or b:
                            ve.wait_ge(bk.full[s_], b + (n_ - 1))
                    link(tt(act[:], bank(("gate", l)), ex[:], ALU.mult))
                    ve.sem_inc(bk.freed(("gate", l)), 1)
                    bk.wait_full(ve, ("up", l), b)
                    link(tt(act[:], bank(("up", l)), act[:], ALU.mult))
                    ve.sem_inc(act_ready, 1)
                    ve.sem_inc(bk.freed(("up", l)), 1)
                    if not last:
                        key = ("xgT", l, 1)
                        bk.wait_full(ve, key, b)
                        link(cp(xgT[:, 4:8], bank(key).rearrange("p (k n) -> p k n", k=4)))
                        ve.sem_inc(xgT_ready, 1)
                        ve.sem_inc(bk.freed(key), 1)

                n0 = link.n
                block_ve(0, False)
                per = link.n - n0
                with ve.Fori(1, NB - 1) as b:
                    link.enter(b - 1, per)
                    block_ve(b, False)
                    link.leave(NB - 2)
                block_ve(NB - 1, True)
                for c in range(2):
                    for i in range(NT):
                        k = c * NT + i
                        ve.wait_ge(yg_sem[k % 4], 16 * (2 * l + k // 4 + 1))
                        if c:
                            ve.wait_ge(x_new, NT * (3 * l + 1) + i + 1)
                        stt(x[:, i], yg[:, k % 4], r["wt"][:, c, i:i + 1], x[:, i], ALU.mult, ALU.add
                            ).then_inc(x_new, 1)


_INS = ['x', 'attn_norm', 'ffn_norm', 'even_w_in', 'even_w_out', 'hg_lb_logits', 'hg_o_norm', 'da_q_norm',
        'da_k_norm', 'da_lambda', 'da_subln', 'odd_w_in', 'gla_w_alpha', 'gla_b_alpha', 'gla_o_norm', 'odd_w_out',
        'moe_w_group', 'moe_b_group', 'moe_w_router', 'moe_b_router', 'moe_w_gate', 'moe_w_up', 'moe_w_down']


def kernel(**inputs):
    import numpy as _np
    import concourse.bacc as _bacc
    from concourse import mybir as _mybir
    from concourse.bass_utils import run_bass_kernel_spmd as _run

    nc = _bacc.Bacc("TRN2", target_bir_lowering=False, num_devices=1)
    arrays, t = {}, {}
    for name in _INS:
        a = _np.ascontiguousarray(inputs[name])
        arrays[f"in_{name}"] = a
        t[name] = nc.dram_tensor(f"in_{name}", a.shape, _mybir.dt.from_np(a.dtype), kind="ExternalInput").ap()
    t["out"] = nc.dram_tensor("out_x", inputs["x"].shape, _mybir.dt.float32, kind="ExternalOutput").ap()
    build(nc, t)
    r = _run(nc, [arrays], core_ids=[0])
    return r.results[0]["out_x"]
```

```python
from contextlib import ExitStack

import concourse.bass as bass
from concourse import mybir

F32 = mybir.dt.float32
I32 = mybir.dt.int32
U8 = mybir.dt.uint8
ALU = mybir.AluOpType
ACT = mybir.ActivationFunctionType
AX = mybir.AxisListType.X

P = 128
EPS = 1e-6
NEG = -1e30


class PsumBanks:

    def __init__(self, full, free):
        self.full, self.free = full, free
        self.count = [0] * 8
        self.last = [None] * 8
        self.uses = {}

    def plan(self, key, banks):
        s = banks[0]
        before = sorted({self.last[b] for b in banks if self.last[b] is not None})
        self.count[s] += 1
        self.uses[key] = (s, self.count[s], before)
        for b in banks:
            self.last[b] = (s, self.count[s])

    def plan_loop(self, key, bank, rounds):
        self.uses[key] = (bank, self.count[bank] + 1, [])
        self.count[bank] += rounds
        self.last[bank] = (bank, self.count[bank])

    def acquire(self, pe, key):
        for s, n in self.uses[key][2]:
            pe.wait_ge(self.free[s], n)

    def acquire_in_loop(self, pe, key, i):
        s, n, _ = self.uses[key]
        pe.wait_ge(self.free[s], i + (n - 1))

    def wait_full(self, eng, key, i=0):
        s, n, _ = self.uses[key]
        eng.wait_ge(self.full[s], i + n)

    def filled(self, key):
        return self.full[self.uses[key][0]]

    def freed(self, key):
        return self.free[self.uses[key][0]]


class Chain:

    def __init__(self, eng, sem):
        self.eng, self.sem, self.n, self.i, self.per = eng, sem, 0, None, 0

    def __call__(self, ins):
        self.n += 1
        ins.then_inc(self.sem, 1)
        if self.i is None:
            self.eng.wait_ge(self.sem, self.n)
        else:
            self.eng.wait_ge(self.sem, self.i * self.per + self.n)

    def enter(self, i, per):
        self.i, self.per, self.start = i, per, self.n

    def leave(self, rounds):
        assert self.n - self.start == self.per
        self.n = self.start + self.per * rounds
        self.i = None


def build(nc, t):
    x_in = t["x"]
    B, T, D = x_in.shape
    NT = T // P
    KD = D // P
    NL = t["attn_norm"].shape[0]
    HW = t["hg_lb_logits"].shape[1]
    NH = 4
    DK = P
    DVS = (t["hg_o_norm"].shape[1], t["gla_o_norm"].shape[1])
    DA_D = t["da_q_norm"].shape[1]
    RANK = t["gla_w_alpha"].shape[1]
    NG, EPG = t["moe_w_group"].shape[2], t["moe_w_router"].shape[3]
    NE = NG * EPG
    NR = NG + NE
    DE = t["moe_w_gate"].shape[3]
    CAP = 96
    NX = (2 * T - 1) // CAP
    NB = NE + NX
    NBC = 32
    FULLS = T // CAP
    GC = 512
    LAM0 = 0.2
    QSCALE = float(DK) ** -0.5
    DASCALE = float(DA_D) ** -0.5
    GATE_SCALE = (1.0, 1.0 / 16.0)
    LEVELS = 7
    assert (B, NT, KD, NL, HW, DE, NH * DVS[1]) == (1, 4, 8, 2, 512, 512, D) and NB <= NBC

    EVEN = [("f", 1), ("q", 0), ("dq", 4), ("dk", 5), ("dv", 6), ("v", 2), ("g", 3)]
    ODD = [("q", 0), ("k", 1), ("v", 2), ("v2", 3), ("g", 4), ("g2", 5)]
    MIX = [EVEN, ODD]
    first_group = [0, len(EVEN) + 2 + 3 * NE]

    def mixer_steps(l):
        units = [("proj", l, k, u) for k, _ in MIX[l] for u in range(4)]
        levels = [[("cum", l), ("prep", l, 0)]]
        for s in range(1, LEVELS):
            levels.append([("prep", l, s), ("mm", l, s - 1), ("put", l, s - 1)])
        levels.append([("mm", l, LEVELS - 1), ("put", l, LEVELS - 1)])
        levels.append([("mm", l, LEVELS), ("put", l, LEVELS), ("inter", l)])
        da = [("da", l, i) for i in range(NT * NH + 1)] if l == 0 else []
        steps = ([("alpha", l)] if l == 1 else []) + units[:4 * 2]
        late = None
        for n, unit in enumerate(units[8:]):
            steps.append(unit)
            if late:
                steps.append(late)
            late = ("dT", *unit[1:]) if unit[2] in ("dq", "dk") else None
            if n < len(levels):
                steps += levels[n]
            if l == 0 and n >= 12:
                steps += da[2 * (n - 12):2 * (n - 12) + 2]
        steps += da[16:]
        for i in range(NT + 2):
            if i < NT:
                steps.append(("out", l, i))
            if 0 <= i - 1 < NT:
                steps.append(("oT", l, i - 1))
            if 0 <= i - 2 < NT:
                steps.append(("wo", l, 0, i - 2))
        for i in range(NT + 3):
            if i < NT:
                steps.append(("wo", l, 1, i))
            if 0 <= i - 1 < NT:
                steps.append(("h", 2 * l + 1, i - 1))
            if 0 <= i - 2 < NT:
                steps.append(("hT", 2 * l + 1, i - 2))
            if 0 <= i - 3 < NT:
                steps.append(("route", l, i - 3))
        return steps

    def norm_steps(n):
        steps = []
        for i in range(NT + 2):
            if i < NT:
                steps.append(("x", n, i))
            if 0 <= i - 1 < NT:
                steps.append(("h", n, i - 1))
            if 0 <= i - 2 < NT:
                steps.append(("hT", n, i - 2))
        return steps

    STEPS = [norm_steps(0) + mixer_steps(0), norm_steps(2) + mixer_steps(1)]
    NBK = [NH * dv // GC for dv in DVS]

    ctx = ExitStack()
    with ctx:
        base = nc.sbuf_base
        base += -base % 64
        cursor = [base]

        def at(name, shape, dt, offset):
            return nc.alloc_sbuf_tensor_at(name, shape, dt, offset=offset)

        def size_of(shape, dt):
            n = 1 if dt == U8 else 4
            for s in shape[1:]:
                n *= s
            return n + (-n % 64)

        def sb(name, shape, dt=F32):
            o = cursor[0]
            cursor[0] += size_of(shape, dt)
            return at(name, shape, dt, o)

        def sem(name):
            return ctx.enter_context(nc.semaphore(name))

        x = sb("x_sb", [P, NT, D])
        wbuf = sb("weight_ring", [P, 3, KD, GC])
        etmp = sb("exp_tmp", [P, 2, GC])
        ident = sb("ident", [P, P])
        masks = sb("level_masks", [P, LEVELS + 1, P], U8)
        ones = sb("ones", [P, P])
        triu = sb("tri_before", [P, P])
        negmask = sb("causal_neg", [P, P])
        reset = sb("scan_reset", [P, T], U8)
        iota_f = sb("iota_free", [P, P])
        tok_id = sb("token_id", [P, NT])
        normw = sb("norm_weight", [P, D])
        rw = sb("router_w", [P, KD, NR])
        rb = sb("router_b", [P, NR])
        lb = sb("lower_bound", [P, 4 * NH])
        onw = sb("o_norm_w", [P, DVS[1]])
        subw = sb("subln_w", [P, DVS[0]])
        dqw = sb("da_q_w", [P, 1])
        dkw = sb("da_k_w", [P, 1])
        lamv = sb("lambda_vecs", [P, 4 * DA_D])
        lam = sb("lambda", [P, 4])
        balpha = sb("b_alpha", [P, NH])
        walpha = sb("w_alpha", [P, NH * DK])
        wa = sb("w_a", [P, KD, RANK])
        ss = sb("sum_sq", [P, 8])
        rstd = sb("rstd", [P, 8])
        xss = sb("x_sum_sq", [P, NT])
        xrs = sb("x_rstd", [P, NT])
        el = sb("exp_last", [P, NH, NT])
        mx = sb("score_max", [P, 2, 2])
        nb = sb("score_bias", [P, 2, 2])
        sm = sb("score_sum", [P, 2, 2])
        rs = sb("score_rec", [P, 2, 2])
        arena = cursor[0]
        h = sb("h", [P, NT, D])
        hT = sb("hT", [P, KD, T])
        Q = sb("Q", [P, NH, T])
        K = sb("K", [P, NH, T])
        C = sb("C", [P, NH, T])
        G = sb("G", [P, NT, D])
        W = sb("W", [P, 2, NH * T])
        AT = sb("AT", [P, NT, NH, P])
        dqT = sb("dqT", [P, NH, T])
        dkT = sb("dkT", [P, NH, T])
        S_at = cursor[0]
        S0 = sb("S0", [P, 2, NH, DVS[0]])
        stag = sb("da_stage", [P, 2, GC])
        assert cursor[0] <= nc.sbuf_usable_end
        dq_at = S_at - 2 * NH * T * 4
        S1 = at("S1", [P, 2, NH, DVS[1]], F32, dq_at)
        aT = at("aT", [P, T], F32, dq_at + 2 * NH * DVS[1] * 4)
        S = [S0, S1]
        QE = Q[:].rearrange("p h n -> p (h n)")
        w_at = dq_at - NT * NH * P * 4 - 2 * NH * T * 4
        prob = at("prob", [P, 2, 2, T], F32, w_at)
        wgt = at("wgt", [P, 2, T], F32, w_at + 4 * T * 4)
        wgtT = at("wgtT", [P, 2, T], F32, w_at + 6 * T * 4)
        cursor[0] = arena + 2 * NT * D * 4
        xg = sb("xg", [P, D])
        xgT = sb("xgT", [P, 2, KD, CAP])
        ex = sb("ex", [P, DE])
        act = sb("act", [P, DE])
        actT = sb("actT", [P, DE // P, CAP])
        yb = sb("yb", [P, D])
        yg = sb("yg", [P, 4, D])
        ohj = sb("ohj", [P, 2, CAP])
        ohb = sb("ohb", [P, 2, NBC])
        idx = sb("idx", [CAP, NBC], I32)
        idxcol = sb("idxcol", [CAP, 1], I32)
        eid = sb("eid", [P, 16], I32)
        rt = {}
        for name, shape in dict(
            L=[NT, NR], gmax=[NT], cand=[NT, NG], m=[NT], ohg=[NT, NG], eg=[NT, NG], gsum=[NT], sel=[NT, EPG, NG],
            xl=[NT, EPG], m1=[NT], oh1=[NT, EPG], xl2=[NT, EPG], m2=[NT], oh2=[NT, EPG], e2=[NT], den=[NT],
            wt=[2, NT], OH=[2, NT, NE], M=[NT, NE], R=[NT, NE], N=[NE], nx=[NE], off=[NE], q=[NT, NE], j=[NT, NE],
            b=[NT, NE], tA=[NT, NE], bc=[2, NT], jc=[2, NT], sl=[2, NT], ein=[16, NE], ein2=[16, NE], eidf=[16],
        ).items():
            rt[name] = sb("r_" + name, [P] + shape)
        slot = sb("slot", [P, 2, NT], I32)
        ii, jj, xx, m1_, m2_ = (at(name, [P, P], I32, dq_at + 4 * P * n) for n, name in enumerate(
            ("iota_i", "iota_j", "iota_x", "mask_1", "mask_2")))
        lbt = at("lb_tmp", [P, 2, NH], F32, dq_at + 4 * P * 5)

        PS = ctx.enter_context(nc.psum_tensor("PS", [P, 8, GC], F32))

        hbuf = [nc.dram_tensor(f"h_rows{l}", (T, D), F32).ap() for l in range(NL)]
        ybuf = [nc.dram_tensor(f"y_rows{l}", (NB * CAP, D), F32).ap() for l in range(NL)]

        bk = PsumBanks([sem(f"bank{b}_full") for b in range(8)], [sem(f"bank{b}_free") for b in range(8)])
        x_loaded = [sem(f"x_loaded{i}") for i in range(NT)]
        par1, par2 = sem("params_even_loaded"), sem("params_rest_loaded")
        nw_loaded = sem("norm_weight_loaded")
        w_loaded = [sem(f"w_loaded{i}") for i in range(3)]
        rw_loaded = sem("router_loaded")
        consts = sem("consts_ready")
        masks_ready = sem("masks_ready")
        v_step, a_step = sem("vector_step"), sem("scalar_step")
        sq_done, rstd_done = sem("sq_done"), sem("rstd_done")
        h_ready, hT_a, hT_v = sem("h_ready"), sem("hT_by_scalar"), sem("hT_by_vector")
        x_new = sem("x_updated")
        e_ready, etmp_free = sem("exp_ready"), sem("exp_tmp_free")
        sig_ready = sem("sigmoid_ready")
        C_ready = sem("log_decay_ready")
        QKV_a, QKV_v = sem("heads_by_scalar"), sem("heads_by_vector")
        st_ready, daT = sem("da_staged"), sem("daT_ready")
        aT_ready = sem("aT_ready")
        D_ready, E_ready, X_ready = sem("diff_ready"), sem("decay_ready"), sem("scaled_ready")
        mm_done, put_done = sem("level_scored"), sem("level_put")
        keT_ready, S_ready = sem("keT_ready"), sem("state_ready")
        o_stat, o_done = sem("o_stat"), sem("o_done")
        nb_ready, p_ready, wgt_ready, wT_ready = sem("bias_ready"), sem("prob_ready"), sem("wgt_ready"), sem("wgtT_ready")
        lam_s, lam_e = sem("lambda_sums"), sem("lambda_exps")
        h_stored = sem("h_stored")
        r_gl, r_eg, r_x2, r_e2 = sem("r_groups"), sem("r_exp_groups"), sem("r_second"), sem("r_exp_second")
        M_ready, oh_ready, idx_ready, eid_ready = sem("assigned"), sem("onehots"), sem("idx_ready"), sem("eid_ready")
        idxcol_ready, gathered = sem("idxcol_ready"), sem("gathered")
        xgT_ready, ex_ready = sem("xgT_ready"), sem("gate_exp_ready")
        act_ready, actT_ready, y_ready, y_stored = sem("act_ready"), sem("actT_ready"), sem("y_ready"), sem("y_stored")
        yg_sem = [sem(f"y_gathered{i}") for i in range(4)]
        stored = sem("out_stored")
        ov_loaded = [sem(f"further_loaded{l}") for l in range(NL)]
        ov_col = [sem(f"further_idxcol{l}") for l in range(NL)]
        ov_gathered = [sem(f"further_gathered{l}") for l in range(NL)]
        ov_pe = [sem(f"further_by_tensor{l}") for l in range(NL)]
        ov_act = [sem(f"further_by_scalar{l}") for l in range(NL)]
        ov_ve = [sem(f"further_by_vector{l}") for l in range(NL)]
        ov_y = [sem(f"further_outputs{l}") for l in range(NL)]
        lb_ready = sem("lower_bound_ready")
        ov_stored = [sem(f"further_stored{l}") for l in range(NL)]
        idx_step, v_half = sem("idx_step"), sem("vector_half")
        gather_issued, group_taken = sem("gather_issued"), sem("group_taken")

        reader, qkv_no, tr_no = {}, {}, {}
        for l in range(NL):
            for s in STEPS[l]:
                kind = s[0]
                if kind == "alpha":
                    bk.plan(s, [4])
                    for u in range(4):
                        bk.plan((*s, u), [u])
                elif kind == "proj":
                    bk.plan(s, [s[3]])
                    reader[first_group[l] + [k for k, _ in MIX[l]].index(s[2])] = s
                    if s[2] not in ("dq", "dk"):
                        qkv_no[s] = len(qkv_no) + 1
                elif kind == "dT":
                    bk.plan(s, [s[3]])
                elif kind == "mm":
                    for i in range(NT):
                        bk.plan((*s, i), [4 + i])
                elif kind == "inter":
                    for i in range(NT - 1):
                        bk.plan((*s, i), [4 + i])
                elif kind == "out":
                    if s[2] < NT - 1:
                        bk.plan(("dS", l, s[2]), [4, 5][:NBK[l]])
                    bk.plan(s, [6, 7][:NBK[l]])
                elif kind == "da":
                    i = s[2]
                    if i < NT * NH:
                        bk.plan(("score", i), [4, 5])
                    if i:
                        bk.plan(("wT", i - 1), [6])
                        if (i - 1) % NH == 0:
                            bk.plan(("pv", (i - 1) // NH), [7])
                elif kind in ("hT", "oT"):
                    tr_no[s] = len(tr_no) + 1
                    for g in range(2):
                        bk.plan((*s, g), [(6 if kind == "hT" else 2) + g])
                elif kind == "wo":
                    bk.plan(s, [s[3] % 2 if s[2] == 0 else s[3]])
                    reader[first_group[l] + len(MIX[l]) + s[2]] = s
                elif kind == "route":
                    if s[2] == 0:
                        bk.plan(("route", l), [5])
            bk.plan(("rank", l), [4])
            bk.plan(("idx", l), [0])
            for k, b in (("gate", 0), ("up", 1), ("down0", 2), ("down1", 3), ("xgT0", 4), ("xgT1", 5), ("actT", 6)):
                bk.plan_loop((k, l), b, NE)

        def bank(key):
            return PS[:, bk.uses[key][0], :]

        def expert_loop(eng, body, link=None):
            body(0, 0)
            n0 = link.n if link else 0
            body(1, 1)
            body(2, 0)
            per = link.n - n0 if link else 0
            with eng.Fori(0, (NE - 6) // 2) as k:
                if link:
                    link.enter(k, per)
                body(k * 2 + 3, 1)
                body(k * 2 + 4, 0)
                if link:
                    link.leave((NE - 6) // 2)
            for b in range(NE - 3, NE):
                body(b, b % 2)

        block = ctx.enter_context(nc.Block())

        @block.sync
        def _(sp):
            def place_free(n, b=0):
                if n - 3 in reader:
                    bk.wait_full(sp, reader[n - 3], b)

            def load_group(n, src):
                place_free(n)
                sp.dma_start(wbuf[:, n % 3], src).then_inc(w_loaded[n % 3], 16)

            def cols(w, c):
                return w[:, c * GC:(c + 1) * GC].rearrange("(k p) n -> p k n", p=P)

            for i in range(NT):
                sp.dma_start(x[:, i], x_in[0, i * P:(i + 1) * P, :]).then_inc(x_loaded[i], 16)
                if i == 0:
                    load_group(0, cols(t["even_w_in"][0], EVEN[0][1]))
            for l in range(NL):
                n = first_group[l]
                if l == 0:
                    for i, (_, c) in enumerate(EVEN):
                        if i:
                            load_group(n + i, cols(t["even_w_in"][0], c))
                    for c in range(2):
                        load_group(n + len(EVEN) + c, cols(t["even_w_out"][0], c))
                n += len(MIX[l]) + 2

                def expert(name, e, slot_, s_, count=16):
                    src = t["moe_w_" + name][l, bass.ds(e, 1)].rearrange("a (k p) n -> p (a k) n", p=P)
                    dst = wbuf[:, slot_ % 3]
                    if name == "down":
                        dst = dst.rearrange("p (k c) n -> p k (c n)", c=2)
                    sp.dma_start(dst, src).then_inc(s_, 16)

                def taken(name, b):
                    bk.wait_full(sp, (name, l), b)
                    sp.sem_inc(group_taken, 1)

                place_free(n)
                expert("gate", 0, n, w_loaded[n % 3])
                place_free(n + 1)
                expert("up", 0, n + 1, w_loaded[(n + 1) % 3])
                place_free(n + 2)
                expert("gate", 1, n + 2, w_loaded[(n + 2) % 3])
                for i in range(NT):
                    sp.wait_ge(h_ready, NT * (2 * l + 1) + i + 1)
                    sp.dma_start(hbuf[l][i * P:(i + 1) * P, :], h[:, i]).then_inc(h_stored, 16)
                bk.wait_full(sp, ("gate", l), 0)
                expert("down", 0, n, w_loaded[n % 3])
                bk.wait_full(sp, ("up", l), 0)
                expert("up", 1, n + 1, w_loaded[(n + 1) % 3])
                with sp.Fori(1, NE - 1) as b:
                    taken("gate", b)
                    expert("gate", b + 1, n + 2, w_loaded[(n + 2) % 3])
                    taken("down1", b - 1)
                    expert("down", b, n, w_loaded[n % 3])
                    taken("up", b)
                    expert("up", b + 1, n + 1, w_loaded[(n + 1) % 3])
                bk.wait_full(sp, ("gate", l), NE - 1)
                expert("down", NE - 1, n + 2, w_loaded[(n + 2) % 3])
                reader[n + 45], reader[n + 46], reader[n + 47] = ("down1", l), ("up", l), ("down1", l)
                last_b = {n + 45: NE - 2, n + 46: NE - 1, n + 47: NE - 1}
                sp.wait_ge(eid_ready, l + 1)
                more = sp.value_load(eid[0:1, 15:16], min_val=0, max_val=NX)
                with sp.If(more > 0):
                    bk.wait_full(sp, ("down1", l), NE - 1)
                    with sp.Fori(0, NX) as b:
                        sp.wait_ge(ov_pe[l], b * 4 + 1)
                        sp.sem_inc(group_taken, 1)
                        e = sp.value_load(eid[0:1, bass.ds(b, 1)], min_val=0, max_val=NE - 1)
                        for g, name in enumerate(("gate", "up", "down")):
                            expert(name, e, g, ov_loaded[l])
                    sp.wait_ge(ov_pe[l], NX * 4 + 1)
                if l + 1 < NL:
                    for g in range(3):
                        bk.wait_full(sp, reader[n + 45 + g], last_b[n + 45 + g])
                        sp.dma_start(wbuf[:, (n + 48 + g) % 3], cols(t["odd_w_in"][0], MIX[1][g][1])
                                     ).then_inc(w_loaded[(n + 48 + g) % 3], 16)
                    for i in range(3, len(MIX[1])):
                        load_group(n + 48 + i, cols(t["odd_w_in"][0], MIX[1][i][1]))
                    for c in range(2):
                        load_group(n + 48 + len(MIX[1]) + c, cols(t["odd_w_out"][0], c))
            for i in range(NT):
                sp.wait_ge(x_new, (NL - 1) * 3 * NT + NT + 2 * (i + 1))
                sp.dma_start(t["out"][0, i * P:(i + 1) * P, :], x[:, i]).then_inc(stored, 16)
            sp.wait_ge(stored, 16 * NT)

        @block.gpsimd
        def _(pool):
            pool.memset(ident[:], 0.0).then_inc(consts, 1)
            pool.memset(ones[:], 1.0).then_inc(consts, 1)
            pool.memset(negmask[:], 0.0).then_inc(consts, 1)
            pool.wait_ge(consts, 3)
            pool.affine_select(out=ident[:], in_=ident[:], compare_op=ALU.not_equal, fill=1.0, base=0,
                               pattern=[[-1, P]], channel_multiplier=1).then_inc(consts, 1)
            pool.affine_select(out=triu[:], in_=ones[:], compare_op=ALU.is_gt, fill=0.0, base=0,
                               pattern=[[1, P]], channel_multiplier=-1).then_inc(consts, 1)
            pool.affine_select(out=negmask[:], in_=negmask[:], compare_op=ALU.is_ge, fill=NEG, base=0,
                               pattern=[[-1, P]], channel_multiplier=1).then_inc(consts, 1)
            pool.iota(iota_f[:], [[1, P]], base=0, channel_multiplier=0,
                      allow_small_or_imprecise_dtypes=True).then_inc(consts, 1)
            pool.iota(tok_id[:], [[P, NT]], base=0, channel_multiplier=1,
                      allow_small_or_imprecise_dtypes=True).then_inc(consts, 1)
            pool.iota(ii[:], [[1, P]], base=0, channel_multiplier=0).then_inc(consts, 1)
            pool.iota(jj[:], [[0, P]], base=0, channel_multiplier=1).then_inc(consts, 1)

            def gather(l, b, col, n0, done):
                pool.tensor_copy(idxcol[:], idx[:, bass.ds(b, 1)]).then_inc(col, 1)
                pool.wait_ge(col, n0)
                pool.sem_inc(gather_issued, 1)
                pool.indirect_dma_start(xg[0:CAP, :], None, hbuf[l][:], bass.IndirectOffsetOnAxis(idxcol[:], 0)
                                        ).then_inc(done, 16)

            def gather_outputs(l, blocks):
                for i in range(NT):
                    for c in range(2):
                        k = 2 * i + c
                        if k >= 4:
                            pool.wait_ge(x_new, NT * (3 * l + 1) + (k - 4) + 1)
                        pool.indirect_dma_start(yg[:, k % 4], None, ybuf[l][0:blocks * CAP], bass.IndirectOffsetOnAxis(
                            slot[:, c, i:i + 1], 0)).then_inc(yg_sem[k % 4], 16)

            for l in range(NL):
                pool.wait_ge(idx_ready, l + 1)
                pool.wait_ge(h_stored, 16 * NT * (l + 1))
                gather(l, 0, idxcol_ready, l * NE + 1, gathered)
                with pool.Fori(1, NE) as b:
                    bk.wait_full(pool, ("xgT1", l), b - 1)
                    gather(l, b, idxcol_ready, b + (l * NE + 1), gathered)
                pool.wait_ge(eid_ready, l + 1)
                more = pool.value_load(eid[0:1, 15:16], min_val=0, max_val=NX)
                pool.wait_ge(y_stored, 16 * NE * (l + 1))
                with pool.If(more > 0):
                    with pool.Fori(0, NX) as b:
                        pool.wait_ge(ov_pe[l], b * 4 + 1)
                        gather(l, b + NE, ov_col[l], b + 1, ov_gathered[l])
                    pool.wait_ge(ov_act[l], 4 * NX)
                    gather_outputs(l, NB)
                with pool.If(more < 1):
                    gather_outputs(l, NE)

        @block.scalar
        def _(sc):
            link = Chain(sc, a_step)
            act_ = sc.activation
            etmp_uses, e_uses, sig_uses = [0], [0], [0]

            def take_etmp():
                if etmp_uses[0]:
                    sc.wait_ge(etmp_free, etmp_uses[0])
                etmp_uses[0] += 1

            def wait_sums():
                sig_uses[0] += 1
                sc.wait_ge(sig_ready, sig_uses[0])

            def param(dst, src, s):
                sc.dma_start(dst, src, allow_slow_non_contiguous=True).then_inc(s, 16)

            def load_norm(n):
                if n:
                    sc.wait_ge(h_ready, NT * n)
                w = t["attn_norm"] if n % 2 == 0 else t["ffn_norm"]
                param(normw[:], w[n // 2:n // 2 + 1, :].broadcast_to([P, D]), nw_loaded)

            def load_router(l):
                param(rw[:, :, 0:NG], t["moe_w_group"][l].rearrange("(k p) g -> p k g", p=P), rw_loaded)
                for g in range(NG):
                    param(rw[:, :, NG + g * EPG:NG + (g + 1) * EPG],
                          t["moe_w_router"][l, g].rearrange("(k p) e -> p k e", p=P), rw_loaded)
                param(rb[:, 0:NG], t["moe_b_group"][l:l + 1, :].broadcast_to([P, NG]), rw_loaded)
                param(rb[:, NG:], t["moe_b_router"][l:l + 1].rearrange("a g e -> a (g e)").broadcast_to([P, NE]),
                      rw_loaded)

            def row_stat(n, i):
                if etmp_uses[0]:
                    sc.wait_ge(etmp_free, etmp_uses[0])
                act_(etmp[:].rearrange("p a b -> p (a b)"), x[:, i], ACT.Square,
                     accum_out=xss[:, i:i + 1]).then_inc(sq_done, 1)
                sc.wait_ge(sq_done, NT * n + i + 1)
                link(act_(xrs[:, i:i + 1], xss[:, i:i + 1], ACT.Ln, scale=1.0 / D, bias=EPS))
                act_(xrs[:, i:i + 1], xrs[:, i:i + 1], ACT.Exp, scale=-0.5).then_inc(rstd_done, 1)

            def head_norm(key, dv):
                nbk = NH * dv // GC
                z = PS[:, bk.uses[key][0]:bk.uses[key][0] + nbk, :]
                bk.wait_full(sc, key)
                take_etmp()
                act_(etmp[:, 0:nbk], z, ACT.Square).then_inc(e_ready, 1)
                wait_sums()
                link(act_(rstd[:, 0:NH], ss[:, 0:NH], ACT.Ln, scale=1.0 / dv, bias=EPS))
                act_(rstd[:, 0:NH], rstd[:, 0:NH], ACT.Exp, scale=-0.5).then_inc(o_stat, 1)

            load_norm(0)
            param(lb[:, 0:NH], t["hg_lb_logits"][0].rearrange("(h p) -> p h", p=P), par1)
            for half in range(2):
                param(dqw[half * DA_D:(half + 1) * DA_D, :], t["da_q_norm"].rearrange("a n -> n a"), par1)
                param(dkw[half * DA_D:(half + 1) * DA_D, :], t["da_k_norm"].rearrange("a n -> n a"), par1)
            param(lamv[:], t["da_lambda"].rearrange("a b n -> a (b n)").broadcast_to([P, 4 * DA_D]), par1)
            param(subw[:], t["da_subln"].broadcast_to([P, DVS[0]]), par1)
            param(onw[:, 0:DVS[0]], t["hg_o_norm"].broadcast_to([P, DVS[0]]), par1)
            for l in range(NL):
                for s in STEPS[l]:
                    kind = s[0]
                    if kind == "x":
                        _, n, i = s
                        if n == 0:
                            sc.wait_ge(x_loaded[i], 16)
                        else:
                            sc.wait_ge(x_new, NT + 2 * (i + 1))
                        row_stat(n, i)
                    elif kind in ("hT", "oT"):
                        key = (*s, 0)
                        i = s[2]
                        bk.wait_full(sc, key)
                        link(act_(hT[:, 0:4, i * P:(i + 1) * P],
                                  bank(key).rearrange("p (k n) -> p k n", k=4), ACT.Copy))
                        sc.sem_inc(hT_a, 1)
                        sc.sem_inc(bk.freed(key), 1)
                        if kind == "hT" and i == NT - 1:
                            if s[1] + 1 < 2 * NL:
                                load_norm(s[1] + 1)
                            if s[1] == 0:
                                sc.wait_ge(lam_s, 1)
                                act_(lam[:, 0:2], lam[:, 2:4], ACT.Exp).then_inc(lam_e, 1)
                                param(balpha[:], t["gla_b_alpha"][0].rearrange("(h p) -> p h", p=P), par2)
                                param(walpha[0:RANK, :], t["gla_w_alpha"][0], par2)
                                param(wa[:], t["odd_w_in"][0][:, NH * 2 * DK + 2 * D:].rearrange(
                                    "(k p) n -> p k n", p=P), par2)
                            if s[1] == 2:
                                param(onw[:], t["gla_o_norm"].broadcast_to([P, DVS[1]]), par2)
                            if s[1] % 2 == 0:
                                load_router(l)
                    elif kind == "alpha":
                        for u in range(4):
                            wait_sums()
                            link(act_(etmp[:, 1], etmp[:, 1], ACT.Exp, scale=-1.0))
                            act_(etmp[:, 1], etmp[:, 1], ACT.Ln, bias=1.0).then_inc(e_ready, 1)
                            etmp_uses[0] += 1
                    elif kind == "proj":
                        _, _, what, u = s
                        bk.wait_full(sc, s)
                        z = bank(s)
                        if what in ("dq", "dk"):
                            take_etmp()
                            act_(etmp[:, 0], z, ACT.Square).then_inc(e_ready, 1)
                            wait_sums()
                            link(act_(rstd[:], ss[:], ACT.Ln, scale=1.0 / DA_D, bias=EPS))
                            act_(rstd[:], rstd[:], ACT.Exp, scale=-0.5).then_inc(o_stat, 1)
                        else:
                            if what == "f":
                                link(act_(C[:, u], z, ACT.Sigmoid))
                                link(act_(K[:, u], z, ACT.Sigmoid, scale=-1.0))
                            elif what == "q" and l == 0:
                                link(act_(Q[:, u], z, ACT.Silu))
                            elif what in ("g", "g2"):
                                c0 = GC if what == "g2" else 0
                                link(act_(G[:, u, c0:c0 + GC], z, ACT.Silu))
                            elif what == "v":
                                link(act_(h[:, u, 0:GC], z, ACT.Copy))
                            elif what in ("v2", "dv"):
                                link(act_(h[:, u, GC:D], z, ACT.Copy))
                            else:
                                link(act_((Q if what == "q" else K)[:, u], z, ACT.Copy))
                            sc.sem_inc(QKV_a, 1)
                            sc.sem_inc(bk.freed(s), 1)
                    elif kind == "dT":
                        what, u = s[2:]
                        bk.wait_full(sc, s)
                        dst, w = (dqT, dqw) if what == "dq" else (dkT, dkw)
                        link(act_(dst[:, :, u * P:(u + 1) * P], bank(s).rearrange("p (h n) -> p h n", h=NH),
                             ACT.Copy, scale=w[:, 0:1]))
                        sc.sem_inc(daT, 1)
                        sc.sem_inc(bk.freed(s), 1)
                    elif kind == "cum":
                        if l == 0:
                            sc.wait_ge(lb_ready, 1)
                            for u in range(NH):
                                link(act_(C[:, u], C[:, u], ACT.Ln, scale=lb[:, 2 * NH + u:2 * NH + u + 1],
                                          bias=lb[:, NH + u:NH + u + 1]))
                                sc.sem_inc(C_ready, 1)
                    elif kind == "prep":
                        sc.wait_ge(D_ready, (LEVELS + 1) * l + s[2] + 1)
                        buf = W[:, s[2] % 2]
                        act_(buf, buf, ACT.Exp, scale=GATE_SCALE[l]).then_inc(E_ready, 1)
                    elif kind == "inter":
                        sc.wait_ge(D_ready, (LEVELS + 1) * (l + 1))
                        act_(W[:, 1], W[:, 1], ACT.Exp, scale=GATE_SCALE[l]).then_inc(E_ready, 1)
                        c_last = C[:].rearrange("p h (i j) -> p h i j", j=P)[:, :, :, P - 1]
                        link(act_(el[:], c_last, ACT.Exp, scale=GATE_SCALE[l]))
                        act_(W[:, 0], C[:].rearrange("p h n -> p (h n)"), ACT.Exp,
                             scale=GATE_SCALE[l]).then_inc(E_ready, 1)
                        for i in range(NT - 1):
                            key = (*s, i)
                            bk.wait_full(sc, key)
                            link(act_(K[:, i], bank(key), ACT.Copy))
                            sc.sem_inc(keT_ready, 1)
                            sc.sem_inc(bk.freed(key), 1)
                    elif kind == "out":
                        head_norm(s, DVS[l])
                    elif kind == "wo" and s[2] == 1:
                        i = s[3]
                        sc.wait_ge(x_new, 3 * NT * l + i + 1)
                        row_stat(2 * l + 1, i)
                    elif kind == "da":
                        i = s[2]
                        if i < NT * NH:
                            n = (i // NH + 1) * P
                            sc.wait_ge(nb_ready, i + 1)
                            s0 = bk.uses[("score", i)][0]
                            if i >= 2:
                                sc.wait_ge(wgt_ready, i - 1)
                            for c in range(2):
                                link(act_(prob[:, i % 2, c, 0:n], PS[:, s0 + c, 0:n], ACT.Exp, scale=DASCALE,
                                          bias=nb[:, i % 2, c:c + 1], accum_out=sm[:, i % 2, c:c + 1]))
                            sc.sem_inc(p_ready, 1)
                            sc.sem_inc(bk.freed(("score", i)), 1)
                        if i:
                            i -= 1
                            n = (i // NH + 1) * P
                            key = ("wT", i)
                            bk.wait_full(sc, key)
                            link(act_(wgtT[:, i % 2, 0:n], bank(key)[:, 0:n], ACT.Copy))
                            sc.sem_inc(wT_ready, 1)
                            sc.sem_inc(bk.freed(key), 1)
                            if i % NH == NH - 1:
                                head_norm(("pv", i // NH), DVS[0])
                sc.wait_ge(r_gl, l + 1)
                act_(rt["eg"][:], rt["eg"][:], ACT.Exp).then_inc(r_eg, 1)
                sc.wait_ge(r_x2, l + 1)
                act_(rt["e2"][:], rt["e2"][:], ACT.Exp).then_inc(r_e2, 1)

                def rows_T(b, par):
                    key = ("xgT0", l)
                    bk.wait_full(sc, key, b)
                    link(act_(xgT[:, par, 0:4], bank(key)[:, 0:4 * CAP].rearrange("p (k n) -> p k n", k=4), ACT.Copy))
                    sc.sem_inc(xgT_ready, 1)
                    sc.sem_inc(bk.freed(key), 1)

                def silu(b):
                    bk.wait_full(sc, ("gate", l), b)
                    if l or not isinstance(b, int) or b:
                        sc.wait_ge(act_ready, b + l * NE)
                    link(act_(ex[0:CAP], bank(("gate", l))[0:CAP], ACT.Silu))
                    sc.sem_inc(ex_ready, 1)
                    sc.sem_inc(bk.freed(("gate", l)), 1)

                def block_act(b, par):
                    last = isinstance(b, int) and b == NE - 1
                    if not last:
                        silu(b + 1)
                    key = ("actT", l)
                    bk.wait_full(sc, key, b)
                    link(act_(actT[:].rearrange("p k n -> p (k n)"), bank(key)[:, 0:4 * CAP], ACT.Copy))
                    sc.sem_inc(actT_ready, 1)
                    sc.sem_inc(bk.freed(key), 1)
                    if not (isinstance(b, int) and b >= NE - 2):
                        rows_T(b + 2, par)
                    if l or not isinstance(b, int) or b:
                        sc.wait_ge(y_stored, b * 16 + 16 * l * NE)
                    for c in range(2):
                        key = (f"down{c}", l)
                        bk.wait_full(sc, key, b)
                        link(act_(yb[0:CAP, c * GC:(c + 1) * GC], bank(key)[0:CAP], ACT.Copy))
                        sc.sem_inc(bk.freed(key), 1)
                    sc.dma_start(ybuf[l][bass.ds(b * CAP, CAP), :], yb[0:CAP, :]).then_inc(y_stored, 16)

                rows_T(0, 0)
                rows_T(1, 1)
                silu(0)
                expert_loop(sc, block_act, link)
                sc.wait_ge(eid_ready, l + 1)
                more = sc.value_load(eid[0:1, 15:16], min_val=0, max_val=NX)
                sc.wait_ge(y_stored, 16 * NE * (l + 1))
                with sc.If(more > 0):
                    with sc.Fori(0, NX) as b:
                        sc.wait_ge(ov_pe[l], b * 4 + 2)
                        for g in range(2):
                            ins = act_(xgT[:, 0, 4 * g:4 * g + 4], PS[:, 4 + g, 0:4 * CAP].rearrange(
                                "p (k n) -> p k n", k=4), ACT.Copy)
                        ins.then_inc(ov_act[l], 1)
                        sc.wait_ge(ov_pe[l], b * 4 + 3)
                        act_(ex[0:CAP], PS[0:CAP, 0, :], ACT.Silu).then_inc(ov_act[l], 1)
                        sc.wait_ge(ov_pe[l], b * 4 + 4)
                        act_(actT[:].rearrange("p k n -> p (k n)"), PS[:, 6, 0:4 * CAP], ACT.Copy
                             ).then_inc(ov_act[l], 1)
                        sc.wait_ge(ov_pe[l], b * 4 + 5)
                        act_(yb[0:CAP, :].rearrange("p (c n) -> p c n", c=2), PS[0:CAP, 2:4, :], ACT.Copy
                             ).then_inc(ov_y[l], 1)
                        sc.wait_ge(ov_y[l], b + 1)
                        sc.dma_start(ybuf[l][bass.ds(b * CAP + NE * CAP, CAP), :], yb[0:CAP, :]
                                     ).then_inc(ov_stored[l], 16)
                        sc.wait_ge(ov_stored[l], b * 16 + 16)
                        sc.sem_inc(ov_act[l], 1)

        @block.tensor
        def _(pe):
            pe.wait_ge(consts, 10)
            n_st = 0
            for l in range(NL):
                n_g = first_group[l]
                n_wo = n_g + len(MIX[l])
                first_wo = True
                for s in STEPS[l]:
                    kind = s[0]
                    if kind in ("hT", "oT"):
                        i = s[2]
                        if kind == "hT":
                            src = h
                            pe.wait_ge(h_ready, NT * s[1] + i + 1)
                        else:
                            src = G
                            pe.wait_ge(o_done, (NT if l == 0 else 2 * NT) + i + 1)
                        for g in range(2):
                            k = (*s, g)
                            bk.acquire(pe, k)
                            for c in range(4):
                                d = (4 * g + c) * P
                                ins = pe.transpose(bank(k)[:, c * P:(c + 1) * P], src[:, i, d:d + P], ident[:])
                            ins.then_inc(bk.filled(k), 1)
                    elif kind == "alpha":
                        n = tr_no[("hT", 2 * l, NT - 1)]
                        pe.wait_ge(hT_a, n)
                        pe.wait_ge(hT_v, n)
                        pe.wait_ge(par2, 16 * 4)
                        bk.acquire(pe, s)
                        for k in range(KD):
                            ins = pe.matmul(bank(s)[0:RANK, :], wa[:, k, :], hT[:, k, :], start=k == 0, stop=k == KD - 1)
                        ins.then_inc(bk.filled(s), 1)
                        pe.wait_ge(aT_ready, 1)
                        for u in range(4):
                            key = (*s, u)
                            bk.acquire(pe, key)
                            pe.matmul(bank(key), walpha[0:RANK, u * P:(u + 1) * P], aT[0:RANK, :], start=True,
                                      stop=True).then_inc(bk.filled(key), 1)
                    elif kind == "proj":
                        _, _, what, u = s
                        g = n_g + [k for k, _ in MIX[l]].index(what)
                        if g == n_g and u == 0:
                            n = tr_no[("hT", 2 * l, NT - 1)]
                            pe.wait_ge(hT_a, n)
                            pe.wait_ge(hT_v, n)
                        if u == 0:
                            pe.wait_ge(w_loaded[g % 3], 16 * (g // 3 + 1))
                        bk.acquire(pe, s)
                        wg = wbuf[:, g % 3]
                        by_feature = what in ("f", "q", "k")
                        for k in range(KD):
                            a, b = ((wg[:, k, u * P:(u + 1) * P], hT[:, k, :]) if by_feature
                                    else (hT[:, k, u * P:(u + 1) * P], wg[:, k, :]))
                            ins = pe.matmul(bank(s), a, b, start=k == 0, stop=k == KD - 1)
                        ins.then_inc(bk.filled(s), 1)
                    elif kind == "dT":
                        n_st += 1
                        pe.wait_ge(st_ready, n_st)
                        bk.acquire(pe, s)
                        for c in range(NH):
                            ins = pe.transpose(bank(s)[:, c * P:(c + 1) * P],
                                               stag[:, s[3] % 2, c * P:(c + 1) * P], ident[:])
                        ins.then_inc(bk.filled(s), 1)
                    elif kind == "mm":
                        lev = s[2]
                        if lev < LEVELS:
                            pe.wait_ge(X_ready, (LEVELS + 2) * l + lev + 1)
                        for i in range(NT):
                            key = (*s, i)
                            bk.acquire(pe, key)
                            for c in range(NH):
                                if lev < LEVELS:
                                    a = b = W[:, lev % 2, c * T + i * P:c * T + (i + 1) * P]
                                else:
                                    a, b = K[:, c, i * P:(i + 1) * P], Q[:, c, i * P:(i + 1) * P]
                                ins = pe.matmul(bank(key)[:, c * P:(c + 1) * P], a, b, start=True, stop=True)
                            ins.then_inc(bk.filled(key), 1)
                    elif kind == "inter":
                        pe.wait_ge(X_ready, (LEVELS + 2) * l + LEVELS + 1)
                        for i in range(NT - 1):
                            key = (*s, i)
                            bk.acquire(pe, key)
                            for c in range(NH):
                                ins = pe.transpose(bank(key)[:, c * P:(c + 1) * P],
                                                   W[:, 1, c * T + i * P:c * T + (i + 1) * P], ident[:])
                            ins.then_inc(bk.filled(key), 1)
                    elif kind == "out":
                        i = s[2]
                        dv = DVS[l]
                        if i == 0:
                            pe.wait_ge(X_ready, (LEVELS + 2) * l + LEVELS + 2)
                            pe.wait_ge(QKV_a, max(v for k, v in qkv_no.items() if k[1] == l and k[2] in ("v", "v2")))
                            pe.wait_ge(put_done, 4 * (LEVELS + 1) * (l + 1))
                        if i < NT - 1:
                            key = ("dS", l, i)
                            pe.wait_ge(keT_ready, (NT - 1) * l + i + 1)
                            bk.acquire(pe, key)
                            ds_ = PS[:, 4:4 + NBK[l], :].rearrange("p a b -> p (a b)")
                            for c in range(NH):
                                ins = pe.matmul(ds_[:, c * dv:(c + 1) * dv], K[:, i, c * P:(c + 1) * P],
                                                h[:, i, c * dv:(c + 1) * dv], start=True, stop=True)
                            ins.then_inc(bk.filled(key), 1)
                        bk.acquire(pe, s)
                        o_ = PS[:, 6:6 + NBK[l], :].rearrange("p a b -> p (a b)")
                        if i:
                            pe.wait_ge(S_ready, (NT - 1) * l + i)
                        for c in range(NH):
                            ins = pe.matmul(o_[:, c * dv:(c + 1) * dv], AT[:, i, c], h[:, i, c * dv:(c + 1) * dv],
                                            start=True, stop=i == 0)
                            if i:
                                ins = pe.matmul(o_[:, c * dv:(c + 1) * dv], QE[:, c * T + i * P:c * T + (i + 1) * P],
                                                S[l][:, (i - 1) % 2, c], start=False, stop=True)
                        ins.then_inc(bk.filled(s), 1)
                    elif kind == "da":
                        i = s[2]
                        if i == 0:
                            pe.wait_ge(daT, 2 * NT)
                            pe.wait_ge(QKV_a, qkv_no[("proj", 0, "dv", 3)])
                        if i < NT * NH:
                            ti, c = divmod(i, NH)
                            n = (ti + 1) * P
                            key = ("score", i)
                            bk.acquire(pe, key)
                            s0 = bk.uses[key][0]
                            for m in range(2):
                                r = slice(m * DA_D, (m + 1) * DA_D)
                                ins = pe.matmul(PS[:, s0 + m, 0:n], dqT[r, c, ti * P:(ti + 1) * P], dkT[r, c, 0:n],
                                                start=True, stop=True)
                            ins.then_inc(bk.filled(key), 1)
                        if i:
                            i -= 1
                            ti, c = divmod(i, NH)
                            key = ("wT", i)
                            pe.wait_ge(wgt_ready, i + 1)
                            bk.acquire(pe, key)
                            for j in range(ti + 1):
                                ins = pe.transpose(bank(key)[:, j * P:(j + 1) * P], wgt[:, i % 2, j * P:(j + 1) * P],
                                                   ident[:])
                            ins.then_inc(bk.filled(key), 1)
                            pe.wait_ge(wT_ready, i + 1)
                            key = ("pv", ti)
                            if c == 0:
                                bk.acquire(pe, key)
                            for j in range(ti + 1):
                                ins = pe.matmul(bank(key)[:, c * P:(c + 1) * P], wgtT[:, i % 2, j * P:(j + 1) * P],
                                                h[:, j, GC + c * P:GC + (c + 1) * P], start=j == 0, stop=j == ti)
                            if c == NH - 1:
                                ins.then_inc(bk.filled(key), 1)
                    elif kind == "wo":
                        _, _, c, i = s
                        g = n_wo + c
                        if i == 0:
                            pe.wait_ge(w_loaded[g % 3], 16 * (g // 3 + 1))
                        if c == 0:
                            pe.wait_ge(hT_a, tr_no[("oT", l, i)])
                            pe.wait_ge(hT_v, tr_no[("oT", l, i)])
                        bk.acquire(pe, s)
                        for k in range(KD):
                            ins = pe.matmul(bank(s), hT[:, k, i * P:(i + 1) * P], wbuf[:, g % 3, k, :],
                                            start=k == 0, stop=k == KD - 1)
                        ins.then_inc(bk.filled(s), 1)
                    elif kind == "route":
                        i = s[2]
                        key = ("route", l)
                        pe.wait_ge(hT_a, tr_no[("hT", 2 * l + 1, i)])
                        pe.wait_ge(hT_v, tr_no[("hT", 2 * l + 1, i)])
                        if i == 0:
                            pe.wait_ge(rw_loaded, 16 * (NG + 3) * (l + 1))
                            bk.acquire(pe, key)
                        for k in range(KD):
                            ins = pe.matmul(bank(key)[:, i * NR:(i + 1) * NR], hT[:, k, i * P:(i + 1) * P], rw[:, k, :],
                                            start=k == 0, stop=k == KD - 1)
                        if i == NT - 1:
                            ins.then_inc(bk.filled(key), 1)
                key = ("rank", l)
                pe.wait_ge(M_ready, l + 1)
                bk.acquire(pe, key)
                M = rt["M"]
                for i in range(NT + 1):
                    n = i + 1 if i < NT else NT
                    for k in range(n):
                        own = i < NT and k == i
                        ins = pe.matmul(bank(key)[:, i * NE:(i + 1) * NE], (triu if own else ones)[:], M[:, k, :],
                                        start=k == 0, stop=k == n - 1)
                ins.then_inc(bk.filled(key), 1)
                key = ("idx", l)
                bk.acquire(pe, key)
                for k in range(2 * NT):
                    pe.wait_ge(oh_ready, 2 * NT * l + k + 1)
                    ins = pe.matmul(bank(key)[0:CAP, 0:NBC], ohj[:, k % 2], ohb[:, k % 2], start=k == 0,
                                    stop=k == 2 * NT - 1)
                    ins.then_inc(bk.filled(key) if k == 2 * NT - 1 else idx_step, 1)

                def weights(pos, b):
                    n = n_wo + 2 + pos
                    pe.wait_ge(w_loaded[n % 3], b * 16 + 16 * (n // 3 + 1))
                    return wbuf[:, n % 3]

                def rows_T(b):
                    pe.wait_ge(gathered, b * 16 + 16 * (l * NE + 1))
                    for g in range(2):
                        key = (f"xgT{g}", l)
                        bk.acquire_in_loop(pe, key, b)
                        for c in range(4):
                            ins = pe.transpose(bank(key)[:, c * CAP:(c + 1) * CAP],
                                               xg[0:CAP, (4 * g + c) * P:(4 * g + c + 1) * P], ident[0:CAP, 0:CAP])
                        ins.then_inc(bk.filled(key), 1)

                def into(name, b, par, wg):
                    key = (name, l)
                    bk.acquire_in_loop(pe, key, b)
                    for k in range(KD):
                        ins = pe.matmul(bank(key)[0:CAP], xgT[:, par, k], wg[:, k, :], start=k == 0, stop=k == KD - 1)
                    ins.then_inc(bk.filled(key), 1)

                def block_pe(b, par):
                    is_int = isinstance(b, int)
                    last = is_int and b == NE - 1
                    if not last:
                        pe.wait_ge(xgT_ready, b * 2 + 2 * (l * NE + 2))
                        into("gate", b + 1, 1 - par, weights(2, b))
                    key = ("actT", l)
                    pe.wait_ge(act_ready, b + (l * NE + 1))
                    bk.acquire_in_loop(pe, key, b)
                    for c in range(DE // P):
                        ins = pe.transpose(bank(key)[:, c * CAP:(c + 1) * CAP], act[0:CAP, c * P:(c + 1) * P],
                                           ident[0:CAP, 0:CAP])
                    ins.then_inc(bk.filled(key), 1)
                    if not (is_int and b >= NE - 2):
                        rows_T(b + 2)
                    wg = weights(47, 0) if last else weights(3, b)
                    pe.wait_ge(actT_ready, b + (l * NE + 1))
                    for c in range(2):
                        key = (f"down{c}", l)
                        bk.acquire_in_loop(pe, key, b)
                        for k in range(DE // P):
                            ins = pe.matmul(bank(key)[0:CAP], actT[:, k], wg[:, 2 * k + c, :], start=k == 0,
                                            stop=k == DE // P - 1)
                        ins.then_inc(bk.filled(key), 1)
                    if not last:
                        into("up", b + 1, 1 - par, weights(4, b))

                rows_T(0)
                pe.wait_ge(xgT_ready, 2 * (l * NE + 1))
                into("gate", 0, 0, weights(0, 0))
                rows_T(1)
                into("up", 0, 0, weights(1, 0))
                expert_loop(pe, block_pe)
                pe.wait_ge(eid_ready, l + 1)
                more = pe.value_load(eid[0:1, 15:16], min_val=0, max_val=NX)
                pe.wait_ge(bk.freed(("down1", l)), bk.uses[("down1", l)][1] + NE - 1)
                with pe.If(more > 0):
                    pe.sem_inc(ov_pe[l], 1)
                    with pe.Fori(0, NX) as b:
                        pe.wait_ge(ov_gathered[l], b * 16 + 16)
                        for c in range(KD):
                            ins = pe.transpose(PS[:, 4 + c // 4, c % 4 * CAP:(c % 4 + 1) * CAP],
                                               xg[0:CAP, c * P:(c + 1) * P], ident[0:CAP, 0:CAP])
                        ins.then_inc(ov_pe[l], 1)
                        pe.wait_ge(ov_act[l], b * 4 + 1)
                        pe.wait_ge(ov_loaded[l], b * 48 + 48)
                        for g in range(2):
                            for k in range(KD):
                                ins = pe.matmul(PS[0:CAP, g, :], xgT[:, 0, k], wbuf[:, g, k, :], start=k == 0,
                                                stop=k == KD - 1)
                        ins.then_inc(ov_pe[l], 1)
                        pe.wait_ge(ov_ve[l], b + 1)
                        for c in range(DE // P):
                            ins = pe.transpose(PS[:, 6, c * CAP:(c + 1) * CAP], act[0:CAP, c * P:(c + 1) * P],
                                               ident[0:CAP, 0:CAP])
                        ins.then_inc(ov_pe[l], 1)
                        pe.wait_ge(ov_act[l], b * 4 + 3)
                        for c in range(2):
                            for k in range(DE // P):
                                ins = pe.matmul(PS[0:CAP, 2 + c, :], actT[:, k], wbuf[:, 2, 2 * k + c, :],
                                                start=k == 0, stop=k == DE // P - 1)
                        ins.then_inc(ov_pe[l], 1)
                        pe.wait_ge(ov_act[l], b * 4 + 4)

        @block.vector
        def _(ve):
            link = Chain(ve, v_step)
            tt, ts, stt, cp = ve.tensor_tensor, ve.tensor_scalar, ve.scalar_tensor_tensor, ve.tensor_copy
            red = ve.tensor_reduce
            e_uses, o_stats, halves, n_st = [0], [0], [0], [0]

            def wait_e():
                e_uses[0] += 1
                ve.wait_ge(e_ready, e_uses[0])

            def head_norm(key, dv, outer, dst):
                z = PS[:, bk.uses[key][0]:bk.uses[key][0] + NH * dv // GC, :].rearrange("p a b -> p (a b)")
                wait_e()
                e = etmp[:].rearrange("p a b -> p (a b)")[:, 0:NH * dv].rearrange("p (h n) -> p h n", h=NH)
                link(red(ss[:, 0:NH], e, AX, ALU.add))
                ve.sem_inc(sig_ready, 1)
                ve.sem_inc(etmp_free, 1)
                o_stats[0] += 1
                ve.wait_ge(o_stat, o_stats[0])
                for c in range(NH):
                    ins = stt(dst[:, c * dv:(c + 1) * dv], z[:, c * dv:(c + 1) * dv], rstd[:, c:c + 1],
                              outer(c), ALU.mult, ALU.mult)
                link(ins)
                ve.sem_inc(o_done, 1)
                ve.sem_inc(bk.freed(key), 1)

            def constants():
                link(ve.memset(AT[:], 0.0))
                link(ve.memset(reset[:], 1.0))
                link(ve.memset(reset[:].rearrange("p (i j) -> p i j", j=P)[:, :, 0], 0.0))
                ve.wait_ge(par1, 16 * 8)
                link(tt(lb[:, NH:2 * NH], lb[:, 0:NH], lb[:, 0:NH], ALU.subtract))
                link(ts(lb[:, NH:2 * NH], lb[:, NH:2 * NH], 1.0, None, ALU.add))
                link(ve.reciprocal(lbt[:, 0], lb[:, NH:2 * NH]))
                link(tt(lbt[:, 1], lb[:, NH:2 * NH], lbt[:, 0], ALU.mult))
                link(tt(lb[:, NH:2 * NH], lbt[:, 1], lbt[:, 1], ALU.subtract))
                link(ts(lb[:, 2 * NH:3 * NH], lb[:, NH:2 * NH], -1.0, 1.0, ALU.mult, ALU.add))
                ve.sem_inc(lb_ready, 1)
                for c in range(2):
                    v = lamv[:].rearrange("p (a n) -> p a n", a=4)
                    link(tt(v[:, 2 * c], v[:, 2 * c], v[:, 2 * c + 1], ALU.mult))
                    ins = red(lam[:, 2 + c:3 + c], v[:, 2 * c], AX, ALU.add)
                    if c == 0:
                        link(ins)
                    else:
                        ins.then_inc(lam_s, 1)
                link(ts(subw[:], subw[:], 1.0 - LAM0, None, ALU.mult))
                ve.wait_ge(consts, 10)
                link(tt(xx[:], ii[:], jj[:], ALU.bitwise_xor))
                link(tt(m1_[:], ii[:], jj[:], ALU.is_gt))
                for s in range(LEVELS):
                    link(stt(m2_[:], xx[:], float(1 << s), m1_[:], ALU.is_ge, ALU.mult))
                    link(stt(masks[:, s], xx[:], float(2 << s), m2_[:], ALU.is_lt, ALU.mult))
                link(tt(masks[:, LEVELS], ii[:], jj[:], ALU.is_equal))

            Cf = C[:].rearrange("p h n -> p (h n)")
            Qf, Kf = Q[:].rearrange("p h n -> p (h n)"), K[:].rearrange("p h n -> p (h n)")
            for l in range(NL):
                for s in STEPS[l]:
                    kind = s[0]
                    if kind == "h":
                        _, n, i = s
                        if i == 0:
                            ve.wait_ge(nw_loaded, 16 * (n + 1))
                            if n == 2:
                                ve.wait_ge(h_stored, 16 * NT)
                        ve.wait_ge(rstd_done, NT * n + i + 1)
                        stt(h[:, i], x[:, i], xrs[:, i:i + 1], normw[:], ALU.mult, ALU.mult).then_inc(h_ready, 1)
                    elif kind == "x" and s[1] == 2:
                        i = s[2]
                        for c in range(2):
                            k = 2 * i + c
                            ve.wait_ge(yg_sem[k % 4], 16 * (k // 4 + 1))
                            if c:
                                ve.wait_ge(x_new, NT + 2 * i + 1)
                            stt(x[:, i], yg[:, k % 4], rt["wt"][:, c, i:i + 1], x[:, i], ALU.mult, ALU.add
                                ).then_inc(x_new, 1)
                    elif kind in ("hT", "oT"):
                        key = (*s, 1)
                        i = s[2]
                        bk.wait_full(ve, key)
                        link(cp(hT[:, 4:8, i * P:(i + 1) * P], bank(key).rearrange("p (k n) -> p k n", k=4)))
                        ve.sem_inc(hT_v, 1)
                        ve.sem_inc(bk.freed(key), 1)
                        if s == ("hT", 0, NT - 1):
                            constants()
                    elif kind == "alpha":
                        ve.wait_ge(par2, 16 * 4)
                        bk.wait_full(ve, s)
                        link(cp(aT[0:RANK, :], bank(s)[0:RANK, :]))
                        ve.sem_inc(aT_ready, 1)
                        ve.sem_inc(bk.freed(s), 1)
                        for u in range(4):
                            key = (*s, u)
                            bk.wait_full(ve, key)
                            b_ = balpha[:, u:u + 1]
                            if u == 0:
                                ve.wait_ge(sq_done, NT * (2 * l + 1))
                            link(ts(etmp[:, 0], bank(key), b_, None, ALU.add))
                            link(stt(etmp[:, 1], etmp[:, 0], -1.0, etmp[:, 0], ALU.mult, ALU.max))
                            ve.sem_inc(bk.freed(key), 1)
                            ve.sem_inc(sig_ready, 1)
                            wait_e()
                            link(stt(C[:, u], etmp[:, 0], 0.0, etmp[:, 1], ALU.min, ALU.subtract))
                            ve.sem_inc(etmp_free, 1)
                    elif kind == "proj":
                        _, _, what, u = s
                        z = bank(s)
                        if what in ("g", "g2"):
                            ve.wait_ge(QKV_a, qkv_no[s])
                            c0 = GC if what == "g2" else 0
                            dv = DVS[l]
                            gd = G[:, u, c0:c0 + GC].rearrange("p (h n) -> p h n", n=dv)
                            link(tt(gd, gd, onw[:, 0:dv].unsqueeze(1).broadcast_to([P, GC // dv, dv]), ALU.mult))
                        elif what in ("dq", "dk"):
                            wait_e()
                            e0 = etmp[:, 0]
                            link(red(ss[:], e0.rearrange("p (g n) -> p g n", n=DA_D), AX, ALU.add))
                            ve.sem_inc(sig_ready, 1)
                            ve.sem_inc(etmp_free, 1)
                            o_stats[0] += 1
                            ve.wait_ge(o_stat, o_stats[0])
                            n_st[0] += 1
                            if n_st[0] > 2:
                                prev = ("dT", 0, "dq" if n_st[0] - 3 < NT else "dk", (n_st[0] - 3) % NT)
                                bk.wait_full(ve, prev)
                            link(tt(stag[:, u % 2].rearrange("p (g n) -> p g n", n=DA_D),
                                    z.rearrange("p (g n) -> p g n", n=DA_D),
                                    rstd[:].unsqueeze(2).broadcast_to([P, 8, DA_D]), ALU.mult))
                            ve.sem_inc(st_ready, 1)
                            ve.sem_inc(bk.freed(s), 1)
                    elif kind == "cum":
                        ve.wait_ge(QKV_a, qkv_no[("proj", l, MIX[l][1][0], NH - 1)])
                        ve.wait_ge(QKV_a, qkv_no[("proj", l, MIX[l][0][0], NH - 1)])
                        link(ts(Qf, Qf, QSCALE, None, ALU.mult))
                        if l == 0:
                            link(tt(K[:], K[:], lb[:, 2 * NH:3 * NH].unsqueeze(2).broadcast_to([P, NH, T]), ALU.mult))
                            ve.wait_ge(C_ready, NH)
                        for c in range(NH):
                            ins = ve.tensor_tensor_scan(C[:, c], reset[:], C[:, c], 0.0, ALU.mult, ALU.add)
                        link(ins)
                    elif kind == "prep":
                        lev = s[2]
                        half = 1 << lev
                        buf = W[:, lev % 2].rearrange("p (m c j) -> p m c j", c=2, j=half)
                        Cv = Cf.rearrange("p (m c j) -> p m c j", c=2, j=half)
                        mid = Cv[:, :, 0, half - 1:half].broadcast_to([P, NH * T // (2 * half), half])
                        if lev >= 2:
                            for i in range(NT):
                                bk.wait_full(ve, ("mm", l, lev - 2, i))
                        tt(buf[:, :, 0], mid, Cv[:, :, 0], ALU.subtract).then_inc(v_half, 1)
                        halves[0] += 1
                        tt(buf[:, :, 1], Cv[:, :, 1], mid, ALU.subtract).then_inc(D_ready, 1)
                        ve.wait_ge(v_half, halves[0])
                        ve.wait_ge(E_ready, (LEVELS + 2) * l + lev + 1)
                        Kv = Kf.rearrange("p (m c j) -> p m c j", c=2, j=half)
                        Qv = Qf.rearrange("p (m c j) -> p m c j", c=2, j=half)
                        tt(buf[:, :, 0], buf[:, :, 0], Kv[:, :, 0], ALU.mult)
                        link(tt(buf[:, :, 1], buf[:, :, 1], Qv[:, :, 1], ALU.mult))
                        ve.sem_inc(X_ready, 1)
                    elif kind == "put":
                        for i in range(NT):
                            key = ("mm", *s[1:], i)
                            bk.wait_full(ve, key)
                            m = masks[:, s[2]].unsqueeze(1).broadcast_to([P, NH, P])
                            link(ve.copy_predicated(AT[:, i], m, bank(key).rearrange("p (h n) -> p h n", h=NH)))
                            ve.sem_inc(bk.freed(key), 1)
                            ve.sem_inc(put_done, 1)
                    elif kind == "inter":
                        n = (LEVELS + 2) * l + LEVELS
                        Cv = C[:].rearrange("p h (i j) -> p (h i) j", j=P)
                        last = Cv[:, :, P - 1:P].broadcast_to([P, NH * NT, P])
                        tt(W[:, 1].rearrange("p (m j) -> p m j", j=P), last, Cv, ALU.subtract).then_inc(D_ready, 1)
                        ve.wait_ge(E_ready, n + 1)
                        tt(W[:, 1], W[:, 1], Kf, ALU.mult).then_inc(X_ready, 1)
                        ve.wait_ge(E_ready, n + 2)
                        tt(QE, W[:, 0], Qf, ALU.mult).then_inc(X_ready, 1)
                    elif kind == "out":
                        i = s[2]
                        dv = DVS[l]
                        if i < NT - 1:
                            key = ("dS", l, i)
                            bk.wait_full(ve, key)
                            if i == 2:
                                bk.wait_full(ve, ("out", l, 1))
                            ds_ = PS[:, 4:4 + NBK[l], :].rearrange("p a b -> p (a b)")
                            for c in range(NH):
                                z = ds_[:, c * dv:(c + 1) * dv]
                                if i == 0:
                                    ins = cp(S[l][:, 0, c], z)
                                else:
                                    ins = stt(S[l][:, i % 2, c], S[l][:, (i - 1) % 2, c], el[:, c, i:i + 1], z,
                                              ALU.mult, ALU.add)
                            link(ins)
                            ve.sem_inc(S_ready, 1)
                            ve.sem_inc(bk.freed(key), 1)
                        head_norm(s, dv, lambda c: G[:, i, c * dv:(c + 1) * dv], G[:, i, 0:NH * dv])
                    elif kind == "da":
                        i = s[2]
                        if i == 0:
                            ve.wait_ge(lam_e, 1)
                            link(tt(lam[:, 2:3], lam[:, 1:2], lam[:, 0:1], ALU.subtract))
                            link(ts(lam[:, 3:4], lam[:, 2:3], -LAM0, None, ALU.add))
                        if i < NT * NH:
                            n = (i // NH + 1) * P
                            key = ("score", i)
                            bk.wait_full(ve, key)
                            s0 = bk.uses[key][0]
                            diag = PS[:, s0:s0 + 2, n - P:n]
                            link(tt(diag, diag, negmask[:].unsqueeze(1).broadcast_to([P, 2, P]), ALU.add))
                            link(red(mx[:, i % 2], PS[:, s0:s0 + 2, 0:n], AX, ALU.max))
                            ts(nb[:, i % 2], mx[:, i % 2], -DASCALE, None, ALU.mult).then_inc(nb_ready, 1)
                            if i >= 2:
                                bk.wait_full(ve, ("wT", i - 2))
                            else:
                                bk.wait_full(ve, ("inter", 0, NT - 2))
                            ve.wait_ge(p_ready, i + 1)
                            link(ve.reciprocal(rs[:, i % 2], sm[:, i % 2]))
                            link(tt(rs[:, i % 2, 1:2], rs[:, i % 2, 1:2], lam[:, 3:4], ALU.mult))
                            link(ts(wgt[:, i % 2, 0:n], prob[:, i % 2, 0, 0:n], rs[:, i % 2, 0:1], None, ALU.mult))
                            stt(wgt[:, i % 2, 0:n], prob[:, i % 2, 1, 0:n], rs[:, i % 2, 1:2], wgt[:, i % 2, 0:n],
                                ALU.mult, ALU.add).then_inc(wgt_ready, 1)
                        if i and i % NH == 0:
                            ti = i // NH - 1
                            head_norm(("pv", ti), DVS[0], lambda c: subw[:], G[:, ti, GC:D])
                    elif kind == "wo":
                        _, _, c, i = s
                        bk.wait_full(ve, s)
                        xs = x[:, i, c * GC:(c + 1) * GC]
                        link(tt(xs, bank(s), xs, ALU.add))
                        ve.sem_inc(bk.freed(s), 1)
                        if c == 1:
                            ve.sem_inc(x_new, 1)
                r = {k: v[:] for k, v in rt.items()}
                key = ("route", l)
                bk.wait_full(ve, key)
                link(tt(r["L"], bank(key)[:, 0:NT * NR].rearrange("p (i n) -> p i n", n=NR),
                        rb[:].unsqueeze(1).broadcast_to([P, NT, NR]), ALU.add))
                ve.sem_inc(bk.freed(key), 1)
                gl = r["L"][:, :, 0:NG]
                elg = r["L"][:, :, NG:NR]

                def bc(a, n):
                    return a.unsqueeze(2).broadcast_to([P, NT, n])

                def first_of(oh, v, m):
                    link(tt(oh, v, bc(m, NG), ALU.is_equal))
                    it = iota_f[:, 0:NG].unsqueeze(1).broadcast_to([P, NT, NG])
                    link(stt(r["cand"], oh, -64.0, it, ALU.mult, ALU.add))
                    link(red(r["m"], r["cand"], AX, ALU.min))
                    link(tt(oh, r["cand"], bc(r["m"], NG), ALU.is_equal))

                link(red(r["gmax"], gl, AX, ALU.max))
                link(tt(r["eg"], gl, bc(r["gmax"], NG), ALU.subtract))
                ve.sem_inc(r_gl, 1)
                first_of(r["ohg"], gl, r["gmax"])
                for i in range(NT):
                    link(tt(r["sel"][:, i], elg[:, i].rearrange("p (g e) -> p e g", g=NG),
                            r["ohg"][:, i].unsqueeze(1).broadcast_to([P, EPG, NG]), ALU.mult))
                link(red(r["xl"], r["sel"], AX, ALU.add))
                link(red(r["m1"], r["xl"], AX, ALU.max))
                first_of(r["oh1"], r["xl"], r["m1"])
                link(stt(r["xl2"], r["oh1"], NEG, r["xl"], ALU.mult, ALU.add))
                link(red(r["m2"], r["xl2"], AX, ALU.max))
                link(tt(r["e2"], r["m2"], r["m1"], ALU.subtract))
                ve.sem_inc(r_x2, 1)
                first_of(r["oh2"], r["xl2"], r["m2"])
                for c, oh in enumerate(("oh1", "oh2")):
                    for i in range(NT):
                        link(tt(r["OH"][:, c, i].rearrange("p (g e) -> p g e", g=NG),
                                r["ohg"][:, i].unsqueeze(2).broadcast_to([P, NG, EPG]),
                                r[oh][:, i].unsqueeze(1).broadcast_to([P, NG, EPG]), ALU.mult))
                link(tt(r["M"], r["OH"][:, 0], r["OH"][:, 1], ALU.add))
                ve.sem_inc(M_ready, 1)
                ve.wait_ge(r_eg, l + 1)
                link(red(r["gsum"], r["eg"], AX, ALU.add))
                ve.wait_ge(r_e2, l + 1)
                link(ts(r["den"], r["e2"], 1.0, None, ALU.add))
                link(tt(r["den"], r["den"], r["gsum"], ALU.mult))
                link(ve.reciprocal(r["wt"][:, 0], r["den"]))
                link(tt(r["wt"][:, 1], r["wt"][:, 0], r["e2"], ALU.mult))
                key = ("rank", l)
                bk.wait_full(ve, key)
                link(cp(r["R"], bank(key)[:, 0:NT * NE].rearrange("p (i n) -> p i n", n=NE)))
                link(cp(r["N"], bank(key)[:, NT * NE:(NT + 1) * NE]))
                ve.sem_inc(bk.freed(key), 1)
                link(ts(r["nx"], r["N"], float(CAP), None, ALU.is_gt))
                for m in range(2, FULLS + 1):
                    link(stt(r["nx"], r["N"], float(m * CAP), r["nx"], ALU.is_gt, ALU.add))
                link(ve.tensor_tensor_scan(r["off"], ones[:, 0:NE], r["nx"], 0.0, ALU.mult, ALU.add))
                link(tt(r["off"], r["off"], r["nx"], ALU.subtract))
                link(ts(r["q"], r["R"], float(CAP), None, ALU.is_ge))
                link(tt(r["ein"][:, 0], r["off"], iota_f[:, 0:NE], ALU.subtract))
                link(ts(r["ein"][:, 0], r["ein"][:, 0], float(NE - 1), None, ALU.add))
                link(tt(r["b"], r["q"], r["ein"][:, 0:1].broadcast_to([P, NT, NE]), ALU.mult))
                for m in range(2, FULLS + 1):
                    link(stt(r["q"], r["R"], float(m * CAP), r["q"], ALU.is_ge, ALU.add))
                link(tt(r["b"], r["b"], r["q"], ALU.add))
                link(tt(r["b"], r["b"], iota_f[:, 0:NE].unsqueeze(1).broadcast_to([P, NT, NE]), ALU.add))
                link(stt(r["j"], r["q"], -float(CAP), r["R"], ALU.mult, ALU.add))
                for c in range(2):
                    link(tt(r["tA"], r["OH"][:, c], r["b"], ALU.mult))
                    link(red(r["bc"][:, c], r["tA"], AX, ALU.add))
                    link(tt(r["tA"], r["OH"][:, c], r["j"], ALU.mult))
                    link(red(r["jc"][:, c], r["tA"], AX, ALU.add))
                link(stt(r["sl"], r["bc"], float(CAP), r["jc"], ALU.mult, ALU.add))
                link(cp(slot[:], r["sl"]))
                for c in range(2):
                    for i in range(NT):
                        k = c * NT + i
                        if k >= 2:
                            ve.wait_ge(idx_step, (2 * NT - 1) * l + k - 1)
                        link(ts(ohj[:, k % 2], iota_f[:, 0:CAP], r["jc"][:, c, i:i + 1], None, ALU.is_equal))
                        link(ts(ohb[:, k % 2], iota_f[:, 0:NBC], r["bc"][:, c, i:i + 1], tok_id[:, i:i + 1],
                                ALU.is_equal, ALU.mult))
                        ve.sem_inc(oh_ready, 1)
                key = ("idx", l)
                bk.wait_full(ve, key)
                link(cp(idx[:], bank(key)[0:CAP, 0:NBC]))
                ve.sem_inc(idx_ready, 1)
                ve.sem_inc(bk.freed(key), 1)
                it8 = iota_f[:, 0:16].unsqueeze(2).broadcast_to([P, 16, NE])
                off8 = r["off"].unsqueeze(1).broadcast_to([P, 16, NE])
                nx8 = r["nx"].unsqueeze(1).broadcast_to([P, 16, NE])
                link(tt(r["ein"], it8, off8, ALU.subtract))
                link(tt(r["ein2"], r["ein"], nx8, ALU.is_lt))
                link(stt(r["ein2"], r["ein"], 0.0, r["ein2"], ALU.is_ge, ALU.mult))
                link(tt(r["ein2"], r["ein2"], iota_f[:, 0:NE].unsqueeze(1).broadcast_to([P, 16, NE]), ALU.mult))
                link(red(r["eidf"], r["ein2"], AX, ALU.add))
                link(red(r["eidf"][:, 15:16], r["nx"], AX, ALU.add))
                link(cp(eid[:], r["eidf"]))
                ve.sem_inc(eid_ready, 1)
                def rows_T(b, par):
                    key = ("xgT1", l)
                    bk.wait_full(ve, key, b)
                    link(cp(xgT[:, par, 4:8], bank(key)[:, 0:4 * CAP].rearrange("p (k n) -> p k n", k=4)))
                    ve.sem_inc(xgT_ready, 1)
                    ve.sem_inc(bk.freed(key), 1)

                def times_up(b):
                    ve.wait_ge(ex_ready, b + (l * NE + 1))
                    if l or not isinstance(b, int) or b:
                        s_, n_, _ = bk.uses[("actT", l)]
                        ve.wait_ge(bk.full[s_], b + (n_ - 1))
                    bk.wait_full(ve, ("up", l), b)
                    link(tt(act[0:CAP], bank(("up", l))[0:CAP], ex[0:CAP], ALU.mult))
                    ve.sem_inc(act_ready, 1)
                    ve.sem_inc(bk.freed(("up", l)), 1)

                def block_ve(b, par):
                    if not (isinstance(b, int) and b >= NE - 2):
                        rows_T(b + 2, par)
                    if not (isinstance(b, int) and b == NE - 1):
                        times_up(b + 1)

                rows_T(0, 0)
                rows_T(1, 1)
                times_up(0)
                expert_loop(ve, block_ve, link)
                more = ve.value_load(eid[0:1, 15:16], min_val=0, max_val=NX)
                with ve.If(more > 0):
                    with ve.Fori(0, NX) as b:
                        ve.wait_ge(ov_act[l], b * 4 + 2)
                        ve.wait_ge(ov_pe[l], b * 4 + 3)
                        tt(act[0:CAP], PS[0:CAP, 1, :], ex[0:CAP], ALU.mult).then_inc(ov_ve[l], 1)
            for i in range(NT):
                for c in range(2):
                    k = 2 * i + c
                    ve.wait_ge(yg_sem[k % 4], 16 * (2 * (NL - 1) + k // 4 + 1))
                    if c:
                        ve.wait_ge(x_new, 3 * NT * (NL - 1) + NT + 2 * i + 1)
                    stt(x[:, i], yg[:, k % 4], rt["wt"][:, c, i:i + 1], x[:, i], ALU.mult, ALU.add).then_inc(x_new, 1)


_INS = ['x', 'attn_norm', 'ffn_norm', 'even_w_in', 'even_w_out', 'hg_lb_logits', 'hg_o_norm', 'da_q_norm',
        'da_k_norm', 'da_lambda', 'da_subln', 'odd_w_in', 'gla_w_alpha', 'gla_b_alpha', 'gla_o_norm', 'odd_w_out',
        'moe_w_group', 'moe_b_group', 'moe_w_router', 'moe_b_router', 'moe_w_gate', 'moe_w_up', 'moe_w_down']


def kernel(**inputs):
    import numpy as _np
    import concourse.bacc as _bacc
    from concourse import mybir as _mybir
    from concourse.bass_utils import run_bass_kernel_spmd as _run

    nc = _bacc.Bacc("TRN2", target_bir_lowering=False, num_devices=1)
    arrays, t = {}, {}
    for name in _INS:
        a = _np.ascontiguousarray(inputs[name])
        arrays[f"in_{name}"] = a
        t[name] = nc.dram_tensor(f"in_{name}", a.shape, _mybir.dt.from_np(a.dtype), kind="ExternalInput").ap()
    t["out"] = nc.dram_tensor("out_x", inputs["x"].shape, _mybir.dt.float32, kind="ExternalOutput").ap()
    build(nc, t)
    r = _run(nc, [arrays], core_ids=[0])
    return r.results[0]["out_x"]
```

```python
from contextlib import ExitStack

import concourse.bass as bass
from concourse import mybir

F32 = mybir.dt.float32
F32R = mybir.dt.float32r
I32 = mybir.dt.int32
U8 = mybir.dt.uint8
ALU = mybir.AluOpType
ACT = mybir.ActivationFunctionType
AX = mybir.AxisListType.X

P = 128
EPS = 1e-6
NEG = -1e30


class PsumBanks:

    def __init__(self, full, free):
        self.full, self.free = full, free
        self.count = [0] * 8
        self.last = [None] * 8
        self.uses = {}

    def plan(self, key, banks):
        s = banks[0]
        before = sorted({self.last[b] for b in banks if self.last[b] is not None})
        self.count[s] += 1
        self.uses[key] = (s, self.count[s], before)
        for b in banks:
            self.last[b] = (s, self.count[s])

    def plan_loop(self, key, banks, rounds):
        s = banks[0]
        self.uses[key] = (s, self.count[s] + 1, [])
        self.count[s] += rounds
        for b in banks:
            self.last[b] = (s, self.count[s])

    def acquire(self, pe, key):
        for s, n in self.uses[key][2]:
            pe.wait_ge(self.free[s], n)

    def acquire_in_loop(self, pe, key, i):
        s, n, _ = self.uses[key]
        pe.wait_ge(self.free[s], i + (n - 1))

    def wait_full(self, eng, key, i=0):
        s, n, _ = self.uses[key]
        eng.wait_ge(self.full[s], i + n)

    def filled(self, key):
        return self.full[self.uses[key][0]]

    def freed(self, key):
        return self.free[self.uses[key][0]]


class Chain:

    def __init__(self, eng, sem):
        self.eng, self.sem, self.n, self.i, self.per = eng, sem, 0, None, 0

    def __call__(self, ins):
        self.n += 1
        ins.then_inc(self.sem, 1)
        if self.i is None:
            self.eng.wait_ge(self.sem, self.n)
        else:
            self.eng.wait_ge(self.sem, self.i * self.per + self.n)

    def enter(self, i, per):
        self.i, self.per, self.start = i, per, self.n

    def leave(self, rounds):
        assert self.n - self.start == self.per
        self.n = self.start + self.per * rounds
        self.i = None


def build(nc, t):
    x_in = t["x"]
    B, T, D = x_in.shape
    NT = T // P
    KD = D // P
    NL = t["attn_norm"].shape[0]
    HW = t["hg_lb_logits"].shape[1]
    NH = 4
    DK = P
    DVS = (t["hg_o_norm"].shape[1], t["gla_o_norm"].shape[1])
    DA_D = t["da_q_norm"].shape[1]
    RANK = t["gla_w_alpha"].shape[1]
    NG, EPG = t["moe_w_group"].shape[2], t["moe_w_router"].shape[3]
    NE = NG * EPG
    NR = NG + NE
    DE = t["moe_w_gate"].shape[3]
    CAP = 96
    NX = (2 * T - 1) // CAP
    NB = NE + NX
    NBC = 32
    FULLS = T // CAP
    GC = 512
    LAM0 = 0.2
    QSCALE = float(DK) ** -0.5
    DASCALE = float(DA_D) ** -0.5
    GATE_SCALE = (1.0, 1.0 / 16.0)
    LEVELS = 7
    assert (B, NT, KD, NL, HW, DE, NH * DVS[1]) == (1, 4, 8, 2, 512, 512, D) and NB <= NBC

    EVEN = [("f", 1), ("q", 0), ("dq", 4), ("dk", 5), ("dv", 6), ("v", 2), ("g", 3)]
    ODD = [("q", 0), ("k", 1), ("v", 2), ("v2", 3), ("g", 4), ("g2", 5)]
    MIX = [EVEN, ODD]
    first_group = [0, len(EVEN) + 2]

    def mixer_steps(l):
        units = [("proj", l, k, u) for k, _ in MIX[l] for u in range(4)]
        levels = [[("cum", l), ("prep", l, 0)]]
        for s in range(1, LEVELS):
            levels.append([("prep", l, s), ("mm", l, s - 1), ("put", l, s - 1)])
        levels.append([("mm", l, LEVELS - 1), ("put", l, LEVELS - 1)])
        levels.append([("mm", l, LEVELS), ("put", l, LEVELS), ("inter", l)])
        da = [("da", l, i) for i in range(NT * NH + 3)] if l == 0 else []
        steps = ([("alpha", l)] if l == 1 else []) + units[:4 * 2]
        late = None
        for n, unit in enumerate(units[8:]):
            if l == 0 and n >= 12:
                steps += [("half", *unit[1:]), da[2 * (n - 12)]]
            steps.append(unit)
            if late:
                steps.append(late)
            late = ("dT", *unit[1:]) if unit[2] in ("dq", "dk") else None
            if n < len(levels):
                steps += levels[n]
            if l == 0 and n >= 12:
                steps.append(da[2 * (n - 12) + 1])
        steps += da[16:]
        for i in range(NT + 2):
            if i < NT:
                steps.append(("out", l, i))
            if 0 <= i - 1 < NT:
                steps.append(("oT", l, i - 1))
            if 0 <= i - 2 < NT:
                steps.append(("wo", l, 0, i - 2))
        for i in range(NT + 3):
            if i < NT:
                steps.append(("wo", l, 1, i))
            if 0 <= i - 1 < NT:
                steps.append(("h", 2 * l + 1, i - 1))
            if 0 <= i - 2 < NT:
                steps.append(("hT", 2 * l + 1, i - 2))
            if 0 <= i - 3 < NT:
                steps.append(("route", l, i - 3))
        return steps

    def norm_steps(n):
        steps = []
        for i in range(NT + 2):
            if i < NT:
                steps.append(("x", n, i))
            if 0 <= i - 1 < NT:
                steps.append(("h", n, i - 1))
            if 0 <= i - 2 < NT:
                steps.append(("hT", n, i - 2))
        return steps

    STEPS = [norm_steps(0) + mixer_steps(0), norm_steps(2) + mixer_steps(1)]
    NBK = [NH * dv // GC for dv in DVS]

    ctx = ExitStack()
    with ctx:
        base = nc.sbuf_base
        base += -base % 64
        cursor = [base]

        def at(name, shape, dt, offset):
            return nc.alloc_sbuf_tensor_at(name, shape, dt, offset=offset)

        def size_of(shape, dt):
            n = 1 if dt == U8 else 4
            for s in shape[1:]:
                n *= s
            return n + (-n % 64)

        def sb(name, shape, dt=F32):
            o = cursor[0]
            cursor[0] += size_of(shape, dt)
            return at(name, shape, dt, o)

        def sem(name):
            return ctx.enter_context(nc.semaphore(name))

        x = sb("x_sb", [P, NT, D])
        wbuf = sb("weight_ring", [P, 3, KD, GC])
        wbuf_at = base + size_of([P, NT, D], F32)
        etmp = sb("exp_tmp", [P, 2, GC])
        ident = sb("ident", [P, P])
        masks = sb("level_masks", [P, LEVELS + 1, P], U8)
        ones = sb("ones", [P, P])
        triu = sb("tri_before", [P, P])
        negmask = sb("causal_neg", [P, P])
        reset = sb("scan_reset", [P, T], U8)
        iota_f = sb("iota_free", [P, P])
        tok_id = sb("token_id", [P, NT])
        normw = sb("norm_weight", [P, D])
        rw = sb("router_w", [P, KD, NR])
        rb = sb("router_b", [P, NR])
        lb = sb("lower_bound", [P, 4 * NH])
        onw = sb("o_norm_w", [P, DVS[1]])
        subw = sb("subln_w", [P, DVS[0]])
        dqw = sb("da_q_w", [P, 1])
        dkw = sb("da_k_w", [P, 1])
        lamv = sb("lambda_vecs", [P, 4 * DA_D])
        lam = sb("lambda", [P, 4])
        balpha = sb("b_alpha", [P, NH])
        walpha = sb("w_alpha", [P, NH * DK])
        wa = sb("w_a", [P, KD, RANK])
        ss = sb("sum_sq", [P, 8])
        rstd = sb("rstd", [P, 8])
        xss = sb("x_sum_sq", [P, NT])
        xrs = sb("x_rstd", [P, NT])
        neghalf = sb("minus_half", [P, 8])
        el = sb("exp_last", [P, NH, NT])
        mx = sb("score_max", [P, 2, 2])
        nb = sb("score_bias", [P, 2, 2])
        sm = sb("score_sum", [P, 2, 2])
        rs = sb("score_rec", [P, 2, 2])
        eid = sb("eid", [P, 16], I32)
        arena = cursor[0]
        h = sb("h", [P, NT, D])
        hT = sb("hT", [P, KD, T])
        Q = sb("Q", [P, NH, T])
        K = sb("K", [P, NH, T])
        C = sb("C", [P, NH, T])
        G = sb("G", [P, NT, D])
        W = sb("W", [P, 2, NH * T])
        AT = sb("AT", [P, NT, NH, P])
        dqT = sb("dqT", [P, NH, T])
        dkT = sb("dkT", [P, NH, T])
        S_at = cursor[0]
        S0 = sb("S0", [P, 2, NH, DVS[0]])
        stag = sb("da_stage", [P, 2, GC])
        assert cursor[0] <= nc.sbuf_usable_end
        dq_at = S_at - 2 * NH * T * 4
        S1 = at("S1", [P, 2, NH, DVS[1]], F32, dq_at)
        aT = at("aT", [P, T], F32, dq_at + 2 * NH * DVS[1] * 4)
        S = [S0, S1]
        QE = Q[:].rearrange("p h n -> p (h n)")
        w_at = dq_at - NT * NH * P * 4 - 2 * NH * T * 4
        prob = at("prob", [P, 2, 2, T], F32, w_at)
        wgt = at("wgt", [P, 2, T], F32, w_at + 4 * T * 4)
        wgtT = at("wgtT", [P, 2, T], F32, w_at + 6 * T * 4)
        cursor[0] = arena + 2 * NT * D * 4
        xg = sb("xg", [P, D])
        xgTh = sb("xgT_high", [P, 2, KD, CAP], F32R)
        xgTl = sb("xgT_low", [P, 2, KD, CAP], F32R)
        ex = sb("ex", [P, DE])
        act = sb("act", [P, DE])
        actTh = sb("actT_high", [P, DE // P, CAP], F32R)
        actTl = sb("actT_low", [P, DE // P, CAP], F32R)
        whi_at = cursor[0]
        whi = sb("weight_high", [P, 2, KD, GC], F32R)
        yb = sb("yb", [P, D])
        yg = at("yg", [P, 4, D], F32, whi_at)
        ohj = sb("ohj", [P, 2, CAP])
        ohb = sb("ohb", [P, 2, NBC])
        idx = sb("idx", [CAP, NBC], I32)
        idxcol = sb("idxcol", [CAP, 1], I32)
        rt = {}
        for name, shape in dict(
            L=[NT, NR], gmax=[NT], cand=[NT, NG], m=[NT], ohg=[NT, NG], eg=[NT, NG], gsum=[NT], sel=[NT, EPG, NG],
            xl=[NT, EPG], m1=[NT], oh1=[NT, EPG], xl2=[NT, EPG], m2=[NT], oh2=[NT, EPG], e2=[NT], den=[NT],
            wt=[2, NT], OH=[2, NT, NE], M=[NT, NE], R=[NT, NE], N=[NE], nx=[NE], off=[NE], q=[NT, NE], j=[NT, NE],
            b=[NT, NE], tA=[NT, NE], bc=[2, NT], jc=[2, NT], sl=[2, NT], ein=[16, NE], ein2=[16, NE], eidf=[16],
        ).items():
            rt[name] = sb("r_" + name, [P] + shape)
        slot = sb("slot", [P, 2, NT], I32)
        size_w = size_of([P, KD, GC], F32)
        w_places = [wbuf_at + j * size_w for j in range(3)] + [arena, arena + size_w, cursor[0]]
        cursor[0] += size_w
        assert cursor[0] <= nc.sbuf_usable_end
        ew = [at(f"expert_w{j}", [P, KD, GC], F32, o) for j, o in enumerate(w_places)]
        ew_lo = [at(f"expert_w_low{j}", [P, KD, GC], F32R, o) for j, o in enumerate(w_places)]
        xgT = at("xgT", [P, KD, CAP], F32, arena + (2 * NT * D + D) * 4)
        actT = at("actT", [P, DE // P, CAP], F32, arena + (2 * NT * D + D + 4 * KD * CAP + 2 * DE) * 4)
        ii, jj, xx, m1_, m2_ = (at(name, [P, P], I32, dq_at + 4 * P * n) for n, name in enumerate(
            ("iota_i", "iota_j", "iota_x", "mask_1", "mask_2")))
        lbt = at("lb_tmp", [P, 2, NH], F32, dq_at + 4 * P * 5)

        PS = ctx.enter_context(nc.psum_tensor("PS", [P, 8, GC], F32))

        hbuf = [nc.dram_tensor(f"h_rows{l}", (T, D), F32).ap() for l in range(NL)]
        ybuf = [nc.dram_tensor(f"y_rows{l}", (NB * CAP, D), F32).ap() for l in range(NL)]

        bk = PsumBanks([sem(f"bank{b}_full") for b in range(8)], [sem(f"bank{b}_free") for b in range(8)])
        x_loaded = [sem(f"x_loaded{i}") for i in range(NT)]
        par1, par2 = sem("params_even_loaded"), sem("params_rest_loaded")
        nw_loaded = sem("norm_weight_loaded")
        w_loaded = [sem(f"w_loaded{i}") for i in range(3)]
        ew_loaded = [sem(f"expert_w_loaded{j}") for j in range(6)]
        rw_loaded = sem("router_loaded")
        consts = sem("consts_ready")
        masks_ready = sem("masks_ready")
        v_step, a_step = sem("vector_step"), sem("scalar_step")
        sq_done, mean_ready, root_ready = sem("sq_done"), sem("mean_square_ready"), sem("root_ready")
        h_ready, hT_a, hT_v = sem("h_ready"), sem("hT_by_scalar"), sem("hT_by_vector")
        x_new = sem("x_updated")
        e_ready, etmp_free = sem("exp_ready"), sem("exp_tmp_free")
        sig_ready = sem("sigmoid_ready")
        C_ready = sem("log_decay_ready")
        QKV_a, QKV_v = sem("heads_by_scalar"), sem("heads_by_vector")
        st_ready, daT = sem("da_staged"), sem("daT_ready")
        aT_ready = sem("aT_ready")
        D_ready, E_ready, X_ready = sem("diff_ready"), sem("decay_ready"), sem("scaled_ready")
        mm_done, put_done = sem("level_scored"), sem("level_put")
        keT_ready, S_ready = sem("keT_ready"), sem("state_ready")
        o_done = sem("o_done")
        nb_ready, p_ready, wgt_ready, wT_ready = sem("bias_ready"), sem("prob_ready"), sem("wgt_ready"), sem("wgtT_ready")
        lam_s, lam_e = sem("lambda_sums"), sem("lambda_exps")
        h_stored = sem("h_stored")
        r_gl, r_eg, r_x2, r_e2 = sem("r_groups"), sem("r_exp_groups"), sem("r_second"), sem("r_exp_second")
        M_ready, oh_ready, idx_ready, eid_ready = sem("assigned"), sem("onehots"), sem("idx_ready"), sem("eid_ready")
        idxcol_ready, gathered = sem("idxcol_ready"), sem("gathered")
        xgT_ready, ex_ready = sem("xgT_ready"), sem("gate_silu_ready")
        xgTh_ready, actTh_ready = sem("xgT_high_ready"), sem("actT_high_ready")
        w_hi, w_lo, w_lo_first = sem("weight_high_ready"), sem("weight_low_ready"), sem("first_low_ready")
        act_ready, actT_ready, y_ready, y_stored = sem("act_ready"), sem("actT_ready"), sem("y_ready"), sem("y_stored")
        yg_sem = [sem(f"y_gathered{i}") for i in range(4)]
        stored = sem("out_stored")
        ov_loaded = [sem(f"further_loaded{l}") for l in range(NL)]
        ov_col = [sem(f"further_idxcol{l}") for l in range(NL)]
        ov_gathered = [sem(f"further_gathered{l}") for l in range(NL)]
        ov_pe = [sem(f"further_by_tensor{l}") for l in range(NL)]
        ov_act = [sem(f"further_by_scalar{l}") for l in range(NL)]
        ov_ve = [sem(f"further_by_vector{l}") for l in range(NL)]
        ov_y = [sem(f"further_outputs{l}") for l in range(NL)]
        lb_ready = sem("lower_bound_ready")
        ov_stored = [sem(f"further_stored{l}") for l in range(NL)]
        idx_step, v_half = sem("idx_step"), sem("vector_half")
        gather_issued, group_taken = sem("gather_issued"), sem("group_taken")

        reader, qkv_no, tr_no = {}, {}, {}
        for l in range(NL):
            for s in STEPS[l]:
                kind = s[0]
                if kind == "alpha":
                    bk.plan(s, [4])
                    for u in range(4):
                        bk.plan((*s, u), [u])
                elif kind == "half":
                    bk.plan(("proj", *s[1:]), [s[3] % 2])
                elif kind == "proj":
                    if s not in bk.uses:
                        bk.plan(s, [s[3]])
                    reader[first_group[l] + [k for k, _ in MIX[l]].index(s[2])] = s
                    if s[2] not in ("dq", "dk"):
                        qkv_no[s] = len(qkv_no) + 1
                elif kind == "dT":
                    bk.plan(s, [s[3]])
                elif kind == "mm":
                    for i in range(NT):
                        bk.plan((*s, i), [4 + i])
                elif kind == "inter":
                    for i in range(NT - 1):
                        bk.plan((*s, i), [4 + i])
                elif kind == "out":
                    if s[2] < NT - 1:
                        bk.plan(("dS", l, s[2]), [4, 5][:NBK[l]])
                    bk.plan(s, [6, 7][:NBK[l]])
                elif kind == "da":
                    i = s[2]
                    if i < NT * NH:
                        bk.plan(("score", i), [4, 5] if i % 2 == 0 else [2, 3])
                    if 0 <= i - 2 < NT * NH:
                        bk.plan(("wT", i - 2), [6])
                    if i >= 3 and (i - 3) % NH == 0:
                        bk.plan(("pv", (i - 3) // NH), [7])
                elif kind in ("hT", "oT"):
                    tr_no[s] = len(tr_no) + 1
                    for g in range(2):
                        bk.plan((*s, g), [(6 if kind == "hT" else 2) + g])
                elif kind == "wo":
                    bk.plan(s, [s[3] % 2 if s[2] == 0 else s[3]])
                    reader[first_group[l] + len(MIX[l]) + s[2]] = s
                elif kind == "route":
                    if s[2] == 0:
                        bk.plan(("route", l), [5])
            bk.plan(("rank", l), [4])
            bk.plan(("idx", l), [0])
            for k, b in (("gate", [0]), ("up", [1]), ("down", [2, 3]), ("xgT", [4, 5]), ("actT", [6])):
                bk.plan_loop((k, l), b, NE)

        def bank(key):
            return PS[:, bk.uses[key][0], :]

        def expert_loop(eng, body, link=None):
            body(0, 0)
            n0 = link.n if link else 0
            body(1, 1)
            body(2, 0)
            per = link.n - n0 if link else 0
            with eng.Fori(0, (NE - 6) // 2) as k:
                if link:
                    link.enter(k, per)
                body(k * 2 + 3, 1)
                body(k * 2 + 4, 0)
                if link:
                    link.leave((NE - 6) // 2)
            for b in range(NE - 3, NE):
                body(b, b % 2)

        SPLITS = 4
        KS = KD // SPLITS
        GATE, DOWN, UP, LAST = 2, 3, 4, 3 * NE - 1
        experts0 = [first_group[l] + len(MIX[l]) + 2 for l in range(NL)]

        def place(l, p0, par):
            j = (p0 + 3 * par) % 6
            return (experts0[l] + j) % 3 if j < 3 else j

        def wait_loaded(eng, l, p0, b, par):
            r = (p0 + 3 * par) // 6
            eng.wait_ge(ew_loaded[place(l, p0, par)], b * 8 + (16 * (8 * l + r + 1) - 8 * par))

        def high_count(l, pos, part):
            return SPLITS * (3 * NE * l + pos) + part + 1

        def low_count(l, pos, part):
            return SPLITS * ((3 * NE - 2) * l + pos - 2) + part + 1

        def parts(l, p0, par, part):
            j = place(l, p0, par)
            r = slice(part * KS, (part + 1) * KS)
            return ew[j][:, r], whi[:, (p0 + par) % 2, r], ew_lo[j][:, r]

        block = ctx.enter_context(nc.Block())

        @block.sync
        def _(sp):
            def place_free(n, b=0):
                if n - 3 in reader:
                    bk.wait_full(sp, reader[n - 3], b)

            def load_group(n, src):
                place_free(n)
                sp.dma_start(wbuf[:, n % 3], src).then_inc(w_loaded[n % 3], 16)

            def cols(w, c):
                return w[:, c * GC:(c + 1) * GC].rearrange("(k p) n -> p k n", p=P)

            for i in range(NT):
                sp.dma_start(x[:, i], x_in[0, i * P:(i + 1) * P, :]).then_inc(x_loaded[i], 16)
                if i == 0:
                    load_group(0, cols(t["even_w_in"][0], EVEN[0][1]))
            for l in range(NL):
                n = first_group[l]
                if l == 0:
                    for i, (_, c) in enumerate(EVEN):
                        if i:
                            load_group(n + i, cols(t["even_w_in"][0], c))
                    for c in range(2):
                        load_group(n + len(EVEN) + c, cols(t["even_w_out"][0], c))
                n += len(MIX[l]) + 2

                def load(name, e, dst, done):
                    src = t["moe_w_" + name][l, bass.ds(e, 1)].rearrange("a (k p) n -> p (a k) n", p=P)
                    if name == "down":
                        dst = dst.rearrange("p (k c) n -> p k (c n)", c=2)
                    sp.dma_start(dst, src).then_inc(done, 16)

                def expert(name, e, p0, par=0):
                    j = place(l, p0, par)
                    load(name, e, ew[j][:], ew_loaded[j])

                def taken(name, b):
                    bk.wait_full(sp, (name, l), b)
                    sp.sem_inc(group_taken, 1)

                for pos, (name, e) in enumerate((("gate", 0), ("up", 0), ("gate", 1))):
                    place_free(n + pos)
                    expert(name, e, pos)
                for i in range(NT):
                    sp.wait_ge(h_ready, NT * (2 * l + 1) + i + 1)
                    sp.dma_start(hbuf[l][i * P:(i + 1) * P, :], h[:, i]).then_inc(h_stored, 16)
                sp.wait_ge(h_stored, 16 * NT * (l + 1))
                bk.wait_full(sp, ("route", l))
                for pos, (name, e) in enumerate((("down", 0), ("up", 1), ("gate", 2))):
                    expert(name, e, 3 + pos)

                def block_loads(b, par, before="down"):
                    taken(before, b - 1 if before == "down" else b)
                    expert("down", b + 1, DOWN + 3, par)
                    taken("up", b)
                    expert("up", b + 2, UP + 3, par)
                    if not (isinstance(b, int) and b == NE - 3):
                        taken("gate", b + 1)
                        expert("gate", b + 3, GATE + 6, par)

                block_loads(0, 0, "gate")
                with sp.Fori(0, (NE - 4) // 2) as k:
                    block_loads(k * 2 + 1, 1)
                    block_loads(k * 2 + 2, 0)
                block_loads(NE - 3, 1)
                taken("gate", NE - 2)
                expert("down", NE - 1, LAST)
                sp.wait_ge(eid_ready, l + 1)
                more = sp.value_load(eid[0:1, 15:16], min_val=0, max_val=NX)
                with sp.If(more > 0):
                    bk.wait_full(sp, ("down", l), NE - 1)
                    with sp.Fori(0, NX) as b:
                        sp.wait_ge(ov_pe[l], b * 4 + 1)
                        sp.sem_inc(group_taken, 1)
                        e = sp.value_load(eid[0:1, bass.ds(b, 1)], min_val=0, max_val=NE - 1)
                        for g, name in enumerate(("gate", "up", "down")):
                            load(name, e, wbuf[:, g], ov_loaded[l])
                    sp.wait_ge(ov_pe[l], NX * 4 + 1)
                if l + 1 < NL:
                    n = first_group[1]
                    for g, last_use in enumerate((("down", NE - 3), ("up", NE - 2), ("gate", NE - 1))):
                        bk.wait_full(sp, (last_use[0], l), last_use[1])
                        sp.dma_start(wbuf[:, (n + g) % 3], cols(t["odd_w_in"][0], MIX[1][g][1])
                                     ).then_inc(w_loaded[(n + g) % 3], 16)
                    for i in range(3, len(MIX[1])):
                        load_group(n + i, cols(t["odd_w_in"][0], MIX[1][i][1]))
                    for c in range(2):
                        load_group(n + len(MIX[1]) + c, cols(t["odd_w_out"][0], c))
            for i in range(NT):
                sp.wait_ge(x_new, (NL - 1) * 3 * NT + NT + 2 * (i + 1))
                sp.dma_start(t["out"][0, i * P:(i + 1) * P, :], x[:, i]).then_inc(stored, 16)
            sp.wait_ge(stored, 16 * NT)

        @block.gpsimd
        def _(pool):
            pool.memset(ident[:], 0.0).then_inc(consts, 1)
            pool.memset(ones[:], 1.0).then_inc(consts, 1)
            pool.memset(negmask[:], 0.0).then_inc(consts, 1)
            pool.memset(neghalf[:], -0.5).then_inc(consts, 1)
            pool.wait_ge(consts, 4)
            pool.affine_select(out=ident[:], in_=ident[:], compare_op=ALU.not_equal, fill=1.0, base=0,
                               pattern=[[-1, P]], channel_multiplier=1).then_inc(consts, 1)
            pool.affine_select(out=triu[:], in_=ones[:], compare_op=ALU.is_gt, fill=0.0, base=0,
                               pattern=[[1, P]], channel_multiplier=-1).then_inc(consts, 1)
            pool.affine_select(out=negmask[:], in_=negmask[:], compare_op=ALU.is_ge, fill=NEG, base=0,
                               pattern=[[-1, P]], channel_multiplier=1).then_inc(consts, 1)
            pool.iota(iota_f[:], [[1, P]], base=0, channel_multiplier=0,
                      allow_small_or_imprecise_dtypes=True).then_inc(consts, 1)
            pool.iota(tok_id[:], [[P, NT]], base=0, channel_multiplier=1,
                      allow_small_or_imprecise_dtypes=True).then_inc(consts, 1)
            pool.iota(ii[:], [[1, P]], base=0, channel_multiplier=0).then_inc(consts, 1)
            pool.iota(jj[:], [[0, P]], base=0, channel_multiplier=1).then_inc(consts, 1)

            def gather(l, b, col, n0, done):
                pool.tensor_copy(idxcol[:], idx[:, bass.ds(b, 1)]).then_inc(col, 1)
                pool.wait_ge(col, n0)
                pool.sem_inc(gather_issued, 1)
                pool.indirect_dma_start(xg[0:CAP, :], None, hbuf[l][:], bass.IndirectOffsetOnAxis(idxcol[:], 0)
                                        ).then_inc(done, 16)

            def gather_outputs(l, blocks):
                for i in range(NT):
                    for c in range(2):
                        k = 2 * i + c
                        if k >= 4:
                            pool.wait_ge(x_new, NT * (3 * l + 1) + (k - 4) + 1)
                        pool.indirect_dma_start(yg[:, k % 4], None, ybuf[l][0:blocks * CAP], bass.IndirectOffsetOnAxis(
                            slot[:, c, i:i + 1], 0)).then_inc(yg_sem[k % 4], 16)

            roots = [0]

            def power(dst):
                roots[0] += 1
                pool.wait_ge(mean_ready, roots[0])
                pool.tensor_tensor(dst, dst, neghalf[:, 0:dst.shape[-1]], ALU.pow).then_inc(root_ready, 1)

            for l in range(NL):
                for s in STEPS[l]:
                    if s[0] == "h":
                        power(xrs[:, s[2]:s[2] + 1])
                    elif s[0] == "proj" and s[2] in ("dq", "dk"):
                        power(rstd[:])
                    elif s[0] == "out" or s[0] == "da" and s[2] >= 3 and (s[2] - 3) % NH == NH - 1:
                        power(rstd[:, 0:NH])
                for pos in range(2):
                    for part in range(SPLITS):
                        pool.wait_ge(w_hi, high_count(l, pos, part))
                        w, hi, lo = parts(l, pos, 0, part)
                        pool.tensor_tensor(lo, w, hi.bitcast(F32), ALU.subtract).then_inc(w_lo_first, 1)
                pool.wait_ge(idx_ready, l + 1)
                pool.wait_ge(h_stored, 16 * NT * (l + 1))
                gather(l, 0, idxcol_ready, l * NE + 1, gathered)
                with pool.Fori(1, NE) as b:
                    bk.wait_full(pool, ("xgT", l), b - 1)
                    gather(l, b, idxcol_ready, b + (l * NE + 1), gathered)
                pool.wait_ge(eid_ready, l + 1)
                more = pool.value_load(eid[0:1, 15:16], min_val=0, max_val=NX)
                pool.wait_ge(y_stored, 16 * NE * (l + 1))
                with pool.If(more > 0):
                    with pool.Fori(0, NX) as b:
                        pool.wait_ge(ov_pe[l], b * 4 + 1)
                        gather(l, b + NE, ov_col[l], b + 1, ov_gathered[l])
                    pool.wait_ge(ov_act[l], 4 * NX)
                    gather_outputs(l, NB)
                with pool.If(more < 1):
                    gather_outputs(l, NE)

        @block.scalar
        def _(sc):
            link = Chain(sc, a_step)
            act_ = sc.activation
            etmp_uses, e_uses, sig_uses = [0], [0], [0]

            def take_etmp():
                if etmp_uses[0]:
                    sc.wait_ge(etmp_free, etmp_uses[0])
                etmp_uses[0] += 1

            def wait_sums():
                sig_uses[0] += 1
                sc.wait_ge(sig_ready, sig_uses[0])

            def param(dst, src, s):
                sc.dma_start(dst, src, allow_slow_non_contiguous=True).then_inc(s, 16)

            def load_norm(n):
                if n:
                    sc.wait_ge(h_ready, NT * n)
                w = t["attn_norm"] if n % 2 == 0 else t["ffn_norm"]
                param(normw[:], w[n // 2:n // 2 + 1, :].broadcast_to([P, D]), nw_loaded)

            def load_router(l):
                param(rw[:, :, 0:NG], t["moe_w_group"][l].rearrange("(k p) g -> p k g", p=P), rw_loaded)
                for g in range(NG):
                    param(rw[:, :, NG + g * EPG:NG + (g + 1) * EPG],
                          t["moe_w_router"][l, g].rearrange("(k p) e -> p k e", p=P), rw_loaded)
                param(rb[:, 0:NG], t["moe_b_group"][l:l + 1, :].broadcast_to([P, NG]), rw_loaded)
                param(rb[:, NG:], t["moe_b_router"][l:l + 1].rearrange("a g e -> a (g e)").broadcast_to([P, NE]),
                      rw_loaded)

            def row_stat(n, i):
                if etmp_uses[0]:
                    sc.wait_ge(etmp_free, etmp_uses[0])
                act_(etmp[:].rearrange("p a b -> p (a b)"), x[:, i], ACT.Square,
                     accum_out=xss[:, i:i + 1]).then_inc(sq_done, 1)
                sc.wait_ge(sq_done, NT * n + i + 1)

            def head_norm(key, dv):
                nbk = NH * dv // GC
                z = PS[:, bk.uses[key][0]:bk.uses[key][0] + nbk, :]
                bk.wait_full(sc, key)
                take_etmp()
                act_(etmp[:, 0:nbk], z, ACT.Square).then_inc(e_ready, 1)

            load_norm(0)
            param(lb[:, 0:NH], t["hg_lb_logits"][0].rearrange("(h p) -> p h", p=P), par1)
            for half in range(2):
                param(dqw[half * DA_D:(half + 1) * DA_D, :], t["da_q_norm"].rearrange("a n -> n a"), par1)
                param(dkw[half * DA_D:(half + 1) * DA_D, :], t["da_k_norm"].rearrange("a n -> n a"), par1)
            param(lamv[:], t["da_lambda"].rearrange("a b n -> a (b n)").broadcast_to([P, 4 * DA_D]), par1)
            param(subw[:], t["da_subln"].broadcast_to([P, DVS[0]]), par1)
            param(onw[:, 0:DVS[0]], t["hg_o_norm"].broadcast_to([P, DVS[0]]), par1)
            for l in range(NL):
                for s in STEPS[l]:
                    kind = s[0]
                    if kind == "x":
                        _, n, i = s
                        if n == 0:
                            sc.wait_ge(x_loaded[i], 16)
                        else:
                            sc.wait_ge(x_new, NT + 2 * (i + 1))
                        row_stat(n, i)
                    elif kind in ("hT", "oT"):
                        key = (*s, 0)
                        i = s[2]
                        bk.wait_full(sc, key)
                        link(act_(hT[:, 0:4, i * P:(i + 1) * P],
                                  bank(key).rearrange("p (k n) -> p k n", k=4), ACT.Copy))
                        sc.sem_inc(hT_a, 1)
                        sc.sem_inc(bk.freed(key), 1)
                        if kind == "hT" and i == NT - 1:
                            if s[1] + 1 < 2 * NL:
                                load_norm(s[1] + 1)
                            if s[1] == 0:
                                sc.wait_ge(lam_s, 1)
                                act_(lam[:, 0:2], lam[:, 2:4], ACT.Exp).then_inc(lam_e, 1)
                                param(balpha[:], t["gla_b_alpha"][0].rearrange("(h p) -> p h", p=P), par2)
                                param(walpha[0:RANK, :], t["gla_w_alpha"][0], par2)
                                param(wa[:], t["odd_w_in"][0][:, NH * 2 * DK + 2 * D:].rearrange(
                                    "(k p) n -> p k n", p=P), par2)
                            if s[1] == 2:
                                param(onw[:], t["gla_o_norm"].broadcast_to([P, DVS[1]]), par2)
                            if s[1] % 2 == 0:
                                load_router(l)
                    elif kind == "alpha":
                        for u in range(4):
                            wait_sums()
                            link(act_(etmp[:, 1], etmp[:, 1], ACT.Exp, scale=-1.0))
                            act_(etmp[:, 1], etmp[:, 1], ACT.Ln, bias=1.0).then_inc(e_ready, 1)
                            etmp_uses[0] += 1
                    elif kind == "proj":
                        _, _, what, u = s
                        bk.wait_full(sc, s)
                        z = bank(s)
                        if what in ("dq", "dk"):
                            take_etmp()
                            act_(etmp[:, 0], z, ACT.Square).then_inc(e_ready, 1)
                        else:
                            if what == "f":
                                link(act_(C[:, u], z, ACT.Sigmoid))
                                link(act_(K[:, u], z, ACT.Sigmoid, scale=-1.0))
                            elif what == "q" and l == 0:
                                link(act_(Q[:, u], z, ACT.Silu))
                            elif what in ("g", "g2"):
                                c0 = GC if what == "g2" else 0
                                link(act_(G[:, u, c0:c0 + GC], z, ACT.Silu))
                            elif what == "v":
                                link(act_(h[:, u, 0:GC], z, ACT.Copy))
                            elif what in ("v2", "dv"):
                                link(act_(h[:, u, GC:D], z, ACT.Copy))
                            else:
                                link(act_((Q if what == "q" else K)[:, u], z, ACT.Copy))
                            sc.sem_inc(QKV_a, 1)
                            sc.sem_inc(bk.freed(s), 1)
                    elif kind == "dT":
                        what, u = s[2:]
                        bk.wait_full(sc, s)
                        dst, w = (dqT, dqw) if what == "dq" else (dkT, dkw)
                        link(act_(dst[:, :, u * P:(u + 1) * P], bank(s).rearrange("p (h n) -> p h n", h=NH),
                             ACT.Copy, scale=w[:, 0:1]))
                        sc.sem_inc(daT, 1)
                        sc.sem_inc(bk.freed(s), 1)
                    elif kind == "cum":
                        if l == 0:
                            sc.wait_ge(lb_ready, 1)
                            for u in range(NH):
                                link(act_(C[:, u], C[:, u], ACT.Ln, scale=lb[:, 2 * NH + u:2 * NH + u + 1],
                                          bias=lb[:, NH + u:NH + u + 1]))
                                sc.sem_inc(C_ready, 1)
                    elif kind == "prep":
                        sc.wait_ge(D_ready, (LEVELS + 1) * l + s[2] + 1)
                        buf = W[:, s[2] % 2]
                        act_(buf, buf, ACT.Exp, scale=GATE_SCALE[l]).then_inc(E_ready, 1)
                    elif kind == "inter":
                        sc.wait_ge(D_ready, (LEVELS + 1) * (l + 1))
                        act_(W[:, 1], W[:, 1], ACT.Exp, scale=GATE_SCALE[l]).then_inc(E_ready, 1)
                        c_last = C[:].rearrange("p h (i j) -> p h i j", j=P)[:, :, :, P - 1]
                        link(act_(el[:], c_last, ACT.Exp, scale=GATE_SCALE[l]))
                        act_(W[:, 0], C[:].rearrange("p h n -> p (h n)"), ACT.Exp,
                             scale=GATE_SCALE[l]).then_inc(E_ready, 1)
                        for i in range(NT - 1):
                            key = (*s, i)
                            bk.wait_full(sc, key)
                            link(act_(K[:, i], bank(key), ACT.Copy))
                            sc.sem_inc(keT_ready, 1)
                            sc.sem_inc(bk.freed(key), 1)
                    elif kind == "out":
                        head_norm(s, DVS[l])
                    elif kind == "wo" and s[2] == 1:
                        i = s[3]
                        sc.wait_ge(x_new, 3 * NT * l + i + 1)
                        row_stat(2 * l + 1, i)
                    elif kind == "da":
                        i = s[2]
                        j = i - 2
                        if 0 <= j < NT * NH:
                            n = (j // NH + 1) * P
                            key = ("wT", j)
                            bk.wait_full(sc, key)
                            link(act_(wgtT[:, j % 2, 0:n], bank(key)[:, 0:n], ACT.Copy))
                            sc.sem_inc(wT_ready, 1)
                            sc.sem_inc(bk.freed(key), 1)
                        if i < NT * NH:
                            n = (i // NH + 1) * P
                            sc.wait_ge(nb_ready, i + 1)
                            s0 = bk.uses[("score", i)][0]
                            if i >= 2:
                                sc.wait_ge(wgt_ready, i - 1)
                            for c in range(2):
                                link(act_(prob[:, i % 2, c, 0:n], PS[:, s0 + c, 0:n], ACT.Exp, scale=DASCALE,
                                          bias=nb[:, i % 2, c:c + 1], accum_out=sm[:, i % 2, c:c + 1]))
                            sc.sem_inc(p_ready, 1)
                            sc.sem_inc(bk.freed(("score", i)), 1)
                        i -= 3
                        if i >= 0 and i % NH == NH - 1:
                            head_norm(("pv", i // NH), DVS[0])
                def high(p0, b=0, par=0):
                    wait_loaded(sc, l, p0, b, par)
                    for part in range(SPLITS):
                        w, hi, _ = parts(l, p0, par, part)
                        act_(hi, w, ACT.Copy).then_inc(w_hi, 1)

                high(0)
                high(1)
                sc.wait_ge(r_gl, l + 1)
                act_(rt["eg"][:], rt["eg"][:], ACT.Exp).then_inc(r_eg, 1)
                sc.wait_ge(r_x2, l + 1)
                act_(rt["e2"][:], rt["e2"][:], ACT.Exp).then_inc(r_e2, 1)

                def rows_T(b, par):
                    key = ("xgT", l)
                    bk.wait_full(sc, key, b)
                    act_(xgTh[:, par].rearrange("p (g k) n -> p g (k n)", g=2), PS[:, 4:6, 0:4 * CAP], ACT.Copy).then_inc(xgTh_ready, 1)

                def silu(b):
                    bk.wait_full(sc, ("gate", l), b)
                    if l or not isinstance(b, int) or b:
                        sc.wait_ge(act_ready, b + l * NE)
                    link(act_(ex[0:CAP], bank(("gate", l))[0:CAP], ACT.Silu))
                    sc.sem_inc(ex_ready, 1)
                    sc.sem_inc(bk.freed(("gate", l)), 1)

                def block_act(b, par):
                    is_int = isinstance(b, int)
                    last = is_int and b == NE - 1
                    if last:
                        bk.wait_full(sc, ("down", l), b - 1)
                        high(LAST)
                    else:
                        bk.wait_full(sc, ("up", l), b)
                        high(DOWN, b, par)
                        silu(b + 1)
                    key = ("actT", l)
                    bk.wait_full(sc, key, b)
                    act_(actTh[:].rearrange("p k n -> p (k n)"), bank(key)[:, 0:4 * CAP], ACT.Copy
                         ).then_inc(actTh_ready, 1)
                    if not last:
                        high(UP, b, par)
                    if not (is_int and b >= NE - 2):
                        rows_T(b + 2, par)
                        bk.wait_full(sc, ("down", l), b)
                        high(GATE + 3, b, par)
                    if l or not is_int or b:
                        sc.wait_ge(y_stored, b * 16 + 16 * l * NE)
                    key = ("down", l)
                    bk.wait_full(sc, key, b)
                    link(act_(yb[0:CAP].rearrange("p (c n) -> p c n", c=2), PS[0:CAP, 2:4], ACT.Copy))
                    sc.sem_inc(bk.freed(key), 1)
                    sc.dma_start(ybuf[l][bass.ds(b * CAP, CAP), :], yb[0:CAP, :]).then_inc(y_stored, 16)

                rows_T(0, 0)
                rows_T(1, 1)
                bk.wait_full(sc, ("gate", l))
                high(GATE)
                silu(0)
                expert_loop(sc, block_act, link)
                sc.wait_ge(eid_ready, l + 1)
                more = sc.value_load(eid[0:1, 15:16], min_val=0, max_val=NX)
                sc.wait_ge(y_stored, 16 * NE * (l + 1))
                with sc.If(more > 0):
                    with sc.Fori(0, NX) as b:
                        sc.wait_ge(ov_pe[l], b * 4 + 2)
                        for g in range(2):
                            ins = act_(xgT[:, 4 * g:4 * g + 4], PS[:, 4 + g, 0:4 * CAP].rearrange(
                                "p (k n) -> p k n", k=4), ACT.Copy)
                        ins.then_inc(ov_act[l], 1)
                        sc.wait_ge(ov_pe[l], b * 4 + 3)
                        act_(ex[0:CAP], PS[0:CAP, 0, :], ACT.Silu).then_inc(ov_act[l], 1)
                        sc.wait_ge(ov_pe[l], b * 4 + 4)
                        act_(actT[:].rearrange("p k n -> p (k n)"), PS[:, 6, 0:4 * CAP], ACT.Copy
                             ).then_inc(ov_act[l], 1)
                        sc.wait_ge(ov_pe[l], b * 4 + 5)
                        act_(yb[0:CAP, :].rearrange("p (c n) -> p c n", c=2), PS[0:CAP, 2:4, :], ACT.Copy
                             ).then_inc(ov_y[l], 1)
                        sc.wait_ge(ov_y[l], b + 1)
                        sc.dma_start(ybuf[l][bass.ds(b * CAP + NE * CAP, CAP), :], yb[0:CAP, :]
                                     ).then_inc(ov_stored[l], 16)
                        sc.wait_ge(ov_stored[l], b * 16 + 16)
                        sc.sem_inc(ov_act[l], 1)

        @block.tensor
        def _(pe):
            pe.wait_ge(consts, 11)
            n_st = 0
            for l in range(NL):
                n_g = first_group[l]
                n_wo = n_g + len(MIX[l])
                first_wo = True
                for s in STEPS[l]:
                    kind = s[0]
                    if kind in ("hT", "oT"):
                        i = s[2]
                        if kind == "hT":
                            src = h
                            pe.wait_ge(h_ready, NT * s[1] + i + 1)
                        else:
                            src = G
                            pe.wait_ge(o_done, (NT if l == 0 else 2 * NT) + i + 1)
                        for g in range(2):
                            k = (*s, g)
                            bk.acquire(pe, k)
                            for c in range(4):
                                d = (4 * g + c) * P
                                ins = pe.transpose(bank(k)[:, c * P:(c + 1) * P], src[:, i, d:d + P], ident[:])
                            ins.then_inc(bk.filled(k), 1)
                    elif kind == "alpha":
                        n = tr_no[("hT", 2 * l, NT - 1)]
                        pe.wait_ge(hT_a, n)
                        pe.wait_ge(hT_v, n)
                        pe.wait_ge(par2, 16 * 4)
                        bk.acquire(pe, s)
                        for k in range(KD):
                            ins = pe.matmul(bank(s)[0:RANK, :], wa[:, k, :], hT[:, k, :], start=k == 0, stop=k == KD - 1)
                        ins.then_inc(bk.filled(s), 1)
                        pe.wait_ge(aT_ready, 1)
                        for u in range(4):
                            key = (*s, u)
                            bk.acquire(pe, key)
                            pe.matmul(bank(key), walpha[0:RANK, u * P:(u + 1) * P], aT[0:RANK, :], start=True,
                                      stop=True).then_inc(bk.filled(key), 1)
                    elif kind in ("proj", "half"):
                        _, _, what, u = s
                        s = ("proj", *s[1:])
                        g = n_g + [k for k, _ in MIX[l]].index(what)
                        if g == n_g and u == 0:
                            n = tr_no[("hT", 2 * l, NT - 1)]
                            pe.wait_ge(hT_a, n)
                            pe.wait_ge(hT_v, n)
                        ks = range(KD)
                        if kind == "half":
                            ks = range(KD // 2)
                        elif ("half", *s[1:]) in STEPS[l]:
                            ks = range(KD // 2, KD)
                        if ks[0] == 0:
                            if u == 0:
                                pe.wait_ge(w_loaded[g % 3], 16 * (g // 3 + 1))
                            bk.acquire(pe, s)
                        wg = wbuf[:, g % 3]
                        by_feature = what in ("f", "q", "k")
                        for k in ks:
                            a, b = ((wg[:, k, u * P:(u + 1) * P], hT[:, k, :]) if by_feature
                                    else (hT[:, k, u * P:(u + 1) * P], wg[:, k, :]))
                            ins = pe.matmul(bank(s), a, b, start=k == 0, stop=k == KD - 1)
                        if ks[-1] == KD - 1:
                            ins.then_inc(bk.filled(s), 1)
                    elif kind == "dT":
                        n_st += 1
                        pe.wait_ge(st_ready, n_st)
                        bk.acquire(pe, s)
                        for c in range(NH):
                            ins = pe.transpose(bank(s)[:, c * P:(c + 1) * P],
                                               stag[:, s[3] % 2, c * P:(c + 1) * P], ident[:])
                        ins.then_inc(bk.filled(s), 1)
                    elif kind == "mm":
                        lev = s[2]
                        if lev < LEVELS:
                            pe.wait_ge(X_ready, (LEVELS + 2) * l + lev + 1)
                        for i in range(NT):
                            key = (*s, i)
                            bk.acquire(pe, key)
                            for c in range(NH):
                                if lev < LEVELS:
                                    a = b = W[:, lev % 2, c * T + i * P:c * T + (i + 1) * P]
                                else:
                                    a, b = K[:, c, i * P:(i + 1) * P], Q[:, c, i * P:(i + 1) * P]
                                ins = pe.matmul(bank(key)[:, c * P:(c + 1) * P], a, b, start=True, stop=True)
                            ins.then_inc(bk.filled(key), 1)
                    elif kind == "inter":
                        pe.wait_ge(X_ready, (LEVELS + 2) * l + LEVELS + 1)
                        for i in range(NT - 1):
                            key = (*s, i)
                            bk.acquire(pe, key)
                            for c in range(NH):
                                ins = pe.transpose(bank(key)[:, c * P:(c + 1) * P],
                                                   W[:, 1, c * T + i * P:c * T + (i + 1) * P], ident[:])
                            ins.then_inc(bk.filled(key), 1)
                    elif kind == "out":
                        i = s[2]
                        dv = DVS[l]
                        if i == 0:
                            pe.wait_ge(X_ready, (LEVELS + 2) * l + LEVELS + 2)
                            pe.wait_ge(QKV_a, max(v for k, v in qkv_no.items() if k[1] == l and k[2] in ("v", "v2")))
                            pe.wait_ge(put_done, 4 * (LEVELS + 1) * (l + 1))
                        if i < NT - 1:
                            key = ("dS", l, i)
                            pe.wait_ge(keT_ready, (NT - 1) * l + i + 1)
                            bk.acquire(pe, key)
                            ds_ = PS[:, 4:4 + NBK[l], :].rearrange("p a b -> p (a b)")
                            for c in range(NH):
                                ins = pe.matmul(ds_[:, c * dv:(c + 1) * dv], K[:, i, c * P:(c + 1) * P],
                                                h[:, i, c * dv:(c + 1) * dv], start=True, stop=True)
                            ins.then_inc(bk.filled(key), 1)
                        bk.acquire(pe, s)
                        o_ = PS[:, 6:6 + NBK[l], :].rearrange("p a b -> p (a b)")
                        if i:
                            pe.wait_ge(S_ready, (NT - 1) * l + i)
                        for c in range(NH):
                            ins = pe.matmul(o_[:, c * dv:(c + 1) * dv], AT[:, i, c], h[:, i, c * dv:(c + 1) * dv],
                                            start=True, stop=i == 0)
                            if i:
                                ins = pe.matmul(o_[:, c * dv:(c + 1) * dv], QE[:, c * T + i * P:c * T + (i + 1) * P],
                                                S[l][:, (i - 1) % 2, c], start=False, stop=True)
                        ins.then_inc(bk.filled(s), 1)
                    elif kind == "da":
                        i = s[2]
                        if i == 0:
                            pe.wait_ge(daT, 2 * NT)
                            pe.wait_ge(QKV_a, qkv_no[("proj", 0, "dv", 3)])
                        if i < NT * NH:
                            ti, c = divmod(i, NH)
                            n = (ti + 1) * P
                            key = ("score", i)
                            bk.acquire(pe, key)
                            s0 = bk.uses[key][0]
                            for m in range(2):
                                r = slice(m * DA_D, (m + 1) * DA_D)
                                ins = pe.matmul(PS[:, s0 + m, 0:n], dqT[r, c, ti * P:(ti + 1) * P], dkT[r, c, 0:n],
                                                start=True, stop=True)
                            ins.then_inc(bk.filled(key), 1)
                        i -= 2
                        if 0 <= i < NT * NH:
                            ti, c = divmod(i, NH)
                            key = ("wT", i)
                            pe.wait_ge(wgt_ready, i + 1)
                            bk.acquire(pe, key)
                            for j in range(ti + 1):
                                ins = pe.transpose(bank(key)[:, j * P:(j + 1) * P], wgt[:, i % 2, j * P:(j + 1) * P],
                                                   ident[:])
                            ins.then_inc(bk.filled(key), 1)
                        i -= 1
                        if i >= 0:
                            ti, c = divmod(i, NH)
                            pe.wait_ge(wT_ready, i + 1)
                            key = ("pv", ti)
                            if c == 0:
                                bk.acquire(pe, key)
                            for j in range(ti + 1):
                                ins = pe.matmul(bank(key)[:, c * P:(c + 1) * P], wgtT[:, i % 2, j * P:(j + 1) * P],
                                                h[:, j, GC + c * P:GC + (c + 1) * P], start=j == 0, stop=j == ti)
                            if c == NH - 1:
                                ins.then_inc(bk.filled(key), 1)
                    elif kind == "wo":
                        _, _, c, i = s
                        g = n_wo + c
                        if i == 0:
                            pe.wait_ge(w_loaded[g % 3], 16 * (g // 3 + 1))
                        if c == 0:
                            pe.wait_ge(hT_a, tr_no[("oT", l, i)])
                            pe.wait_ge(hT_v, tr_no[("oT", l, i)])
                        bk.acquire(pe, s)
                        for k in range(KD):
                            ins = pe.matmul(bank(s), hT[:, k, i * P:(i + 1) * P], wbuf[:, g % 3, k, :],
                                            start=k == 0, stop=k == KD - 1)
                        ins.then_inc(bk.filled(s), 1)
                    elif kind == "route":
                        i = s[2]
                        key = ("route", l)
                        pe.wait_ge(hT_a, tr_no[("hT", 2 * l + 1, i)])
                        pe.wait_ge(hT_v, tr_no[("hT", 2 * l + 1, i)])
                        if i == 0:
                            pe.wait_ge(rw_loaded, 16 * (NG + 3) * (l + 1))
                            bk.acquire(pe, key)
                        for k in range(KD):
                            ins = pe.matmul(bank(key)[:, i * NR:(i + 1) * NR], hT[:, k, i * P:(i + 1) * P], rw[:, k, :],
                                            start=k == 0, stop=k == KD - 1)
                        if i == NT - 1:
                            ins.then_inc(bk.filled(key), 1)
                key = ("rank", l)
                pe.wait_ge(M_ready, l + 1)
                bk.acquire(pe, key)
                M = rt["M"]
                for i in range(NT + 1):
                    n = i + 1 if i < NT else NT
                    for k in range(n):
                        own = i < NT and k == i
                        ins = pe.matmul(bank(key)[:, i * NE:(i + 1) * NE], (triu if own else ones)[:], M[:, k, :],
                                        start=k == 0, stop=k == n - 1)
                ins.then_inc(bk.filled(key), 1)
                key = ("idx", l)
                bk.acquire(pe, key)
                for k in range(2 * NT):
                    pe.wait_ge(oh_ready, 2 * NT * l + k + 1)
                    ins = pe.matmul(bank(key)[0:CAP, 0:NBC], ohj[:, k % 2], ohb[:, k % 2], start=k == 0,
                                    stop=k == 2 * NT - 1)
                    ins.then_inc(bk.filled(key) if k == 2 * NT - 1 else idx_step, 1)

                def three(out, pairs, first, final):
                    (ah, al), (bh, bl) = pairs
                    pe.matmul(out, ah, bh, start=first, stop=False)
                    pe.matmul(out, ah, bl, start=False, stop=False)
                    return pe.matmul(out, al, bh, start=False, stop=final)

                def wait_low(pos, b, part):
                    if pos < 2:
                        pe.wait_ge(w_lo_first, SPLITS * (2 * l + pos) + part + 1)
                    else:
                        pe.wait_ge(w_lo, b * (3 * SPLITS) + low_count(l, pos, part))

                def rows_T(b):
                    key = ("xgT", l)
                    pe.wait_ge(gathered, b * 16 + 16 * (l * NE + 1))
                    bk.acquire_in_loop(pe, key, b)
                    for c in range(KD):
                        ins = pe.transpose(PS[:, 4 + c // 4, c % 4 * CAP:(c % 4 + 1) * CAP],
                                           xg[0:CAP, c * P:(c + 1) * P], ident[0:CAP, 0:CAP])
                    ins.then_inc(bk.filled(key), 1)

                def act_T(b):
                    key = ("actT", l)
                    pe.wait_ge(act_ready, b + (l * NE + 1))
                    bk.acquire_in_loop(pe, key, b)
                    for c in range(DE // P):
                        ins = pe.transpose(bank(key)[:, c * CAP:(c + 1) * CAP], act[0:CAP, c * P:(c + 1) * P],
                                           ident[0:CAP, 0:CAP])
                    ins.then_inc(bk.filled(key), 1)

                def into(name, b, par, p0, b0, par0, midway=None):
                    key = (name, l)
                    hi, lo = whi[:, (p0 + par0) % 2], ew_lo[place(l, p0, par0)]
                    bk.acquire_in_loop(pe, key, b)
                    for k in range(KD):
                        if k % KS == 0:
                            wait_low(p0, b0, k // KS)
                        if k == KD // 2 and midway:
                            midway()
                        ins = three(bank(key)[0:CAP], ((xgTh[:, par, k], xgTl[:, par, k]),
                                                       (hi[:, k], lo[:, k])), k == 0, k == KD - 1)
                    ins.then_inc(bk.filled(key), 1)

                def block_pe(b, par):
                    is_int = isinstance(b, int)
                    last = is_int and b == NE - 1
                    if last:
                        act_T(b)
                    else:
                        pe.wait_ge(xgT_ready, b + (l * NE + 2))
                        into("gate", b + 1, 1 - par, GATE, b, par, lambda: act_T(b))
                    if not (is_int and b >= NE - 2):
                        rows_T(b + 2)
                    p0, b0, par0 = (LAST, 0, 0) if last else (DOWN, b, par)
                    hi, lo = whi[:, (p0 + par0) % 2], ew_lo[place(l, p0, par0)]
                    pe.wait_ge(actT_ready, b + (l * NE + 1))
                    key = ("down", l)
                    bk.acquire_in_loop(pe, key, b)
                    for k in range(DE // P):
                        wait_low(p0, b0, k)
                        for c in range(2):
                            ins = three(PS[0:CAP, 2 + c], ((actTh[:, k], actTl[:, k]),
                                                           (hi[:, 2 * k + c], lo[:, 2 * k + c])),
                                        k == 0, k == DE // P - 1)
                    ins.then_inc(bk.filled(key), 1)
                    if not last:
                        into("up", b + 1, 1 - par, UP, b, par)

                rows_T(0)
                pe.wait_ge(xgT_ready, l * NE + 1)
                into("gate", 0, 0, 0, 0, 0)
                rows_T(1)
                into("up", 0, 0, 1, 0, 0)
                expert_loop(pe, block_pe)
                pe.wait_ge(eid_ready, l + 1)
                more = pe.value_load(eid[0:1, 15:16], min_val=0, max_val=NX)
                pe.wait_ge(bk.freed(("down", l)), bk.uses[("down", l)][1] + NE - 1)
                with pe.If(more > 0):
                    pe.sem_inc(ov_pe[l], 1)
                    with pe.Fori(0, NX) as b:
                        pe.wait_ge(ov_gathered[l], b * 16 + 16)
                        for c in range(KD):
                            ins = pe.transpose(PS[:, 4 + c // 4, c % 4 * CAP:(c % 4 + 1) * CAP],
                                               xg[0:CAP, c * P:(c + 1) * P], ident[0:CAP, 0:CAP])
                        ins.then_inc(ov_pe[l], 1)
                        pe.wait_ge(ov_act[l], b * 4 + 1)
                        pe.wait_ge(ov_loaded[l], b * 48 + 48)
                        for g in range(2):
                            for k in range(KD):
                                ins = pe.matmul(PS[0:CAP, g, :], xgT[:, k], wbuf[:, g, k, :], start=k == 0,
                                                stop=k == KD - 1)
                        ins.then_inc(ov_pe[l], 1)
                        pe.wait_ge(ov_ve[l], b + 1)
                        for c in range(DE // P):
                            ins = pe.transpose(PS[:, 6, c * CAP:(c + 1) * CAP], act[0:CAP, c * P:(c + 1) * P],
                                               ident[0:CAP, 0:CAP])
                        ins.then_inc(ov_pe[l], 1)
                        pe.wait_ge(ov_act[l], b * 4 + 3)
                        for c in range(2):
                            for k in range(DE // P):
                                ins = pe.matmul(PS[0:CAP, 2 + c, :], actT[:, k], wbuf[:, 2, 2 * k + c, :],
                                                start=k == 0, stop=k == DE // P - 1)
                        ins.then_inc(ov_pe[l], 1)
                        pe.wait_ge(ov_act[l], b * 4 + 4)

        @block.vector
        def _(ve):
            link = Chain(ve, v_step)
            tt, ts, stt, cp = ve.tensor_tensor, ve.tensor_scalar, ve.scalar_tensor_tensor, ve.tensor_copy
            red = ve.tensor_reduce
            e_uses, halves, n_st, roots = [0], [0], [0], [0]

            def wait_e():
                e_uses[0] += 1
                ve.wait_ge(e_ready, e_uses[0])

            def rsqrt(dst, sums, n):
                roots[0] += 1
                ts(dst, sums, 1.0 / n, EPS, ALU.mult, ALU.add).then_inc(mean_ready, 1)
                ve.wait_ge(root_ready, roots[0])

            def head_norm(key, dv, outer, dst):
                z = PS[:, bk.uses[key][0]:bk.uses[key][0] + NH * dv // GC, :].rearrange("p a b -> p (a b)")
                wait_e()
                e = etmp[:].rearrange("p a b -> p (a b)")[:, 0:NH * dv].rearrange("p (h n) -> p h n", h=NH)
                link(red(ss[:, 0:NH], e, AX, ALU.add))
                ve.sem_inc(etmp_free, 1)
                rsqrt(rstd[:, 0:NH], ss[:, 0:NH], dv)
                for c in range(NH):
                    ins = stt(dst[:, c * dv:(c + 1) * dv], z[:, c * dv:(c + 1) * dv], rstd[:, c:c + 1],
                              outer(c), ALU.mult, ALU.mult)
                link(ins)
                ve.sem_inc(o_done, 1)
                ve.sem_inc(bk.freed(key), 1)

            def constants():
                link(ve.memset(AT[:], 0.0))
                link(ve.memset(reset[:], 1.0))
                link(ve.memset(reset[:].rearrange("p (i j) -> p i j", j=P)[:, :, 0], 0.0))
                ve.wait_ge(par1, 16 * 8)
                link(tt(lb[:, NH:2 * NH], lb[:, 0:NH], lb[:, 0:NH], ALU.subtract))
                link(ts(lb[:, NH:2 * NH], lb[:, NH:2 * NH], 1.0, None, ALU.add))
                link(ve.reciprocal(lbt[:, 0], lb[:, NH:2 * NH]))
                link(tt(lbt[:, 1], lb[:, NH:2 * NH], lbt[:, 0], ALU.mult))
                link(tt(lb[:, NH:2 * NH], lbt[:, 1], lbt[:, 1], ALU.subtract))
                link(ts(lb[:, 2 * NH:3 * NH], lb[:, NH:2 * NH], -1.0, 1.0, ALU.mult, ALU.add))
                ve.sem_inc(lb_ready, 1)
                for c in range(2):
                    v = lamv[:].rearrange("p (a n) -> p a n", a=4)
                    link(tt(v[:, 2 * c], v[:, 2 * c], v[:, 2 * c + 1], ALU.mult))
                    ins = red(lam[:, 2 + c:3 + c], v[:, 2 * c], AX, ALU.add)
                    if c == 0:
                        link(ins)
                    else:
                        ins.then_inc(lam_s, 1)
                link(ts(subw[:], subw[:], 1.0 - LAM0, None, ALU.mult))
                ve.wait_ge(consts, 11)
                link(tt(xx[:], ii[:], jj[:], ALU.bitwise_xor))
                link(tt(m1_[:], ii[:], jj[:], ALU.is_gt))
                for s in range(LEVELS):
                    link(stt(m2_[:], xx[:], float(1 << s), m1_[:], ALU.is_ge, ALU.mult))
                    link(stt(masks[:, s], xx[:], float(2 << s), m2_[:], ALU.is_lt, ALU.mult))
                link(tt(masks[:, LEVELS], ii[:], jj[:], ALU.is_equal))

            Cf = C[:].rearrange("p h n -> p (h n)")
            Qf, Kf = Q[:].rearrange("p h n -> p (h n)"), K[:].rearrange("p h n -> p (h n)")
            for l in range(NL):
                for s in STEPS[l]:
                    kind = s[0]
                    if kind == "h":
                        _, n, i = s
                        if i == 0:
                            ve.wait_ge(nw_loaded, 16 * (n + 1))
                            if n == 2:
                                ve.wait_ge(h_stored, 16 * NT)
                        ve.wait_ge(sq_done, NT * n + i + 1)
                        rsqrt(xrs[:, i:i + 1], xss[:, i:i + 1], D)
                        stt(h[:, i], x[:, i], xrs[:, i:i + 1], normw[:], ALU.mult, ALU.mult).then_inc(h_ready, 1)
                    elif kind == "x" and s[1] == 2:
                        i = s[2]
                        for c in range(2):
                            k = 2 * i + c
                            ve.wait_ge(yg_sem[k % 4], 16 * (k // 4 + 1))
                            if c:
                                ve.wait_ge(x_new, NT + 2 * i + 1)
                            stt(x[:, i], yg[:, k % 4], rt["wt"][:, c, i:i + 1], x[:, i], ALU.mult, ALU.add
                                ).then_inc(x_new, 1)
                    elif kind in ("hT", "oT"):
                        key = (*s, 1)
                        i = s[2]
                        bk.wait_full(ve, key)
                        link(cp(hT[:, 4:8, i * P:(i + 1) * P], bank(key).rearrange("p (k n) -> p k n", k=4)))
                        ve.sem_inc(hT_v, 1)
                        ve.sem_inc(bk.freed(key), 1)
                        if s == ("hT", 0, NT - 1):
                            constants()
                    elif kind == "alpha":
                        link(ve.memset(AT[:], 0.0))
                        ve.wait_ge(par2, 16 * 4)
                        bk.wait_full(ve, s)
                        link(cp(aT[0:RANK, :], bank(s)[0:RANK, :]))
                        ve.sem_inc(aT_ready, 1)
                        ve.sem_inc(bk.freed(s), 1)
                        for u in range(4):
                            key = (*s, u)
                            bk.wait_full(ve, key)
                            b_ = balpha[:, u:u + 1]
                            if u == 0:
                                ve.wait_ge(sq_done, NT * (2 * l + 1))
                            link(ts(etmp[:, 0], bank(key), b_, None, ALU.add))
                            link(stt(etmp[:, 1], etmp[:, 0], -1.0, etmp[:, 0], ALU.mult, ALU.max))
                            ve.sem_inc(bk.freed(key), 1)
                            ve.sem_inc(sig_ready, 1)
                            wait_e()
                            link(stt(C[:, u], etmp[:, 0], 0.0, etmp[:, 1], ALU.min, ALU.subtract))
                            ve.sem_inc(etmp_free, 1)
                    elif kind == "proj":
                        _, _, what, u = s
                        z = bank(s)
                        if what in ("g", "g2"):
                            ve.wait_ge(QKV_a, qkv_no[s])
                            c0 = GC if what == "g2" else 0
                            dv = DVS[l]
                            gd = G[:, u, c0:c0 + GC].rearrange("p (h n) -> p h n", n=dv)
                            link(tt(gd, gd, onw[:, 0:dv].unsqueeze(1).broadcast_to([P, GC // dv, dv]), ALU.mult))
                        elif what in ("dq", "dk"):
                            wait_e()
                            e0 = etmp[:, 0]
                            link(red(ss[:], e0.rearrange("p (g n) -> p g n", n=DA_D), AX, ALU.add))
                            ve.sem_inc(etmp_free, 1)
                            rsqrt(rstd[:], ss[:], DA_D)
                            n_st[0] += 1
                            if n_st[0] > 2:
                                prev = ("dT", 0, "dq" if n_st[0] - 3 < NT else "dk", (n_st[0] - 3) % NT)
                                bk.wait_full(ve, prev)
                            link(tt(stag[:, u % 2].rearrange("p (g n) -> p g n", n=DA_D),
                                    z.rearrange("p (g n) -> p g n", n=DA_D),
                                    rstd[:].unsqueeze(2).broadcast_to([P, 8, DA_D]), ALU.mult))
                            ve.sem_inc(st_ready, 1)
                            ve.sem_inc(bk.freed(s), 1)
                    elif kind == "cum":
                        ve.wait_ge(QKV_a, qkv_no[("proj", l, MIX[l][1][0], NH - 1)])
                        ve.wait_ge(QKV_a, qkv_no[("proj", l, MIX[l][0][0], NH - 1)])
                        link(ts(Qf, Qf, QSCALE, None, ALU.mult))
                        if l == 0:
                            link(tt(K[:], K[:], lb[:, 2 * NH:3 * NH].unsqueeze(2).broadcast_to([P, NH, T]), ALU.mult))
                            ve.wait_ge(C_ready, NH)
                        for c in range(NH):
                            ins = ve.tensor_tensor_scan(C[:, c], reset[:], C[:, c], 0.0, ALU.mult, ALU.add)
                        link(ins)
                    elif kind == "prep":
                        lev = s[2]
                        half = 1 << lev
                        buf = W[:, lev % 2].rearrange("p (m c j) -> p m c j", c=2, j=half)
                        Cv = Cf.rearrange("p (m c j) -> p m c j", c=2, j=half)
                        mid = Cv[:, :, 0, half - 1:half].broadcast_to([P, NH * T // (2 * half), half])
                        if lev >= 2:
                            for i in range(NT):
                                bk.wait_full(ve, ("mm", l, lev - 2, i))
                        tt(buf[:, :, 0], mid, Cv[:, :, 0], ALU.subtract).then_inc(v_half, 1)
                        halves[0] += 1
                        tt(buf[:, :, 1], Cv[:, :, 1], mid, ALU.subtract).then_inc(D_ready, 1)
                        ve.wait_ge(v_half, halves[0])
                        ve.wait_ge(E_ready, (LEVELS + 2) * l + lev + 1)
                        Kv = Kf.rearrange("p (m c j) -> p m c j", c=2, j=half)
                        Qv = Qf.rearrange("p (m c j) -> p m c j", c=2, j=half)
                        tt(buf[:, :, 0], buf[:, :, 0], Kv[:, :, 0], ALU.mult)
                        link(tt(buf[:, :, 1], buf[:, :, 1], Qv[:, :, 1], ALU.mult))
                        ve.sem_inc(X_ready, 1)
                    elif kind == "put":
                        for i in range(NT):
                            key = ("mm", *s[1:], i)
                            bk.wait_full(ve, key)
                            m = masks[:, s[2]].unsqueeze(1).broadcast_to([P, NH, P])
                            link(ve.copy_predicated(AT[:, i], m, bank(key).rearrange("p (h n) -> p h n", h=NH)))
                            ve.sem_inc(bk.freed(key), 1)
                            ve.sem_inc(put_done, 1)
                    elif kind == "inter":
                        n = (LEVELS + 2) * l + LEVELS
                        Cv = C[:].rearrange("p h (i j) -> p (h i) j", j=P)
                        last = Cv[:, :, P - 1:P].broadcast_to([P, NH * NT, P])
                        tt(W[:, 1].rearrange("p (m j) -> p m j", j=P), last, Cv, ALU.subtract).then_inc(D_ready, 1)
                        ve.wait_ge(E_ready, n + 1)
                        tt(W[:, 1], W[:, 1], Kf, ALU.mult).then_inc(X_ready, 1)
                        ve.wait_ge(E_ready, n + 2)
                        tt(QE, W[:, 0], Qf, ALU.mult).then_inc(X_ready, 1)
                    elif kind == "out":
                        i = s[2]
                        dv = DVS[l]
                        if i < NT - 1:
                            key = ("dS", l, i)
                            bk.wait_full(ve, key)
                            if i == 2:
                                bk.wait_full(ve, ("out", l, 1))
                            ds_ = PS[:, 4:4 + NBK[l], :].rearrange("p a b -> p (a b)")
                            for c in range(NH):
                                z = ds_[:, c * dv:(c + 1) * dv]
                                if i == 0:
                                    ins = cp(S[l][:, 0, c], z)
                                else:
                                    ins = stt(S[l][:, i % 2, c], S[l][:, (i - 1) % 2, c], el[:, c, i:i + 1], z,
                                              ALU.mult, ALU.add)
                            link(ins)
                            ve.sem_inc(S_ready, 1)
                            ve.sem_inc(bk.freed(key), 1)
                        head_norm(s, dv, lambda c: G[:, i, c * dv:(c + 1) * dv], G[:, i, 0:NH * dv])
                    elif kind == "da":
                        i = s[2]
                        if i == 0:
                            ve.wait_ge(lam_e, 1)
                            link(tt(lam[:, 2:3], lam[:, 1:2], lam[:, 0:1], ALU.subtract))
                            link(ts(lam[:, 3:4], lam[:, 2:3], -LAM0, None, ALU.add))
                        if i < NT * NH:
                            n = (i // NH + 1) * P
                            key = ("score", i)
                            bk.wait_full(ve, key)
                            s0 = bk.uses[key][0]
                            diag = PS[:, s0:s0 + 2, n - P:n]
                            link(tt(diag, diag, negmask[:].unsqueeze(1).broadcast_to([P, 2, P]), ALU.add))
                            link(red(mx[:, i % 2], PS[:, s0:s0 + 2, 0:n], AX, ALU.max))
                            ts(nb[:, i % 2], mx[:, i % 2], -DASCALE, None, ALU.mult).then_inc(nb_ready, 1)
                        i -= 1
                        if 0 <= i < NT * NH:
                            n = (i // NH + 1) * P
                            if i >= 2:
                                bk.wait_full(ve, ("wT", i - 2))
                            else:
                                bk.wait_full(ve, ("inter", 0, NT - 2))
                            ve.wait_ge(p_ready, i + 1)
                            link(ve.reciprocal(rs[:, i % 2], sm[:, i % 2]))
                            link(tt(rs[:, i % 2, 1:2], rs[:, i % 2, 1:2], lam[:, 3:4], ALU.mult))
                            link(ts(wgt[:, i % 2, 0:n], prob[:, i % 2, 0, 0:n], rs[:, i % 2, 0:1], None, ALU.mult))
                            stt(wgt[:, i % 2, 0:n], prob[:, i % 2, 1, 0:n], rs[:, i % 2, 1:2], wgt[:, i % 2, 0:n],
                                ALU.mult, ALU.add).then_inc(wgt_ready, 1)
                        i -= 2
                        if i >= 0 and i % NH == NH - 1:
                            ti = i // NH
                            head_norm(("pv", ti), DVS[0], lambda c: subw[:], G[:, ti, GC:D])
                    elif kind == "wo":
                        _, _, c, i = s
                        bk.wait_full(ve, s)
                        xs = x[:, i, c * GC:(c + 1) * GC]
                        link(tt(xs, bank(s), xs, ALU.add))
                        ve.sem_inc(bk.freed(s), 1)
                        if c == 1:
                            ve.sem_inc(x_new, 1)
                r = {k: v[:] for k, v in rt.items()}
                key = ("route", l)
                bk.wait_full(ve, key)
                link(tt(r["L"], bank(key)[:, 0:NT * NR].rearrange("p (i n) -> p i n", n=NR),
                        rb[:].unsqueeze(1).broadcast_to([P, NT, NR]), ALU.add))
                ve.sem_inc(bk.freed(key), 1)
                gl = r["L"][:, :, 0:NG]
                elg = r["L"][:, :, NG:NR]

                def bc(a, n):
                    return a.unsqueeze(2).broadcast_to([P, NT, n])

                def first_of(oh, v, m):
                    link(tt(oh, v, bc(m, NG), ALU.is_equal))
                    it = iota_f[:, 0:NG].unsqueeze(1).broadcast_to([P, NT, NG])
                    link(stt(r["cand"], oh, -64.0, it, ALU.mult, ALU.add))
                    link(red(r["m"], r["cand"], AX, ALU.min))
                    link(tt(oh, r["cand"], bc(r["m"], NG), ALU.is_equal))

                link(red(r["gmax"], gl, AX, ALU.max))
                link(tt(r["eg"], gl, bc(r["gmax"], NG), ALU.subtract))
                ve.sem_inc(r_gl, 1)
                first_of(r["ohg"], gl, r["gmax"])
                for i in range(NT):
                    link(tt(r["sel"][:, i], elg[:, i].rearrange("p (g e) -> p e g", g=NG),
                            r["ohg"][:, i].unsqueeze(1).broadcast_to([P, EPG, NG]), ALU.mult))
                link(red(r["xl"], r["sel"], AX, ALU.add))
                link(red(r["m1"], r["xl"], AX, ALU.max))
                first_of(r["oh1"], r["xl"], r["m1"])
                link(stt(r["xl2"], r["oh1"], NEG, r["xl"], ALU.mult, ALU.add))
                link(red(r["m2"], r["xl2"], AX, ALU.max))
                link(tt(r["e2"], r["m2"], r["m1"], ALU.subtract))
                ve.sem_inc(r_x2, 1)
                first_of(r["oh2"], r["xl2"], r["m2"])
                for c, oh in enumerate(("oh1", "oh2")):
                    for i in range(NT):
                        link(tt(r["OH"][:, c, i].rearrange("p (g e) -> p g e", g=NG),
                                r["ohg"][:, i].unsqueeze(2).broadcast_to([P, NG, EPG]),
                                r[oh][:, i].unsqueeze(1).broadcast_to([P, NG, EPG]), ALU.mult))
                link(tt(r["M"], r["OH"][:, 0], r["OH"][:, 1], ALU.add))
                ve.sem_inc(M_ready, 1)
                ve.wait_ge(r_eg, l + 1)
                link(red(r["gsum"], r["eg"], AX, ALU.add))
                ve.wait_ge(r_e2, l + 1)
                link(ts(r["den"], r["e2"], 1.0, None, ALU.add))
                link(tt(r["den"], r["den"], r["gsum"], ALU.mult))
                link(ve.reciprocal(r["wt"][:, 0], r["den"]))
                link(tt(r["wt"][:, 1], r["wt"][:, 0], r["e2"], ALU.mult))
                key = ("rank", l)
                bk.wait_full(ve, key)
                link(cp(r["R"], bank(key)[:, 0:NT * NE].rearrange("p (i n) -> p i n", n=NE)))
                link(cp(r["N"], bank(key)[:, NT * NE:(NT + 1) * NE]))
                ve.sem_inc(bk.freed(key), 1)
                link(ts(r["nx"], r["N"], float(CAP), None, ALU.is_gt))
                for m in range(2, FULLS + 1):
                    link(stt(r["nx"], r["N"], float(m * CAP), r["nx"], ALU.is_gt, ALU.add))
                link(ve.tensor_tensor_scan(r["off"], ones[:, 0:NE], r["nx"], 0.0, ALU.mult, ALU.add))
                link(tt(r["off"], r["off"], r["nx"], ALU.subtract))
                link(ts(r["q"], r["R"], float(CAP), None, ALU.is_ge))
                link(tt(r["ein"][:, 0], r["off"], iota_f[:, 0:NE], ALU.subtract))
                link(ts(r["ein"][:, 0], r["ein"][:, 0], float(NE - 1), None, ALU.add))
                link(tt(r["b"], r["q"], r["ein"][:, 0:1].broadcast_to([P, NT, NE]), ALU.mult))
                for m in range(2, FULLS + 1):
                    link(stt(r["q"], r["R"], float(m * CAP), r["q"], ALU.is_ge, ALU.add))
                link(tt(r["b"], r["b"], r["q"], ALU.add))
                link(tt(r["b"], r["b"], iota_f[:, 0:NE].unsqueeze(1).broadcast_to([P, NT, NE]), ALU.add))
                link(stt(r["j"], r["q"], -float(CAP), r["R"], ALU.mult, ALU.add))
                for c in range(2):
                    link(tt(r["tA"], r["OH"][:, c], r["b"], ALU.mult))
                    link(red(r["bc"][:, c], r["tA"], AX, ALU.add))
                    link(tt(r["tA"], r["OH"][:, c], r["j"], ALU.mult))
                    link(red(r["jc"][:, c], r["tA"], AX, ALU.add))
                link(stt(r["sl"], r["bc"], float(CAP), r["jc"], ALU.mult, ALU.add))
                link(cp(slot[:], r["sl"]))
                for c in range(2):
                    for i in range(NT):
                        k = c * NT + i
                        if k >= 2:
                            ve.wait_ge(idx_step, (2 * NT - 1) * l + k - 1)
                        link(ts(ohj[:, k % 2], iota_f[:, 0:CAP], r["jc"][:, c, i:i + 1], None, ALU.is_equal))
                        link(ts(ohb[:, k % 2], iota_f[:, 0:NBC], r["bc"][:, c, i:i + 1], tok_id[:, i:i + 1],
                                ALU.is_equal, ALU.mult))
                        ve.sem_inc(oh_ready, 1)
                key = ("idx", l)
                bk.wait_full(ve, key)
                link(cp(idx[:], bank(key)[0:CAP, 0:NBC]))
                ve.sem_inc(idx_ready, 1)
                ve.sem_inc(bk.freed(key), 1)
                it8 = iota_f[:, 0:16].unsqueeze(2).broadcast_to([P, 16, NE])
                off8 = r["off"].unsqueeze(1).broadcast_to([P, 16, NE])
                nx8 = r["nx"].unsqueeze(1).broadcast_to([P, 16, NE])
                link(tt(r["ein"], it8, off8, ALU.subtract))
                link(tt(r["ein2"], r["ein"], nx8, ALU.is_lt))
                link(stt(r["ein2"], r["ein"], 0.0, r["ein2"], ALU.is_ge, ALU.mult))
                link(tt(r["ein2"], r["ein2"], iota_f[:, 0:NE].unsqueeze(1).broadcast_to([P, 16, NE]), ALU.mult))
                link(red(r["eidf"], r["ein2"], AX, ALU.add))
                link(red(r["eidf"][:, 15:16], r["nx"], AX, ALU.add))
                link(cp(eid[:], r["eidf"]))
                ve.sem_inc(eid_ready, 1)
                def low(p0, b=0, par=0):
                    for part in range(SPLITS):
                        w, hi, lo = parts(l, p0, par, part)
                        ve.wait_ge(w_hi, b * (3 * SPLITS) + high_count(l, p0, part))
                        tt(lo, w, hi.bitcast(F32), ALU.subtract).then_inc(w_lo, 1)

                def rows_T(b, par):
                    key = ("xgT", l)
                    ve.wait_ge(xgTh_ready, b + (l * NE + 1))
                    def halves_of(a):
                        return a.rearrange("p (g k) n -> p g (k n)", g=2)
                    link(tt(halves_of(xgTl[:, par]), PS[:, 4:6, 0:4 * CAP], halves_of(xgTh[:, par].bitcast(F32)),
                            ALU.subtract))
                    ve.sem_inc(xgT_ready, 1)
                    ve.sem_inc(bk.freed(key), 1)

                def times_up(b):
                    ve.wait_ge(ex_ready, b + (l * NE + 1))
                    if l or not isinstance(b, int) or b:
                        s_, n_, _ = bk.uses[("actT", l)]
                        ve.wait_ge(bk.full[s_], b + (n_ - 1))
                    bk.wait_full(ve, ("up", l), b)
                    link(tt(act[0:CAP], bank(("up", l))[0:CAP], ex[0:CAP], ALU.mult))
                    ve.sem_inc(act_ready, 1)
                    ve.sem_inc(bk.freed(("up", l)), 1)

                def block_ve(b, par):
                    is_int = isinstance(b, int)
                    last = is_int and b == NE - 1
                    if last:
                        low(LAST)
                    else:
                        low(DOWN, b, par)
                    key = ("actT", l)
                    ve.wait_ge(actTh_ready, b + (l * NE + 1))
                    link(tt(actTl[:].rearrange("p k n -> p (k n)"), bank(key)[:, 0:4 * CAP],
                            actTh[:].rearrange("p k n -> p (k n)").bitcast(F32), ALU.subtract))
                    ve.sem_inc(actT_ready, 1)
                    ve.sem_inc(bk.freed(key), 1)
                    if not last:
                        low(UP, b, par)
                    if not (is_int and b >= NE - 2):
                        rows_T(b + 2, par)
                        low(GATE + 3, b, par)
                    if not last:
                        times_up(b + 1)

                rows_T(0, 0)
                rows_T(1, 1)
                low(GATE)
                times_up(0)
                expert_loop(ve, block_ve, link)
                more = ve.value_load(eid[0:1, 15:16], min_val=0, max_val=NX)
                with ve.If(more > 0):
                    with ve.Fori(0, NX) as b:
                        ve.wait_ge(ov_act[l], b * 4 + 2)
                        ve.wait_ge(ov_pe[l], b * 4 + 3)
                        tt(act[0:CAP], PS[0:CAP, 1, :], ex[0:CAP], ALU.mult).then_inc(ov_ve[l], 1)
            for i in range(NT):
                for c in range(2):
                    k = 2 * i + c
                    ve.wait_ge(yg_sem[k % 4], 16 * (2 * (NL - 1) + k // 4 + 1))
                    if c:
                        ve.wait_ge(x_new, 3 * NT * (NL - 1) + NT + 2 * i + 1)
                    stt(x[:, i], yg[:, k % 4], rt["wt"][:, c, i:i + 1], x[:, i], ALU.mult, ALU.add).then_inc(x_new, 1)


_INS = ['x', 'attn_norm', 'ffn_norm', 'even_w_in', 'even_w_out', 'hg_lb_logits', 'hg_o_norm', 'da_q_norm',
        'da_k_norm', 'da_lambda', 'da_subln', 'odd_w_in', 'gla_w_alpha', 'gla_b_alpha', 'gla_o_norm', 'odd_w_out',
        'moe_w_group', 'moe_b_group', 'moe_w_router', 'moe_b_router', 'moe_w_gate', 'moe_w_up', 'moe_w_down']


def kernel(**inputs):
    import numpy as _np
    import concourse.bacc as _bacc
    from concourse import mybir as _mybir
    from concourse.bass_utils import run_bass_kernel_spmd as _run

    nc = _bacc.Bacc("TRN2", target_bir_lowering=False, num_devices=1)
    arrays, t = {}, {}
    for name in _INS:
        a = _np.ascontiguousarray(inputs[name])
        arrays[f"in_{name}"] = a
        t[name] = nc.dram_tensor(f"in_{name}", a.shape, _mybir.dt.from_np(a.dtype), kind="ExternalInput").ap()
    t["out"] = nc.dram_tensor("out_x", inputs["x"].shape, _mybir.dt.float32, kind="ExternalOutput").ap()
    build(nc, t)
    r = _run(nc, [arrays], core_ids=[0])
    return r.results[0]["out_x"]
```
